# Optimizing a Trainium2 kernel written in Bass

```python
import jax, jax.numpy as jnp
from jax import lax
import numpy as np

D_MODEL = 1024
BATCH = 1
SEQ = 1024
DEPTH = 1

D_MIX = D_MODEL
D_CONV = D_MIX // 2
D_GMLP = D_MIX - D_CONV
N_CONV_GROUPS = 8
N_GMLP_HEADS = 8
GMLP_HEAD_DIM = D_GMLP // N_GMLP_HEADS
CONV_WIDTH = 31
CHUNK = 128
N_PROJ = 2 * D_CONV + 2 * D_GMLP
N_KEYS = 128
N_EXPERTS = N_KEYS * N_KEYS
PEER_HEADS = 8
D_KEY = 256
D_HALF = D_KEY // 2
TOPK = 16
TOKEN_BLOCK = 128
N_COND = 6
EPS = 1e-6

kernel_name = "hybrid_conv_gmlp_peer_adaln"

def rms_norm(x, g):
    xf = x.astype(jnp.float32)
    y = xf * lax.rsqrt(jnp.mean(xf * xf, axis=-1, keepdims=True) + EPS)
    return (y * g.astype(jnp.float32)).astype(x.dtype)

def group_layer_norm(x, n_groups, g, b):
    shp = x.shape
    xf = x.astype(jnp.float32).reshape(shp[:-1] + (n_groups, shp[-1] // n_groups))
    mu = jnp.mean(xf, axis=-1, keepdims=True)
    var = jnp.mean(jnp.square(xf - mu), axis=-1, keepdims=True)
    y = ((xf - mu) * lax.rsqrt(var + EPS)).reshape(shp)
    return (y * g.astype(jnp.float32) + b.astype(jnp.float32)).astype(x.dtype)

def conformer_conv_groups(a_val, a_gate, conv_w, conv_b, g_ln, b_ln):
    a = a_val * jax.nn.sigmoid(a_gate)
    y = lax.conv_general_dilated(
        a, conv_w[:, None, :].astype(a.dtype), window_strides=(1,),
        padding=[(CONV_WIDTH - 1, 0)],
        dimension_numbers=('NWC', 'WIO', 'NWC'),
        feature_group_count=D_CONV) + conv_b
    y = group_layer_norm(y, N_CONV_GROUPS, g_ln, b_ln)
    return jax.nn.silu(y)

def gmlp_groups(z, w_s, b_s, g_ln, b_ln, mask):
    B, S, _ = z.shape
    z = jax.nn.gelu(z)
    u, v = jnp.split(z, 2, axis=-1)
    v = group_layer_norm(v, N_GMLP_HEADS, g_ln, b_ln)
    v = v.reshape(B, S // CHUNK, CHUNK, N_GMLP_HEADS, GMLP_HEAD_DIM)
    mixed = jnp.einsum('hts,bnshd->bnthd', w_s * mask, v)
    mixed = mixed + jnp.transpose(b_s)[None, None, :, :, None]
    return u * mixed.reshape(B, S, D_GMLP)

def peer_ffn(h, w_q, sub_keys, expert_u, expert_v):
    B, S, D = h.shape
    T = B * S
    hf = h.reshape(T, D)
    q = (hf @ w_q).reshape(T, PEER_HEADS, 2, D_HALF)
    s = jnp.einsum('thid,hind->thin', q, sub_keys)
    sv, si = lax.top_k(s, TOPK)
    cand = (sv[:, :, 0, :, None] + sv[:, :, 1, None, :]).reshape(T, PEER_HEADS, TOPK * TOPK)
    cidx = (si[:, :, 0, :, None] * N_KEYS + si[:, :, 1, None, :]).reshape(T, PEER_HEADS, TOPK * TOPK)
    top_s, pos = lax.top_k(cand, TOPK)
    eidx = jnp.take_along_axis(cidx, pos, axis=-1)
    gates = jax.nn.softmax(top_s.astype(jnp.float32), axis=-1).astype(h.dtype)
    nb = T // TOKEN_BLOCK

    def apply_block(args):
        hb, eb, gb = args
        u = expert_u[eb]
        act = jax.nn.gelu(jnp.einsum('thkd,td->thk', u, hb)) * gb
        return jnp.einsum('thk,thkd->td', act, expert_v[eb])

    y = lax.map(apply_block, (hf.reshape(nb, TOKEN_BLOCK, D),
                              eidx.reshape(nb, TOKEN_BLOCK, PEER_HEADS, TOPK),
                              gates.reshape(nb, TOKEN_BLOCK, PEER_HEADS, TOPK)))
    return y.reshape(B, S, D)

def setup_inputs(seed: int = 0) -> dict:
    key = jax.random.key(seed)
    ks = jax.random.split(key, 24)
    n = jax.random.normal
    L, D = DEPTH, D_MODEL
    return {
        "x": n(ks[0], (BATCH, SEQ, D), jnp.float32),
        "c": n(ks[1], (BATCH, D), jnp.float32),
        "w_ada": n(ks[2], (L, D, N_COND * D), jnp.float32) * (0.5 * D ** -0.5),
        "b_ada": n(ks[3], (L, N_COND * D), jnp.float32) * 0.02,
        "g_norm1": 1.0 + 0.02 * n(ks[4], (L, D), jnp.float32),
        "w_in": n(ks[5], (L, D, N_PROJ), jnp.float32) * D ** -0.5,
        "b_in": n(ks[6], (L, N_PROJ), jnp.float32) * 0.02,
        "conv_w": n(ks[7], (L, CONV_WIDTH, D_CONV), jnp.float32) * CONV_WIDTH ** -0.5,
        "conv_b": n(ks[8], (L, D_CONV), jnp.float32) * 0.02,
        "g_conv_ln": 1.0 + 0.02 * n(ks[9], (L, D_CONV), jnp.float32),
        "b_conv_ln": n(ks[10], (L, D_CONV), jnp.float32) * 0.02,
        "g_v_ln": 1.0 + 0.02 * n(ks[11], (L, D_GMLP), jnp.float32),
        "b_v_ln": n(ks[12], (L, D_GMLP), jnp.float32) * 0.02,
        "w_spatial": n(ks[13], (L, N_GMLP_HEADS, CHUNK, CHUNK), jnp.float32) * CHUNK ** -0.5,
        "b_spatial": 1.0 + 0.02 * n(ks[14], (L, N_GMLP_HEADS, CHUNK), jnp.float32),
        "w_out": n(ks[15], (L, D_MIX, D), jnp.float32) * D_MIX ** -0.5,
        "b_out": n(ks[16], (L, D), jnp.float32) * 0.02,
        "g_norm2": 1.0 + 0.02 * n(ks[17], (L, D), jnp.float32),
        "w_query": n(ks[18], (L, D, PEER_HEADS * D_KEY), jnp.float32) * D ** -0.5,
        "sub_keys": n(ks[19], (L, PEER_HEADS, 2, N_KEYS, D_HALF), jnp.float32) * D_HALF ** -0.5,
        "expert_u": n(ks[20], (L, N_EXPERTS, D), jnp.float32) * D ** -0.5,
        "expert_v": n(ks[21], (L, N_EXPERTS, D), jnp.float32) * PEER_HEADS ** -0.5,
        "g_final": 1.0 + 0.02 * n(ks[22], (D,), jnp.float32),
    }

def reference(x, c, w_ada, b_ada, g_norm1, w_in, b_in, conv_w, conv_b, g_conv_ln, b_conv_ln,
              g_v_ln, b_v_ln, w_spatial, b_spatial, w_out, b_out, g_norm2, w_query, sub_keys,
              expert_u, expert_v, g_final):
    mask = jnp.tril(jnp.ones((CHUNK, CHUNK), dtype=w_spatial.dtype))
    for l in range(DEPTH):
        cond = jax.nn.silu(c) @ w_ada[l] + b_ada[l]
        sh1, sc1, gt1, sh2, sc2, gt2 = jnp.split(cond[:, None, :], N_COND, axis=-1)
        h = rms_norm(x, g_norm1[l]) * (1.0 + sc1) + sh1
        p = h @ w_in[l] + b_in[l]
        a_val, a_gate, z = jnp.split(p, [D_CONV, 2 * D_CONV], axis=-1)
        ya = conformer_conv_groups(a_val, a_gate, conv_w[l], conv_b[l], g_conv_ln[l], b_conv_ln[l])
        yb = gmlp_groups(z, w_spatial[l], b_spatial[l], g_v_ln[l], b_v_ln[l], mask)
        y = jnp.concatenate([ya, yb], axis=-1) @ w_out[l] + b_out[l]
        x = x + gt1 * y
        h2 = rms_norm(x, g_norm2[l]) * (1.0 + sc2) + sh2
        x = x + gt2 * peer_ffn(h2, w_query[l], sub_keys[l], expert_u[l], expert_v[l])
    return rms_norm(x, g_final)


_drawn_inputs = setup_inputs


def setup_inputs(seed=0):
    import zlib

    import numpy as np

    out = dict(_drawn_inputs(seed))
    spreads = {}
    factors = {'b_ada': 2.931,
     'g_norm1': 8.0,
     'b_in': 8.0,
     'conv_b': 64.0,
     'g_conv_ln': 200.0,
     'b_conv_ln': 200.0,
     'g_v_ln': 38.602,
     'b_v_ln': 39.975,
     'b_spatial': 28.463,
     'b_out': 198.225,
     'g_norm2': 54.352,
     'g_final': 22.212}
    for name, (base, spread) in spreads.items():
        noise = np.random.default_rng([zlib.crc32(name.encode()), seed]).standard_normal(out[name].shape)
        drawn = base * np.exp(spread * noise) if base else spread * noise
        out[name] = __import__('jax').numpy.asarray(drawn.astype(out[name].dtype))
    for name, factor in factors.items():
        out[name] = (out[name] * factor).astype(out[name].dtype)
    return out
```

```python
from contextlib import ExitStack

import concourse.bass as bass
from concourse import mybir

F32 = mybir.dt.float32
U32 = mybir.dt.uint32
I32 = mybir.dt.int32
ALU = mybir.AluOpType
ACT = mybir.ActivationFunctionType
AX = mybir.AxisListType

P = 128
D = 1024
DT = D // P
SEQ = 1024
NB = SEQ // P
DC = D // 2
CT = DC // P
TAPS = 31
CARRY = TAPS - 1
GROUPS = 8
GW = DC // GROUPS
N_PROJ = 2 * D
N_COND = 6
HEADS = 8
NK = 128
TOPK = 16
QT = 2 * HEADS
PAIRS = HEADS * TOPK
EPS = 1e-6
BELOW_ALL = -3.0e38
BANK = 512


class ClearedChain:

    def __init__(self, eng, sem, per_round):
        self.eng, self.sem, self.per_round, self.n = eng, sem, per_round, 0

    def round(self, first):
        if not first:
            self.eng.wait_ge(self.sem, self.per_round)
            self.eng.sem_clear(self.sem)
        self.n = 0

    def did(self, ins):
        ins.then_inc(self.sem, 1)
        self.n += 1

    def wait(self):
        self.eng.wait_ge(self.sem, self.n)

    def end(self):
        assert self.n == self.per_round, (self.n, self.per_round)


class Chain:

    def __init__(self, eng, sem, per_round=0):
        self.eng, self.sem, self.per_round = eng, sem, per_round
        self.base, self.n = 0, 0

    def round(self, b):
        self.base, self.n = b * self.per_round, 0

    def did(self, ins):
        ins.then_inc(self.sem, 1)
        self.n += 1

    def wait(self, behind=0):
        self.eng.wait_ge(self.sem, self.base + (self.n - behind))

    def end(self):
        assert self.n == self.per_round, (self.n, self.per_round)


def build(nc, x, c, w_ada, b_ada, g_norm1, w_in, b_in, conv_w, conv_b, g_conv_ln, b_conv_ln, g_v_ln,
          b_v_ln, w_spatial, b_spatial, w_out, b_out, g_norm2, w_query, sub_keys, expert_u, expert_v,
          g_final, out):
    cond_dram = nc.dram_tensor("cond_scratch", [N_COND * D], F32).ap()
    x1_dram = nc.dram_tensor("x1_scratch", [SEQ, D], F32).ap()
    with ExitStack() as ctx:
        ident = ctx.enter_context(nc.sbuf_tensor("ident", [P, P], F32))
        ss2 = ctx.enter_context(nc.sbuf_tensor("ss2", [P, NB], F32))
        eps = ctx.enter_context(nc.sbuf_tensor("eps", [P, 1], F32))
        keysT = ctx.enter_context(nc.sbuf_tensor("keysT", [P, QT, NK], F32))
        w_proj = ctx.enter_context(nc.sbuf_tensor("w_proj", [P, DT, N_PROJ], F32))
        w_q_loaded = ctx.enter_context(nc.semaphore("w_q_loaded"))
        with ExitStack() as mix:
            consts = setup_block(nc, mix, ident, eps, keysT, w_proj, cond_dram, x, c, w_ada, b_ada, g_norm1, w_in, b_in,
                                 conv_w, conv_b, g_conv_ln, b_conv_ln, g_v_ln, b_v_ln, w_spatial,
                                 b_spatial, w_out, b_out, sub_keys)
            mixer_block(nc, consts, w_proj, ident, eps, ss2, x1_dram, w_query, w_q_loaded)
        experts_block(nc, w_proj, w_q_loaded, keysT, ident, eps, ss2, x1_dram, cond_dram, g_norm2,
                      expert_u, expert_v, g_final, out)


def broadcast(row):
    return row.partition_broadcast(P)


def setup_block(nc, mix, ident, eps, keysT, w_proj, cond_dram, x, c, w_ada, b_ada, g_norm1, w_in, b_in, conv_w, conv_b,
                g_conv_ln, b_conv_ln, g_v_ln, b_v_ln, w_spatial, b_spatial, w_out, b_out, sub_keys):
    k = {}

    def keep(name, shape):
        k[name] = mix.enter_context(nc.sbuf_tensor(name, shape, F32))
        return k[name]

    w_in_sb = w_proj
    w_out_sb = keep("w_out_sb", [P, DT, D])
    x_all = keep("x_all", [P, NB, D])
    rs1 = keep("rs1", [P, NB])
    g1_col = keep("g1_col", [P, DT])
    sh1_col = keep("sh1_col", [P, DT])
    cols = keep("cols", [P, 36])
    gate_bias = keep("gate_bias", [P, CT])
    conv_taps = keep("conv_taps", [P, CT, TAPS])
    ws = keep("ws", [P, GROUPS, P])
    rows = keep("rows", [P, 6, DC])
    gt1 = keep("gt1", [P, D])
    gt1_b_out = keep("gt1_b_out", [P, D])
    C, G1, BIN, CB, BS = (0, 8), (8, 8), (16, 8), (24, 4), (28, 8)
    k["bv_col"], k["cb_col"], k["bs_col"] = cols[:, 16:20], cols[:, 24:28], cols[:, 28:36]
    bz, g_conv, b_conv, g_v, b_v = rows[:, 0:2, :], rows[:, 2, :], rows[:, 3, :], rows[:, 4, :], rows[:, 5, :]
    k.update(bz=bz, g_conv=g_conv, b_conv=b_conv, g_v=g_v, b_v=b_v)
    NCH = N_COND * D // BANK

    with ExitStack() as ctx:
        def sb(name, shape):
            return ctx.enter_context(nc.sbuf_tensor(name, shape, F32))

        def sem(name):
            return ctx.enter_context(nc.semaphore(name))

        staged = sb("staged", [36, P])
        staged_cond = sb("staged_cond", [16, P])
        taps_rows = sb("taps_rows", [TAPS, DC])
        silu_half = sb("silu_half", [P, DT])
        silu_tanh = sb("silu_tanh", [P, DT])
        silu_c = sb("silu_c", [P, DT])
        cond_row = sb("cond_row", [1, 2, BANK])
        bada_row = sb("bada_row", [1, 2, BANK])
        one_plus = sb("one_plus", [P, DT])
        mean_sq = sb("mean_sq", [P, NB])
        rms = sb("rms", [P, NB])
        w_ada_all = sb("w_ada_sb", [P, 2, DT, BANK])
        w_ada_sb = [w_ada_all[:, i, :, :] for i in range(2)]
        junk = w_out_sb[:, 0, :]
        ws_raw = w_out_sb[:, 1, :].rearrange("p (h s) -> p h s", h=GROUPS)
        keys_raw = w_out_sb[:, 2:4, :].rearrange("p a (t d) -> p (a t) d", d=P)
        rows_ps = ctx.enter_context(nc.psum_tensor("rows_ps", [P, BANK], F32))
        taps_ps = ctx.enter_context(nc.psum_tensor("taps_ps", [P, CT, TAPS + 1], F32))
        ws_ps = ctx.enter_context(nc.psum_tensor("ws_ps", [P, GROUPS, P], F32))
        cond_ps = [ctx.enter_context(nc.psum_tensor(f"cond_ps{i}", [P, BANK], F32)) for i in range(2)]

        ident_done = sem("ident_done")
        eps_set = sem("eps_set")
        small_loaded = sem("small_loaded")
        keys_loaded = sem("keys_loaded")
        rows_loaded = sem("rows_loaded")
        x_loaded = sem("x_loaded")
        w_ada_loaded = [sem(f"w_ada_loaded{i}") for i in range(2)]
        b_ada_loaded = [sem(f"b_ada_loaded{i}") for i in range(2)]
        w_loaded = sem("w_loaded")
        cols_transposed = sem("cols_transposed")
        cols_ready = sem("cols_ready")
        silu_halved = sem("silu_halved")
        tanh_done = sem("tanh_done")
        silu_ready = sem("silu_ready")
        taps_transposed = sem("taps_transposed")
        ws_transposed = sem("ws_transposed")
        ws_copied = sem("ws_copied")
        ws_masked = sem("ws_masked")
        cond_done = sem("cond_done")
        cond_added = sem("cond_added")
        cond_stored = [sem(f"cond_stored{i}") for i in range(2)]
        cond_reloaded = sem("cond_reloaded")
        cond_transposed = sem("cond_transposed")
        gt1_loaded = sem("gt1_loaded")
        squares_done = sem("squares_done")
        rms_done = sem("rms_done")
        dve_chain = sem("setup_dve_chain")
        block = ctx.enter_context(nc.Block())

        @block.sync
        def _(sp):
            w_in_v = w_in[0].rearrange("(t p) n -> p t n", p=P)
            w_ada_v = w_ada[0].rearrange("(t p) n -> p t n", p=P)
            b_ada_v = b_ada.rearrange("l (g n) -> l g n", n=BANK)
            sp.dma_start(staged[C[0]:C[0] + C[1], :], c[0].rearrange("(t p) -> t p", p=P)).then_inc(small_loaded, 16)
            sp.dma_start(staged[G1[0]:G1[0] + G1[1], :], g_norm1[0].rearrange("(t p) -> t p", p=P)).then_inc(small_loaded, 16)
            sp.dma_start(staged[BIN[0]:BIN[0] + BIN[1], :], b_in[0, 0:D].rearrange("(t p) -> t p", p=P)).then_inc(small_loaded, 16)
            sp.dma_start(staged[CB[0]:CB[0] + CB[1], :], conv_b[0].rearrange("(t p) -> t p", p=P)).then_inc(small_loaded, 16)
            sp.dma_start(staged[BS[0]:BS[0] + BS[1], :], b_spatial[0]).then_inc(small_loaded, 16)
            sp.dma_start(taps_rows[:, :], conv_w[0]).then_inc(small_loaded, 16)
            sp.dma_start(ws_raw, w_spatial[0].rearrange("h t s -> t h s")).then_inc(small_loaded, 16)
            sp.dma_start(keys_raw, sub_keys[0].rearrange("h i n d -> n (h i) d")).then_inc(keys_loaded, 16)
            for g in range(NCH):
                i = g % 2
                if g >= 2:
                    sp.wait_ge(cond_done, g - 1)
                    sp.wait_ge(cond_added, g - 1)
                sp.dma_start(w_ada_sb[i], w_ada_v[:, :, g * BANK:(g + 1) * BANK]).then_inc(w_ada_loaded[i], 16)
                sp.dma_start(bada_row[:, i, :], b_ada_v[:, g, :]).then_inc(b_ada_loaded[i], 16)
                if g >= 1:
                    sp.wait_ge(cond_added, g)
                    sp.dma_start(cond_dram[(g - 1) * BANK:g * BANK].rearrange("(a n) -> a n", a=1),
                                 cond_row[:, (g - 1) % 2, :]).then_inc(cond_stored[(g - 1) % 2], 16)
                if g == 1:
                    for r, row in ((0, b_in[0, D:D + DC]), (1, b_in[0, D + DC:2 * D]), (2, g_conv_ln[0]),
                                   (3, b_conv_ln[0]), (4, g_v_ln[0]), (5, b_v_ln[0])):
                        sp.dma_start(rows[:, r, :], broadcast(row)).then_inc(rows_loaded, 16)
                    sp.dma_start(gt1_b_out[:, :], broadcast(b_out[0])).then_inc(rows_loaded, 16)
                    sp.dma_start(x_all[:, :, :], x[0].rearrange("(b p) d -> p b d", p=P)).then_inc(x_loaded, 16)
                if 2 <= g < 2 + DT // 2:
                    t = 2 * (g - 2)
                    sp.dma_start(w_in_sb[:, t:t + 2, :], w_in_v[:, t:t + 2, :]).then_inc(w_loaded, 16)
            sp.wait_ge(cond_added, NCH)
            sp.dma_start(cond_dram[(NCH - 1) * BANK:].rearrange("(a n) -> a n", a=1),
                         cond_row[:, (NCH - 1) % 2, :]).then_inc(cond_stored[(NCH - 1) % 2], 16)
            sp.wait_ge(squares_done, NB)
            sp.wait_ge(ws_transposed, 1 + QT // DT)
            sp.dma_start(w_out_sb[:, :, :], w_out[0].rearrange("(t p) n -> p t n", p=P)).then_inc(w_loaded, 16)
            for i in range(2):
                sp.wait_ge(cond_stored[i], 16 * NCH // 2)
            sp.dma_start(staged_cond[:, :], cond_dram[0:2 * D].rearrange("(t p) -> t p", p=P)).then_inc(cond_reloaded, 16)
            sp.dma_start(gt1[:, :], broadcast(cond_dram[2 * D:3 * D])).then_inc(gt1_loaded, 16)
            sp.wait_ge(w_loaded, 16 * (DT // 2 + 1))

        @block.gpsimd
        def _(pool):
            pool.memset(eps[:, :], EPS).then_inc(eps_set, 1)
            pool.memset(ident[:, :], 0.0).then_inc(ident_done, 1)
            pool.wait_ge(ident_done, 1)
            pool.affine_select(out=ident[:, :], in_=ident[:, :], compare_op=ALU.not_equal, fill=1.0, base=0,
                               pattern=[[-1, P]], channel_multiplier=1).then_inc(ident_done, 1)
            pool.wait_ge(ws_copied, 1)
            pool.affine_select(out=ws[:, :, :], in_=ws[:, :, :], compare_op=ALU.is_ge, fill=0.0, base=0,
                               pattern=[[0, GROUPS], [1, P]], channel_multiplier=-1).then_inc(ws_masked, 1)
            pool.wait_ge(ws_masked, 1)

        @block.scalar
        def _(act):
            act.wait_ge(silu_halved, 1)
            act.activation(silu_tanh[:, :], silu_half[:, :], ACT.Tanh).then_inc(tanh_done, 1)
            for i, to in enumerate((ws[:, :, :], keysT[:, 0:DT, :], keysT[:, DT:, :])):
                act.wait_ge(ws_transposed, i + 1)
                act.copy(to, ws_ps[:, :, :]).then_inc(ws_copied, 1)
            act.wait_ge(x_loaded, 16)
            for b in range(NB):
                if b:
                    act.wait_ge(squares_done, b)
                act.activation(junk, x_all[:, b, :], ACT.Square, accum_out=mean_sq[:, b:b + 1]).then_inc(squares_done, 1)
            act.wait_ge(squares_done, NB)
            act.wait_ge(eps_set, 1)
            act.activation(rms[:, :], mean_sq[:, :], ACT.Sqrt, scale=1.0 / D, bias=eps[:, :]).then_inc(rms_done, 1)

        @block.tensor
        def _(pe):
            pe.wait_ge(ident_done, 2)
            pe.wait_ge(small_loaded, 7 * 16)
            pe.transpose(rows_ps[:, 0:36], staged[:, :], ident[0:36, 0:36]).then_inc(cols_transposed, 1)
            for m in range(CT):
                last = pe.transpose(taps_ps[:, m, 0:TAPS], taps_rows[:, m * P:(m + 1) * P], ident[0:TAPS, 0:TAPS])
            last.then_inc(taps_transposed, 1)
            for h in range(GROUPS):
                last = pe.transpose(ws_ps[:, h, :], ws_raw[:, h, :], ident[:, :])
            last.then_inc(ws_transposed, 1)
            pe.wait_ge(keys_loaded, 16)
            for i in range(QT // DT):
                pe.wait_ge(ws_copied, i + 1)
                for t in range(DT):
                    last = pe.transpose(ws_ps[:, t, :], keys_raw[:, i * DT + t, :], ident[:, :])
                last.then_inc(ws_transposed, 1)
            pe.wait_ge(silu_ready, 1)
            for g in range(NCH):
                pe.wait_ge(w_ada_loaded[g % 2], 16 * (g // 2 + 1))
                if g >= 2:
                    pe.wait_ge(cond_added, g - 1)
                for t in range(DT):
                    last = pe.matmul(cond_ps[g % 2][0:1, :], silu_c[:, t:t + 1], w_ada_sb[g % 2][:, t, :],
                                     start=(t == 0), stop=(t == DT - 1))
                last.then_inc(cond_done, 1)
            pe.wait_ge(cond_reloaded, 16)
            pe.wait_ge(cols_ready, 1)
            pe.transpose(rows_ps[:, 64:80], staged_cond[:, :], ident[0:16, 0:16]).then_inc(cond_transposed, 1)

        @block.vector
        def _(dve):
            ch = Chain(dve, dve_chain)
            dve.wait_ge(cols_transposed, 1)
            dve.tensor_copy(cols[:, :], rows_ps[:, 0:36]).then_inc(cols_ready, 1)
            dve.wait_ge(cols_ready, 1)
            dve.tensor_scalar(silu_half[:, :], cols[:, 0:DT], 0.5, None, ALU.mult).then_inc(silu_halved, 1)
            ch.did(dve.tensor_scalar(gate_bias[:, :], cols[:, 20:24], 0.5, None, ALU.mult))
            dve.wait_ge(tanh_done, 1)
            dve.wait_ge(silu_halved, 1)
            dve.scalar_tensor_tensor(out=silu_c[:, :], in0=silu_tanh[:, :], scalar=1.0, in1=silu_half[:, :],
                                     op0=ALU.add, op1=ALU.mult).then_inc(silu_ready, 1)
            dve.wait_ge(taps_transposed, 1)
            ch.did(dve.tensor_copy(conv_taps[:, :, :], taps_ps[:, :, 0:TAPS]))
            for g in range(NCH):
                dve.wait_ge(cond_done, g + 1)
                dve.wait_ge(b_ada_loaded[g % 2], 16 * (g // 2 + 1))
                if g >= 2:
                    dve.wait_ge(cond_stored[g % 2], 16 * (g // 2))
                dve.tensor_tensor(cond_row[:, g % 2, :], cond_ps[g % 2][0:1, :], bada_row[:, g % 2, :],
                                  ALU.add).then_inc(cond_added, 1)
            dve.wait_ge(rows_loaded, 7 * 16)
            ch.did(dve.tensor_scalar(g_conv, g_conv, 0.5, None, ALU.mult))
            ch.did(dve.tensor_scalar(b_conv, b_conv, 0.5, None, ALU.mult))
            dve.wait_ge(rms_done, 1)
            ch.did(dve.reciprocal(rs1[:, :], rms[:, :]))
            dve.wait_ge(cond_transposed, 1)
            ch.did(dve.tensor_copy(sh1_col[:, :], rows_ps[:, 64:64 + DT]))
            ch.did(dve.tensor_scalar(one_plus[:, :], rows_ps[:, 64 + DT:64 + 2 * DT], 1.0, None, ALU.add))
            ch.wait()
            ch.did(dve.tensor_tensor(g1_col[:, :], one_plus[:, :], cols[:, 8:16], ALU.mult))
            dve.wait_ge(gt1_loaded, 16)
            ch.did(dve.tensor_tensor(gt1_b_out[:, :], gt1_b_out[:, :], gt1[:, :], ALU.mult))
            ch.wait()
    return k


def mixer_block(nc, k, w_in_sb, ident, eps, ss2, x1_dram, w_query, w_q_loaded):
    K1, K2 = 8, 130
    w_out_sb, x_all, ws = k["w_out_sb"], k["x_all"], k["ws"]
    taps, cb, bv = k["conv_taps"], k["cb_col"], k["bv_col"]
    HALF = DT // 2
    with ExitStack() as ctx:
        def sb(name, shape):
            return ctx.enter_context(nc.sbuf_tensor(name, shape, F32))

        def ps(name, shape):
            return ctx.enter_context(nc.psum_tensor(name, shape, F32))

        def sem(name):
            return ctx.enter_context(nc.semaphore(name))

        xn = sb("xn", [P, D])
        hT = sb("hT", [P, DT, P])
        gate_tanh = sb("gate_tanh", [P, CT, P])
        a = sb("a", [P, CT, CARRY + P])
        acc = sb("acc", [P, CT, P])
        z = sb("z", [P, 2, DC])
        u = sb("u", [P, DC])
        v = sb("v", [P, GROUPS, GW])
        vn = sb("vn", [P, GROUPS, GW])
        squares = sb("squares", [P, GROUPS, GW])
        cc = sb("cc", [P, GROUPS, GW])
        total = sb("total", [P, 2, GROUPS])
        var = sb("var", [P, 2, GROUPS])
        std = sb("std", [P, 2, GROUPS])
        silu_tanh = sb("mix_silu_tanh", [P, DC])
        y_conv = sb("y_conv", [P, DC])
        y_gmlp = sb("y_gmlp", [P, GROUPS, GW])
        yT = sb("yT", [P, DT, P])
        yo = sb("yo", [P, D])
        turned_ps = ps("turned_ps", [P, DT, P])
        conv_ps = ps("conv_ps", [P, GROUPS, GW])
        val_ps = ps("val_ps", [P, CT, P])
        gates_ps = ps("gates_ps", [P, CT, P])
        wide_ps = ps("wide_ps", [P, 2, BANK])
        mixed_ps = ps("mixed_ps", [P, GROUPS, GW])

        xn_ready = sem("xn_ready")
        xn_turned = sem("xn_turned")
        hT_ready = sem("hT_ready")
        x_biased = sem("x_biased")
        gates_ready = sem("gates_ready")
        gate_tanh_ready = sem("gate_tanh_ready")
        val_ready = sem("val_ready")
        a_ready = sem("a_ready")
        z_ready = sem("z_ready")
        z_biased = sem("z_biased")
        gelu_done = sem("gelu_done")
        v_var = sem("v_var")
        v_std = sem("v_std")
        vn_ready = sem("vn_ready")
        mixed = sem("mixed")
        gmlp_ready = sem("gmlp_ready")
        conv_done = sem("conv_done")
        conv_turned = sem("conv_turned")
        conv_var = sem("conv_var")
        conv_std = sem("conv_std")
        conv_normed = sem("conv_normed")
        conv_tanh = sem("conv_tanh")
        y_ready = sem("y_ready")
        y_turned = sem("y_turned")
        yT_ready = sem("yT_ready")
        out_ready = sem("out_ready")
        carry_cleared = sem("carry_cleared")
        out_taken = sem("out_taken")
        x1_ready = sem("x1_ready")
        x1_squared = sem("x1_squared")
        x1_stored = sem("x1_stored")
        chain1 = sem("chain1")
        chain2 = sem("chain2")
        block = ctx.enter_context(nc.Block())

        @block.sync
        def _(sp):
            x1_v = x1_dram.rearrange("(b p) d -> b p d", p=P)
            w_v = w_query[0].rearrange("(t p) n -> p t n", p=P)
            sp.wait_ge(z_ready, 2 * NB)
            for t in range(0, DT, 2):
                sp.dma_start(w_in_sb[:, t:t + 2, :], w_v[:, t:t + 2, :]).then_inc(w_q_loaded, 16)
            with sp.Fori(0, NB) as b:
                sp.wait_ge(x1_ready, b + 1)
                sp.dma_start(x1_v[b], x_all[:, b, :]).then_inc(x1_stored, 16)
            sp.wait_ge(x1_stored, 16 * NB)

        @block.gpsimd
        def _(pool):
            with pool.Fori(0, NB) as b:
                pool.wait_ge(xn_ready, b + 1)
                pool.tensor_tensor(x_all[:, b, :], x_all[:, b, :], k["gt1_b_out"][:, :], ALU.add).then_inc(x_biased, 1)

        @block.scalar
        def _(act):
            def norm(b):
                act.activation(xn[:, :], x_all[:, b, :], ACT.Copy, scale=k["rs1"][:, bass.ds(b, 1)]).then_inc(xn_ready, 1)

            def project_in(b):
                act.wait_ge(xn_turned, b + 1)
                for i in range(2):
                    for t in range(i * HALF, (i + 1) * HALF):
                        last = act.activation(hT[:, t, :], turned_ps[:, t, :], ACT.Identity,
                                              scale=k["g1_col"][:, t:t + 1], bias=k["sh1_col"][:, t:t + 1])
                    last.then_inc(hT_ready, 1)
                act.wait_ge(gates_ready, b + 1)
                for m in range(CT):
                    last = act.activation(gate_tanh[:, m, :], gates_ps[:, m, :], ACT.Tanh, scale=0.5,
                                          bias=k["gate_bias"][:, m:m + 1])
                last.then_inc(gate_tanh_ready, 1)
                for i, to in ((1, v[:, :, :].rearrange("p h c -> p (h c)")), (0, u[:, :])):
                    act.wait_ge(z_biased, 2 * b + 2 - i)
                    act.activation(to, z[:, i, :], ACT.Gelu_apprx_tanh).then_inc(gelu_done, 1)

            def project_in_end(b):
                act.wait_ge(v_var, b + 1)
                act.activation(std[:, 0, :], var[:, 0, :], ACT.Sqrt, scale=1.0 / GW, bias=eps[:, :]).then_inc(v_std, 1)

            def conv(b):
                act.wait_ge(conv_var, b + 1)
                act.activation(std[:, 1, :], var[:, 1, :], ACT.Sqrt, scale=1.0 / GW, bias=eps[:, :]).then_inc(conv_std, 1)
                act.wait_ge(conv_normed, b + 1)
                act.activation(silu_tanh[:, :], cc[:, :, :].rearrange("p h c -> p (h c)"), ACT.Tanh).then_inc(conv_tanh, 1)

            def turned(b):
                act.wait_ge(y_turned, b + 1)
                act.copy(yT[:, :, :], turned_ps[:, :, :]).then_inc(yT_ready, 1)

            norm(0)
            project_in(0)
            project_in_end(0)
            norm(1)
            project_in(1)
            project_in_end(1)
            conv(0)
            with act.Fori(1, NB - 1) as i:
                norm(i + 1)
                turned(i - 1)
                project_in(i + 1)
                project_in_end(i + 1)
                conv(i)
            turned(NB - 2)
            conv(NB - 1)
            turned(NB - 1)
            for b in range(NB):
                act.wait_ge(x1_ready, b + 1)
                if b:
                    act.wait_ge(x1_squared, b)
                act.activation(xn[:, :], x_all[:, b, :], ACT.Square, accum_out=ss2[:, b:b + 1]).then_inc(x1_squared, 1)

        @block.tensor
        def _(pe):
            def project_in(b, early=False):
                pe.wait_ge(xn_ready, b + 1)
                for t in range(DT):
                    last = pe.transpose(turned_ps[:, t, :], xn[:, t * P:(t + 1) * P], ident[:, :])
                last.then_inc(xn_turned, 1)
                for m, to, sig in ((CT, gates_ps, gates_ready), (0, val_ps, val_ready)):
                    for j in range(CT):
                        for t in range(DT):
                            if (m, j) == (CT, 0) and t % HALF == 0:
                                pe.wait_ge(hT_ready, 2 * b + (t // HALF + 1))
                            last = pe.matmul(to[:, j, :], w_in_sb[:, t, (m + j) * P:(m + j + 1) * P], hT[:, t, :],
                                             start=(t == 0), stop=(t == DT - 1))
                    last.then_inc(sig, 1)
                if not early:
                    pe.wait_ge(out_taken, b - 1)
                for i in (1, 0):
                    for t in range(DT):
                        last = pe.matmul(wide_ps[:, i, :], hT[:, t, :], w_in_sb[:, t, D + i * DC:D + (i + 1) * DC],
                                         start=(t == 0), stop=(t == DT - 1))
                    last.then_inc(z_ready, 1)

            def turn_y(b):
                pe.wait_ge(gmlp_ready, b + 1)
                pe.wait_ge(y_ready, b + 1)
                gm = y_gmlp[:, :, :].rearrange("p h c -> p (h c)")
                for t in range(DT):
                    src = (y_conv[:, :] if t < CT else gm)[:, (t % CT) * P:(t % CT + 1) * P]
                    last = pe.transpose(turned_ps[:, t, :], src, ident[:, :])
                last.then_inc(y_turned, 1)

            def mix(b):
                pe.wait_ge(vn_ready, b + 1)
                for h in range(GROUPS):
                    last = pe.matmul(mixed_ps[:, h, :], ws[:, h, :], vn[:, h, :], start=True, stop=True)
                last.then_inc(mixed, 1)

            def turn_conv(b):
                pe.wait_ge(conv_done, b + 1)
                for m in range(CT):
                    last = pe.transpose(conv_ps[:, 2 * m:2 * m + 2, :].rearrange("p g c -> p (g c)"), acc[:, m, :], ident[:, :])
                last.then_inc(conv_turned, 1)

            def project_out(b, tail=False):
                pe.wait_ge(yT_ready, b + 1)
                if tail:
                    pe.wait_ge(z_biased, 2 * NB)
                    pe.wait_ge(out_taken, b + 1)
                for i in range(2):
                    if not tail:
                        pe.wait_ge(z_biased, 2 * b + 6 - i)
                    for t in range(DT):
                        last = pe.matmul(wide_ps[:, i, :], yT[:, t, :], w_out_sb[:, t, i * BANK:(i + 1) * BANK],
                                         start=(t == 0), stop=(t == DT - 1))
                last.then_inc(out_ready, 1)

            project_in(0, early=True)
            mix(0)
            project_in(1, early=True)
            turn_conv(0)
            with pe.Fori(1, NB - 1) as i:
                turn_y(i - 1)
                mix(i)
                pe.wait_ge(yT_ready, i)
                project_in(i + 1)
                turn_conv(i)
                project_out(i - 1)
            turn_y(NB - 2)
            mix(NB - 1)
            turn_conv(NB - 1)
            project_out(NB - 2, tail=True)
            turn_y(NB - 1)
            project_out(NB - 1, tail=True)

        @block.vector
        def _(dve):
            ch1, ch2 = Chain(dve, chain1, K1), Chain(dve, chain2, K2)

            def over_groups(t):
                return t.unsqueeze(2).to_broadcast([P, GROUPS, GW])

            def moments(ch, src, centred, i, var_ready):
                ch.did(dve.tensor_reduce(total[:, i, :], src, AX.X, ALU.add))
                ch.wait()
                ch.did(dve.scalar_tensor_tensor(out=centred, in0=over_groups(total[:, i, :]), scalar=-1.0 / GW, in1=src,
                                                op0=ALU.mult, op1=ALU.add))
                ch.wait()
                ch.did(dve.tensor_tensor(squares[:, :, :], centred, centred, ALU.mult))
                ch.wait()
                dve.tensor_reduce(var[:, i, :], squares[:, :, :], AX.X, ALU.add).then_inc(var_ready, 1)

            def scaled(ch, t, i, std_ready, b, g, shift, ready):
                dve.wait_ge(std_ready, b + 1)
                ch.did(dve.reciprocal(std[:, i, :], std[:, i, :]))
                ch.wait()
                ch.did(dve.tensor_tensor(t, t, over_groups(std[:, i, :]), ALU.mult))
                ch.wait()
                ch.did(dve.tensor_tensor(t, t, g.rearrange("p (h c) -> p h c", h=GROUPS), ALU.mult))
                ch.wait()
                dve.tensor_tensor(t, t, shift.rearrange("p (h c) -> p h c", h=GROUPS), ALU.add).then_inc(ready, 1)

            def take_a(b):
                ch1.round(b)
                ch1.did(dve.tensor_copy(a[:, :, 0:CARRY], a[:, :, P:P + CARRY]))
                dve.wait_ge(gate_tanh_ready, b + 1)
                ch1.did(dve.tensor_scalar(gate_tanh[:, :, :], gate_tanh[:, :, :], 1.0, 0.5, ALU.add, ALU.mult))
                ch1.wait()
                dve.wait_ge(val_ready, b + 1)
                for m in range(CT):
                    last = dve.scalar_tensor_tensor(out=a[:, m, CARRY:], in0=val_ps[:, m, :], scalar=bv[:, m:m + 1],
                                                    in1=gate_tanh[:, m, :], op0=ALU.add, op1=ALU.mult)
                last.then_inc(a_ready, 1)

            def take_z(b):
                for i in (1, 0):
                    dve.wait_ge(z_ready, 2 * b + 2 - i)
                    dve.tensor_tensor(z[:, i, :], wide_ps[:, i, :], k["bz"][:, i, :], ALU.add).then_inc(z_biased, 1)
                dve.wait_ge(gelu_done, 2 * b + 1)
                moments(ch1, v[:, :, :], vn[:, :, :], 0, v_var)

            def norm_v(b):
                scaled(ch1, vn[:, :, :], 0, v_std, b, k["g_v"], k["b_v"], vn_ready)
                ch1.end()

            def conv(b):
                ch2.round(b)
                dve.wait_ge(a_ready, b + 1)
                for w in range(TAPS):
                    for m in range(CT):
                        src, tap = a[:, m, w:w + P], taps[:, m, w:w + 1]
                        if w == 0:
                            ch2.did(dve.tensor_scalar(acc[:, m, :], src, tap, cb[:, m:m + 1], ALU.mult, ALU.add))
                        else:
                            ch2.wait(behind=CT - 1)
                            ins = dve.scalar_tensor_tensor(out=acc[:, m, :], in0=src, scalar=tap, in1=acc[:, m, :],
                                                           op0=ALU.mult, op1=ALU.add)
                            if (w, m) == (TAPS - 1, CT - 1):
                                ins.then_inc(conv_done, 1)
                            else:
                                ch2.did(ins)

            def gate_mixed(b):
                dve.wait_ge(mixed, b + 1)
                dve.wait_ge(gelu_done, 2 * b + 2)
                ch2.did(dve.tensor_tensor(y_gmlp[:, :, :], mixed_ps[:, :, :], over_groups(k["bs_col"]), ALU.add))
                ch2.wait()
                gm = y_gmlp[:, :, :].rearrange("p h c -> p (h c)")
                dve.tensor_tensor(gm, gm, u[:, :], ALU.mult).then_inc(gmlp_ready, 1)

            def conv_moments(b):
                dve.wait_ge(conv_turned, b + 1)
                moments(ch2, conv_ps[:, :, :], cc[:, :, :], 1, conv_var)

            def conv_norm(b):
                scaled(ch2, cc[:, :, :], 1, conv_std, b, k["g_conv"], k["b_conv"], conv_normed)

            def conv_silu(b):
                dve.wait_ge(conv_normed, b + 1)
                dve.wait_ge(conv_tanh, b + 1)
                dve.scalar_tensor_tensor(out=y_conv[:, :], in0=silu_tanh[:, :], scalar=1.0,
                                         in1=cc[:, :, :].rearrange("p h c -> p (h c)"),
                                         op0=ALU.add, op1=ALU.mult).then_inc(y_ready, 1)
                ch2.end()

            def residual(b):
                dve.wait_ge(out_ready, b + 1)
                dve.tensor_tensor(yo[:, :], wide_ps[:, :, :].rearrange("p a n -> p (a n)"), k["gt1"][:, :],
                                  ALU.mult).then_inc(out_taken, 1)
                dve.wait_ge(out_taken, b + 2)
                dve.wait_ge(x_biased, b + 1)
                dve.tensor_tensor(x_all[:, b, :], x_all[:, b, :], yo[:, :], ALU.add).then_inc(x1_ready, 1)

            dve.memset(a[:, :, P:P + CARRY], 0.0).then_inc(carry_cleared, 1)
            dve.wait_ge(carry_cleared, 1)
            dve.sem_inc(out_taken, 1)
            take_a(0)
            take_z(0)
            norm_v(0)
            conv(0)
            gate_mixed(0)
            take_a(1)
            take_z(1)
            conv_moments(0)
            norm_v(1)
            conv_norm(0)
            conv_silu(0)
            with dve.Fori(1, NB - 1) as i:
                conv(i)
                gate_mixed(i)
                take_a(i + 1)
                take_z(i + 1)
                conv_moments(i)
                norm_v(i + 1)
                conv_norm(i)
                residual(i - 1)
                conv_silu(i)
            conv(NB - 1)
            gate_mixed(NB - 1)
            conv_moments(NB - 1)
            conv_norm(NB - 1)
            conv_silu(NB - 1)
            residual(NB - 2)
            dve.wait_ge(x1_ready, NB - 1)
            residual(NB - 1)


def experts_block(nc, w_q, w_q_loaded, keysT, ident, eps, ss2, x1_dram, cond_dram, g_norm2,
                  expert_u, expert_v, g_final, out):
    QG = 4
    HG = QG // 2
    NG = QT // QG
    KQ, KF = 181, 2
    with ExitStack() as ctx:
        def sb(name, shape, dt=F32):
            return ctx.enter_context(nc.sbuf_tensor(name, shape, dt))

        def ps(name, shape):
            return ctx.enter_context(nc.psum_tensor(name, shape, F32))

        def sem(name):
            return ctx.enter_context(nc.semaphore(name))

        slots = sb("slots", [P, TOPK, D])
        g2 = sb("g2", [P, D])
        sh2 = sb("sh2", [P, D])
        gt2 = sb("gt2", [P, D])
        gf = sb("gf", [P, D])
        x1_next = sb("x1_next", [P, D])
        h_next = sb("h_next", [P, D])
        h_cur = sb("h_cur", [P, D])
        hT = sb("h2T", [P, DT, P])
        qT = sb("qT", [P, QG, P])
        scores = sb("scores", [P, 2, QG, NK])
        beaten = sb("beaten", [P, 2, NK])
        top = sb("top", [P, QG, TOPK])
        top_at = sb("top_at", [P, QG, TOPK], U32)
        top_at_f = sb("top_at_f", [P, QG, TOPK])
        cand = sb("cand", [P, HG, TOPK, TOPK])
        cand2 = sb("cand2", [P, HG, TOPK * TOPK])
        best_at = sb("best_at", [P, HG, TOPK], U32)
        pos = sb("pos", [P, 2, HG, TOPK], U32)
        pos_f = sb("pos_f", [P, 2, HG * TOPK])
        onehot = sb("onehot", [P, HG * TOPK, TOPK])
        half_at = sb("half_at", [P, 2, HG * TOPK])
        best = sb("best", [P, HEADS, TOPK])
        expert_f = sb("expert_f", [P, PAIRS])
        sixteen = sb("sixteen", [P, TOPK])
        sixteen_i = sb("sixteen_i", [P, TOPK], I32)
        gate_sum = sb("gate_sum", [P, HEADS])
        experts = sb("experts", [P, NB, PAIRS], U32)
        gates = sb("gates", [P, NB, PAIRS])
        rs2 = sb("rs2", [P, NB])
        wanted = sb("wanted", [P, 2, TOPK], U32)
        dots = sb("dots", [P, 2, TOPK])
        dots_gelu = sb("dots_gelu", [P, 2, TOPK])
        coef = sb("coef", [P, 2, TOPK])
        diag = sb("diag", [P, 4, P])
        out_sb = sb("out_sb", [P, D])
        peer = sb("peer", [P, D])
        final_ss = sb("final_ss", [P, 1])
        final_rms = sb("final_rms", [P, 1])
        final_rs = sb("final_rs", [P, 1])
        y_ps = ps("y_ps", [P, 2, BANK])
        turned_ps = ps("turned2_ps", [P, DT, P])
        q_ps = ps("q_ps", [P, QG, P])
        s_ps = ps("s_ps", [P, QG, NK])

        rows2_loaded = sem("rows2_loaded")
        g2_ready = sem("g2_ready")
        rms2_ready = sem("rms2_ready")
        rs2_ready = sem("rs2_ready")
        iota_done = sem("iota_done")
        sixteen_ready = sem("sixteen_ready")
        x1_loaded = sem("x1_loaded")
        xn_ready = sem("xn2_ready")
        h_ready = sem("h_ready")
        h_turned = sem("h_turned")
        hT_ready = sem("h2T_ready")
        h_copied = sem("h_copied")
        q_ready = sem("q_ready")
        qT_ready = sem("qT_ready")
        s_ready = sem("s_ready")
        scores_ready = sem("scores_ready")
        scores_free = sem("scores_free")
        scores_seen = sem("scores_seen")
        less_max = sem("less_max")
        exp_done = sem("exp_done")
        chosen = sem("chosen")
        staged = sem("staged")
        claims = sem("claims")
        u_used = sem("u_used")
        slot_free = sem("slot_free")
        landed = [sem(f"landed{i}") for i in range(TOPK)]
        gelu_done = sem("dots_gelu_done")
        coef_ready = sem("coef_ready")
        diag_ready = sem("diag_ready")
        y_ready = sem("peer_ready")
        y_taken = sem("y_taken")
        x1_final_loaded = sem("x1_final_loaded")
        final_summed = sem("final_summed")
        final_squared = sem("final_squared")
        final_rooted = sem("final_rooted")
        out_ready = sem("final_ready")
        out_free = sem("out_free")
        chainq = sem("chainq")
        chainf = sem("chainf")
        setup_chain = sem("experts_setup_chain")
        block = ctx.enter_context(nc.Block())
        x1_v = x1_dram.rearrange("(b p) d -> b p d", p=P)
        out_v = out[0].rearrange("(b p) d -> b p d", p=P)

        @block.sync
        def _(sp):
            sp.dma_start(x1_next[:, :], x1_v[0]).then_inc(x1_loaded, 16)
            for to, row in ((sh2, cond_dram[3 * D:4 * D]), (h_cur, cond_dram[4 * D:5 * D]),
                            (gt2, cond_dram[5 * D:6 * D]), (g2, g_norm2[0]), (gf, g_final)):
                sp.dma_start(to[:, :], broadcast(row)).then_inc(rows2_loaded, 16)

            def finish(b):
                sp.wait_ge(out_free, 16 * b + 16)
                sp.dma_start(out_sb[:, :], x1_v[b]).then_inc(x1_final_loaded, 16)
                sp.wait_ge(out_ready, b + 1)
                sp.dma_start(out_v[b], out_sb[:, :]).then_inc(out_free, 16)

            with sp.Fori(0, NB - 1) as b:
                sp.wait_ge(xn_ready, b + 1)
                sp.dma_start(x1_next[:, :], x1_v[b + 1]).then_inc(x1_loaded, 16)
                finish(b)
            finish(NB - 1)
            sp.wait_ge(out_free, 16 * NB + 16)

        @block.gpsimd
        def _(pool):
            pool.iota(sixteen_i[:, :], pattern=[[1, TOPK]], base=0, channel_multiplier=0).then_inc(iota_done, 1)
            pool.sem_inc(out_free, 16)
            with pool.Fori(0, NB) as b:
                pool.wait_ge(chosen, b + 1)
                for h in range(HEADS):
                    n = b * HEADS + h
                    pool.tensor_copy(wanted[:, h % 2, :], experts[:, b, h * TOPK:(h + 1) * TOPK]).then_inc(staged, 1)
                    pool.wait_ge(staged, n + 1)
                    for j in range(TOPK):
                        pool.wait_ge(slot_free, n * TOPK + (j + 1))
                        pool.sem_inc(claims, 1)
                        pool.indirect_dma_start(slots[:, j, :], None, expert_u[0],
                                                bass.IndirectOffsetOnAxis(ap=wanted[:, h % 2, j:j + 1], axis=0)
                                                ).then_inc(landed[j], 16)
                    for j in range(TOPK):
                        pool.wait_ge(u_used, n * TOPK + (j + 1))
                        pool.sem_inc(claims, 1)
                        pool.indirect_dma_start(slots[:, j, :], None, expert_v[0],
                                                bass.IndirectOffsetOnAxis(ap=wanted[:, h % 2, j:j + 1], axis=0)
                                                ).then_inc(landed[j], 16)

        @block.scalar
        def _(act):
            def norm(b, first=False):
                if not first:
                    act.wait_ge(h_copied, b)
                act.wait_ge(x1_loaded, 16 * b + 16)
                act.activation(h_next[:, :], x1_next[:, :], ACT.Copy, scale=rs2[:, bass.ds(b, 1)]).then_inc(xn_ready, 1)

            def turned(b):
                act.wait_ge(h_turned, b + 1)
                act.copy(hT[:, :, :], turned_ps[:, :, :]).then_inc(hT_ready, 1)

            def query(b, g):
                act.wait_ge(q_ready, NG * b + (g + 1))
                act.copy(qT[:, :, :], q_ps[:, :, :]).then_inc(qT_ready, 1)
                act.wait_ge(s_ready, NG * b + (g + 1))
                act.wait_ge(scores_free, NG * b + (g + 1))
                act.copy(scores[:, g % 2, :, :], s_ps[:, :, :]).then_inc(scores_ready, 1)

            def softmax(b):
                act.wait_ge(less_max, b + 1)
                act.activation(best[:, :, :], best[:, :, :], ACT.Exp).then_inc(exp_done, 1)

            def head(b, h):
                n = b * HEADS + h
                act.wait_ge(u_used, (n + 1) * TOPK)
                act.activation(dots_gelu[:, h % 2, :], dots[:, h % 2, :], ACT.Gelu_apprx_tanh).then_inc(gelu_done, 1)
                act.wait_ge(coef_ready, n + 1)
                for j in range(TOPK):
                    act.wait_ge(slot_free, n * TOPK + (j + 1 + TOPK - 4))
                    act.activation(diag[:, j % 4, :], ident[:, :], ACT.Copy,
                                   scale=coef[:, h % 2, j:j + 1]).then_inc(diag_ready, 1)

            def final(b):
                act.wait_ge(final_summed, b + 1)
                act.activation(peer[:, :], out_sb[:, :], ACT.Square, accum_out=final_ss[:, :]).then_inc(final_squared, 1)
                act.wait_ge(final_squared, b + 1)
                act.activation(final_rms[:, :], final_ss[:, :], ACT.Sqrt, scale=1.0 / D, bias=eps[:, :]).then_inc(final_rooted, 1)

            act.activation(rs2[:, :], ss2[:, :], ACT.Sqrt, scale=1.0 / D, bias=eps[:, :]).then_inc(rms2_ready, 1)
            act.wait_ge(rs2_ready, 1)

            def piece(b, h, first=False):
                if h == 0:
                    norm(b, first)
                elif h == 1:
                    turned(b)
                elif h < 2 + NG:
                    query(b, h - 2)
                elif h == 7:
                    softmax(b)

            for h in range(HEADS):
                piece(0, h, first=True)
            with act.Fori(0, NB - 1) as b:
                for h in range(HEADS):
                    head(b, h)
                    piece(b + 1, h)
                final(b)
            for h in range(HEADS):
                head(NB - 1, h)
            final(NB - 1)

        @block.tensor
        def _(pe):
            def turn(b):
                pe.wait_ge(h_ready, b + 1)
                for t in range(DT):
                    last = pe.transpose(turned_ps[:, t, :], h_next[:, t * P:(t + 1) * P], ident[:, :])
                last.then_inc(h_turned, 1)

            def query(b, g):
                pe.wait_ge(hT_ready, b + 1)
                for j in range(QG):
                    q = g * QG + j
                    for t in range(DT):
                        last = pe.matmul(q_ps[:, j, :], w_q[:, t, q * P:(q + 1) * P], hT[:, t, :],
                                         start=(t == 0), stop=(t == DT - 1))
                last.then_inc(q_ready, 1)
                pe.wait_ge(qT_ready, NG * b + (g + 1))
                for j in range(QG):
                    last = pe.matmul(s_ps[:, j, :], qT[:, j, :], keysT[:, g * QG + j, :], start=True, stop=True)
                last.then_inc(s_ready, 1)

            def head(b, h):
                n = b * HEADS + h
                for j in range(TOPK):
                    pe.wait_ge(diag_ready, n * TOPK + (j + 1))
                    pe.wait_ge(landed[j], 32 * n + 32)
                    if h == 0 and j == 0:
                        pe.wait_ge(y_taken, b + 1)
                    for i in range(2):
                        last = pe.matmul(y_ps[:, i, :], diag[:, j % 4, :], slots[:, j, i * BANK:(i + 1) * BANK],
                                         start=(h == 0 and j == 0), stop=(h == HEADS - 1 and j == TOPK - 1))
                    last.then_inc(slot_free, 1)

            pe.sem_inc(slot_free, TOPK)
            def piece(b, h):
                if h == 1:
                    turn(b)
                elif 2 <= h < 2 + NG:
                    query(b, h - 2)

            for h in range(HEADS):
                if h == 2:
                    pe.wait_ge(w_q_loaded, 16 * DT // 2)
                piece(0, h)
            with pe.Fori(0, NB - 1) as b:
                for h in range(HEADS):
                    head(b, h)
                    piece(b + 1, h)
            for h in range(HEADS):
                head(NB - 1, h)

        @block.vector
        def _(dve):
            cq, cf, cs = ClearedChain(dve, chainq, KQ), Chain(dve, chainf, KF), Chain(dve, setup_chain)

            def modulate(b):
                dve.wait_ge(xn_ready, b + 1)
                cq.did(dve.tensor_tensor(h_next[:, :], h_next[:, :], g2[:, :], ALU.mult))
                cq.wait()
                dve.tensor_tensor(h_next[:, :], h_next[:, :], sh2[:, :], ALU.add).then_inc(h_ready, 1)

            def top16(values, without, to, at):
                cq.did(dve.max(to[:, 0:8], values))
                cq.wait()
                cq.did(dve.max_index(at[:, 0:8], to[:, 0:8], values))
                cq.did(dve.match_replace(without, to[:, 0:8], values, BELOW_ALL))
                cq.wait()
                cq.did(dve.max(to[:, 8:16], without))
                cq.wait()
                cq.did(dve.max_index(at[:, 8:16], to[:, 8:16], without))

            def choose(b, g):
                dve.wait_ge(scores_ready, NG * b + (g + 1))
                dve.sem_inc(scores_seen, 1)
                for j in range(QG):
                    top16(scores[:, g % 2, j, :], beaten[:, j % 2, :], top[:, j, :], top_at[:, j, :])
                cq.wait()
                dve.tensor_copy(top_at_f[:, :, :], top_at[:, :, :]).then_inc(scores_free, 1)
                for i in range(HG):
                    first = top[:, 2 * i, :].unsqueeze(2).to_broadcast([P, TOPK, TOPK])
                    second = top[:, 2 * i + 1, :].unsqueeze(1).to_broadcast([P, TOPK, TOPK])
                    cq.did(dve.tensor_tensor(cand[:, i, :, :], first, second, ALU.add))
                cq.wait()
                for i in range(HG):
                    top16(cand[:, i, :, :].rearrange("p a b -> p (a b)"), cand2[:, i, :],
                          best[:, g * HG + i, :], best_at[:, i, :])
                cq.wait()
                cq.did(dve.tensor_scalar(pos[:, 0, :, :], best_at[:, :, :], 4, None, ALU.logical_shift_right))
                cq.did(dve.tensor_scalar(pos[:, 1, :, :], best_at[:, :, :], TOPK - 1, None, ALU.bitwise_and))
                cq.wait()
                cq.did(dve.tensor_copy(pos_f[:, :, :], pos[:, :, :, :].rearrange("p a h k -> p a (h k)")))
                dve.wait_ge(scores_free, NG * b + (g + 3))
                for i in range(2):
                    cq.wait()
                    cq.did(dve.tensor_tensor(onehot[:, :, :], pos_f[:, i, :].unsqueeze(2).to_broadcast([P, HG * TOPK, TOPK]),
                                             sixteen[:, :].unsqueeze(1).to_broadcast([P, HG * TOPK, TOPK]), ALU.is_equal))
                    cq.wait()
                    for hh in range(HG):
                        part = onehot[:, hh * TOPK:(hh + 1) * TOPK, :]
                        at = top_at_f[:, 2 * hh + i, :].unsqueeze(1).to_broadcast([P, TOPK, TOPK])
                        cq.did(dve.tensor_tensor(part, part, at, ALU.mult))
                    cq.wait()
                    cq.did(dve.tensor_reduce(half_at[:, i, :], onehot[:, :, :], AX.X, ALU.add))
                cq.wait()
                cq.did(dve.scalar_tensor_tensor(out=expert_f[:, g * HG * TOPK:(g + 1) * HG * TOPK], in0=half_at[:, 0, :],
                                                scalar=float(NK), in1=half_at[:, 1, :], op0=ALU.mult, op1=ALU.add))

            def over_heads(t):
                return t.to_broadcast([P, HEADS, TOPK])

            def less_maximum(b):
                cq.wait()
                cq.did(dve.tensor_copy(gate_sum[:, :].unsqueeze(2), best[:, :, 0:1]))
                cq.wait()
                dve.tensor_tensor(best[:, :, :], best[:, :, :], over_heads(gate_sum[:, :].unsqueeze(2)),
                                  ALU.subtract).then_inc(less_max, 1)

            def gate(b):
                dve.wait_ge(exp_done, b + 1)
                cq.did(dve.tensor_reduce(gate_sum[:, :], best[:, :, :], AX.X, ALU.add))
                cq.wait()
                cq.did(dve.reciprocal(gate_sum[:, :], gate_sum[:, :]))
                cq.wait()
                cq.did(dve.tensor_tensor(gates[:, b, :].rearrange("p (h k) -> p h k", h=HEADS), best[:, :, :],
                                         over_heads(gate_sum[:, :].unsqueeze(2)), ALU.mult))
                cq.wait()
                dve.tensor_copy(experts[:, b, :], expert_f[:, :]).then_inc(chosen, 1)
                dve.wait_ge(chosen, b + 1)
                cq.end()

            def head(b, h):
                n = b * HEADS + h
                if h == 0:
                    dve.wait_ge(h_copied, b + 1)
                for j in range(TOPK):
                    dve.wait_ge(landed[j], 32 * n + 16)
                    dve.tensor_tensor_reduce(out=slots[:, j, :], in0=slots[:, j, :], in1=h_cur[:, :], scale=1.0, scalar=0.0,
                                             op0=ALU.mult, op1=ALU.add, accum_out=dots[:, h % 2, j:j + 1]).then_inc(u_used, 1)
                dve.wait_ge(gelu_done, n + 1)
                dve.tensor_tensor(coef[:, h % 2, :], dots_gelu[:, h % 2, :], gates[:, b, h * TOPK:(h + 1) * TOPK],
                                  ALU.mult).then_inc(coef_ready, 1)

            def take_h(b):
                dve.wait_ge(h_ready, b + 1)
                dve.tensor_copy(h_cur[:, :], h_next[:, :]).then_inc(h_copied, 1)

            def final(b):
                cf.round(b)
                dve.wait_ge(slot_free, (b + 1) * PAIRS + TOPK)
                dve.tensor_tensor(peer[:, :], y_ps[:, :, :].rearrange("p a n -> p (a n)"), gt2[:, :],
                                  ALU.mult).then_inc(y_taken, 1)
                dve.wait_ge(y_taken, b + 2)
                dve.wait_ge(x1_final_loaded, 16 * b + 16)
                dve.tensor_tensor(out_sb[:, :], out_sb[:, :], peer[:, :], ALU.add).then_inc(final_summed, 1)
                dve.wait_ge(final_rooted, b + 1)
                cf.did(dve.reciprocal(final_rs[:, :], final_rms[:, :]))
                cf.wait()
                cf.did(dve.tensor_scalar(out_sb[:, :], out_sb[:, :], final_rs[:, :], None, ALU.mult))
                cf.wait()
                dve.tensor_tensor(out_sb[:, :], out_sb[:, :], gf[:, :], ALU.mult).then_inc(out_ready, 1)
                cf.end()

            def piece(b, h, first=False):
                if h == 0:
                    cq.round(first)
                    modulate(b)
                elif 3 <= h < 3 + NG:
                    choose(b, h - 3)
                elif h == 7:
                    less_maximum(b)
                    gate(b)

            dve.wait_ge(rms2_ready, 1)
            dve.reciprocal(rs2[:, :], rs2[:, :]).then_inc(rs2_ready, 1)
            dve.wait_ge(iota_done, 1)
            dve.tensor_copy(sixteen[:, :], sixteen_i[:, :]).then_inc(sixteen_ready, 1)
            dve.wait_ge(sixteen_ready, 1)
            dve.wait_ge(rows2_loaded, 5 * 16)
            cs.did(dve.tensor_scalar(h_cur[:, :], h_cur[:, :], 1.0, None, ALU.add))
            cs.wait()
            dve.tensor_tensor(g2[:, :], g2[:, :], h_cur[:, :], ALU.mult).then_inc(g2_ready, 1)
            dve.wait_ge(g2_ready, 1)
            dve.sem_inc(y_taken, 1)
            dve.sem_inc(scores_free, 2)
            for h in range(HEADS):
                piece(0, h, first=True)
            take_h(0)
            with dve.Fori(0, NB - 1) as b:
                for h in range(HEADS):
                    head(b, h)
                    piece(b + 1, h)
                take_h(b + 1)
                final(b)
            for h in range(HEADS):
                head(NB - 1, h)
            final(NB - 1)


_INS = ["x", "c", "w_ada", "b_ada", "g_norm1", "w_in", "b_in", "conv_w", "conv_b", "g_conv_ln", "b_conv_ln",
        "g_v_ln", "b_v_ln", "w_spatial", "b_spatial", "w_out", "b_out", "g_norm2", "w_query", "sub_keys",
        "expert_u", "expert_v", "g_final"]
_OUT = (1, SEQ, D)


def kernel(**inputs):
    import numpy as np
    import concourse.bacc as bacc
    from concourse.bass_utils import run_bass_kernel_spmd

    nc = bacc.Bacc("TRN2", target_bir_lowering=False, num_devices=1)
    arrays, args = {}, []
    for name in _INS:
        a = np.ascontiguousarray(inputs[name])
        arrays[f"in_{name}"] = a
        args.append(nc.dram_tensor(f"in_{name}", a.shape, mybir.dt.from_np(a.dtype), kind="ExternalInput").ap())
    out = nc.dram_tensor("out_0", _OUT, F32, kind="ExternalOutput").ap()
    build(nc, *args, out)
    r = run_bass_kernel_spmd(nc, [arrays], core_ids=[0])
    return r.results[0]["out_0"]
```

```python
from contextlib import ExitStack, contextmanager

import concourse.bass as bass
from concourse import mybir

F32 = mybir.dt.float32
U32 = mybir.dt.uint32
I32 = mybir.dt.int32
ALU = mybir.AluOpType
ACT = mybir.ActivationFunctionType
AX = mybir.AxisListType

P = 128
D = 1024
DT = D // P
SEQ = 1024
NB = SEQ // P
DC = D // 2
CT = DC // P
TAPS = 31
CARRY = TAPS - 1
GROUPS = 8
GW = DC // GROUPS
N_PROJ = 2 * D
N_COND = 6
HEADS = 8
NK = 128
TOPK = 16
QT = 2 * HEADS
PAIRS = HEADS * TOPK
EPS = 1e-6
BELOW_ALL = -3.0e38
NDENSE = 3
NGATHER = NB - NDENSE - 2
NCHUNK = 4
CHUNK = NDENSE * P // NCHUNK
BANK = 512


@contextmanager
def own_semaphores(nc):
    made = []

    def sem(name):
        made.append(nc.alloc_semaphore(name))
        return made[-1]

    yield sem
    nc.clear_and_free_semaphores(made)
    nc.all_engine_barrier()


class ClearedChain:

    def __init__(self, eng, sem, per_round):
        self.eng, self.sem, self.per_round, self.n = eng, sem, per_round, 0

    def round(self, first):
        if not first:
            self.eng.wait_ge(self.sem, self.per_round)
            self.eng.sem_clear(self.sem)
        self.n = 0

    def did(self, ins):
        ins.then_inc(self.sem, 1)
        self.n += 1

    def wait(self):
        self.eng.wait_ge(self.sem, self.n)

    def end(self):
        assert self.n == self.per_round, (self.n, self.per_round)


class Chain:

    def __init__(self, eng, sem, per_round=0):
        self.eng, self.sem, self.per_round = eng, sem, per_round
        self.base, self.n = 0, 0

    def round(self, b):
        self.base, self.n = b * self.per_round, 0

    def did(self, ins):
        ins.then_inc(self.sem, 1)
        self.n += 1

    def wait(self, behind=0):
        self.eng.wait_ge(self.sem, self.base + (self.n - behind))

    def end(self):
        assert self.n == self.per_round, (self.n, self.per_round)


def build(nc, x, c, w_ada, b_ada, g_norm1, w_in, b_in, conv_w, conv_b, g_conv_ln, b_conv_ln, g_v_ln,
          b_v_ln, w_spatial, b_spatial, w_out, b_out, g_norm2, w_query, sub_keys, expert_u, expert_v,
          g_final, out):
    cond_dram = nc.dram_tensor("cond_scratch", [N_COND * D], F32).ap()
    x1_dram = nc.dram_tensor("x1_scratch", [SEQ, D], F32).ap()
    h_dram = nc.dram_tensor("h_scratch", [NB, P, D], F32).ap()
    hT_dram = nc.dram_tensor("hT_scratch", [NB, P, D], F32).ap()
    y_dram = nc.dram_tensor("y_scratch", [2, P, D], F32).ap()
    table_dram = nc.dram_tensor("table_scratch", [NCHUNK, NK, NK, CHUNK], F32).ap()
    with ExitStack() as ctx:
        ident = ctx.enter_context(nc.sbuf_tensor("ident", [P, P], F32))
        eps = ctx.enter_context(nc.sbuf_tensor("eps", [P, 1], F32))
        ss2 = ctx.enter_context(nc.sbuf_tensor("ss2", [P, NB], F32))
        experts = ctx.enter_context(nc.sbuf_tensor("experts", [P, NB, PAIRS], U32))
        gates = ctx.enter_context(nc.sbuf_tensor("gates", [P, NB, PAIRS], F32))
        with ExitStack() as proj:
            keysT = proj.enter_context(nc.sbuf_tensor("keysT", [P, QT, NK], F32))
            w_proj = proj.enter_context(nc.sbuf_tensor("w_proj", [P, DT, N_PROJ], F32))
            w_q_loaded = proj.enter_context(nc.semaphore("w_q_loaded"))
            with ExitStack() as mix:
                consts = setup_block(nc, mix, ident, eps, keysT, w_proj, cond_dram, x, c, w_ada, b_ada, g_norm1,
                                     w_in, b_in, conv_w, conv_b, g_conv_ln, b_conv_ln, g_v_ln, b_v_ln,
                                     w_spatial, b_spatial, w_out, b_out, sub_keys)
                mixer_block(nc, consts, w_proj, ident, eps, ss2, experts, gates, x1_dram, w_query, w_q_loaded)
            routing_block(nc, w_proj, w_q_loaded, keysT, experts, gates, ident, eps, ss2, x1_dram, cond_dram,
                          h_dram, hT_dram, y_dram, g_norm2, expert_u, expert_v)
        table_block(nc, experts, gates, ident, h_dram, y_dram, table_dram, expert_u, expert_v)
        y_all = ctx.enter_context(nc.sbuf_tensor("y_all", [P, NB, D], F32))
        dense_block(nc, experts, gates, ident, y_all, h_dram, hT_dram, y_dram, table_dram, expert_u, expert_v)
        final_block(nc, y_all, eps, x1_dram, cond_dram, g_final, out)


def broadcast(row):
    return row.partition_broadcast(P)


def setup_block(nc, mix, ident, eps, keysT, w_proj, cond_dram, x, c, w_ada, b_ada, g_norm1, w_in, b_in, conv_w, conv_b,
                g_conv_ln, b_conv_ln, g_v_ln, b_v_ln, w_spatial, b_spatial, w_out, b_out, sub_keys):
    k = {}

    def keep(name, shape):
        k[name] = mix.enter_context(nc.sbuf_tensor(name, shape, F32))
        return k[name]

    w_in_sb = w_proj
    w_out_sb = keep("w_out_sb", [P, DT, D])
    x_all = keep("x_all", [P, NB, D])
    rs1 = keep("rs1", [P, NB])
    g1_col = keep("g1_col", [P, DT])
    sh1_col = keep("sh1_col", [P, DT])
    cols = keep("cols", [P, 36])
    gate_bias = keep("gate_bias", [P, CT])
    conv_taps = keep("conv_taps", [P, CT, TAPS])
    ws = keep("ws", [P, GROUPS, P])
    rows = keep("rows", [P, 6, DC])
    gt1 = keep("gt1", [P, D])
    gt1_b_out = keep("gt1_b_out", [P, D])
    C, G1, BIN, CB, BS = (0, 8), (8, 8), (16, 8), (24, 4), (28, 8)
    k["bv_col"], k["cb_col"], k["bs_col"] = cols[:, 16:20], cols[:, 24:28], cols[:, 28:36]
    bz, g_conv, b_conv, g_v, b_v = rows[:, 0:2, :], rows[:, 2, :], rows[:, 3, :], rows[:, 4, :], rows[:, 5, :]
    k.update(bz=bz, g_conv=g_conv, b_conv=b_conv, g_v=g_v, b_v=b_v)
    NCH = N_COND * D // BANK

    with own_semaphores(nc) as sem, ExitStack() as ctx:
        def sb(name, shape):
            return ctx.enter_context(nc.sbuf_tensor(name, shape, F32))

        staged = sb("staged", [36, P])
        staged_cond = sb("staged_cond", [16, P])
        silu_half = sb("silu_half", [P, DT])
        silu_tanh = sb("silu_tanh", [P, DT])
        silu_c = sb("silu_c", [P, DT])
        cond_row = sb("cond_row", [1, 2, BANK])
        one_plus = sb("one_plus", [P, DT])
        mean_sq = sb("mean_sq", [P, NB])
        rms = sb("rms", [P, NB])
        w_ada_all = sb("w_ada_sb", [P, 2, DT, BANK])
        w_ada_sb = [w_ada_all[:, i, :, :] for i in range(2)]
        junk = w_out_sb[:, 0, :]
        ws_raw = w_out_sb[:, 1, :].rearrange("p (h s) -> p h s", h=GROUPS)
        keys_raw = w_out_sb[:, 2:4, :].rearrange("p a (t d) -> p (a t) d", d=P)
        taps_rows = w_out_sb[0:TAPS, 4, 0:DC]
        bada_row = gt1[0:1, :].rearrange("p (a n) -> p a n", a=2)
        rows_ps = ctx.enter_context(nc.psum_tensor("rows_ps", [P, BANK], F32))
        taps_ps = ctx.enter_context(nc.psum_tensor("taps_ps", [P, CT, TAPS + 1], F32))
        ws_ps = ctx.enter_context(nc.psum_tensor("ws_ps", [P, GROUPS, P], F32))
        cond_ps = [ctx.enter_context(nc.psum_tensor(f"cond_ps{i}", [P, BANK], F32)) for i in range(2)]

        ident_done = sem("ident_done")
        eps_set = sem("eps_set")
        small_loaded = sem("small_loaded")
        keys_loaded = sem("keys_loaded")
        rows_loaded = sem("rows_loaded")
        x_loaded = sem("x_loaded")
        w_ada_loaded = [sem(f"w_ada_loaded{i}") for i in range(2)]
        b_ada_loaded = [sem(f"b_ada_loaded{i}") for i in range(2)]
        w_loaded = sem("w_loaded")
        cols_transposed = sem("cols_transposed")
        cols_ready = sem("cols_ready")
        silu_halved = sem("silu_halved")
        tanh_done = sem("tanh_done")
        silu_ready = sem("silu_ready")
        taps_transposed = sem("taps_transposed")
        ws_transposed = sem("ws_transposed")
        ws_copied = sem("ws_copied")
        ws_masked = sem("ws_masked")
        cond_done = sem("cond_done")
        cond_added = sem("cond_added")
        cond_stored = [sem(f"cond_stored{i}") for i in range(2)]
        cond_reloaded = sem("cond_reloaded")
        cond_transposed = sem("cond_transposed")
        gt1_loaded = sem("gt1_loaded")
        squares_done = sem("squares_done")
        rms_done = sem("rms_done")
        dve_chain = sem("setup_dve_chain")
        block = ctx.enter_context(nc.Block())

        @block.sync
        def _(sp):
            w_in_v = w_in[0].rearrange("(t p) n -> p t n", p=P)
            w_ada_v = w_ada[0].rearrange("(t p) n -> p t n", p=P)
            b_ada_v = b_ada.rearrange("l (g n) -> l g n", n=BANK)
            sp.dma_start(staged[C[0]:C[0] + C[1], :], c[0].rearrange("(t p) -> t p", p=P)).then_inc(small_loaded, 16)
            sp.dma_start(staged[G1[0]:G1[0] + G1[1], :], g_norm1[0].rearrange("(t p) -> t p", p=P)).then_inc(small_loaded, 16)
            sp.dma_start(staged[BIN[0]:BIN[0] + BIN[1], :], b_in[0, 0:D].rearrange("(t p) -> t p", p=P)).then_inc(small_loaded, 16)
            sp.dma_start(staged[CB[0]:CB[0] + CB[1], :], conv_b[0].rearrange("(t p) -> t p", p=P)).then_inc(small_loaded, 16)
            sp.dma_start(staged[BS[0]:BS[0] + BS[1], :], b_spatial[0]).then_inc(small_loaded, 16)
            sp.dma_start(taps_rows[:, :], conv_w[0]).then_inc(small_loaded, 16)
            sp.dma_start(ws_raw, w_spatial[0].rearrange("h t s -> t h s")).then_inc(small_loaded, 16)
            sp.dma_start(keys_raw, sub_keys[0].rearrange("h i n d -> n (h i) d")).then_inc(keys_loaded, 16)
            for g in range(NCH):
                i = g % 2
                if g >= 2:
                    sp.wait_ge(cond_done, g - 1)
                    sp.wait_ge(cond_added, g - 1)
                sp.dma_start(w_ada_sb[i], w_ada_v[:, :, g * BANK:(g + 1) * BANK]).then_inc(w_ada_loaded[i], 16)
                sp.dma_start(bada_row[:, i, :], b_ada_v[:, g, :]).then_inc(b_ada_loaded[i], 16)
                if g >= 1:
                    sp.wait_ge(cond_added, g)
                    sp.dma_start(cond_dram[(g - 1) * BANK:g * BANK].rearrange("(a n) -> a n", a=1),
                                 cond_row[:, (g - 1) % 2, :]).then_inc(cond_stored[(g - 1) % 2], 16)
                if g == 1:
                    for r, row in ((0, b_in[0, D:D + DC]), (1, b_in[0, D + DC:2 * D]), (2, g_conv_ln[0]),
                                   (3, b_conv_ln[0]), (4, g_v_ln[0]), (5, b_v_ln[0])):
                        sp.dma_start(rows[:, r, :], broadcast(row)).then_inc(rows_loaded, 16)
                    sp.dma_start(gt1_b_out[:, :], broadcast(b_out[0])).then_inc(rows_loaded, 16)
                    sp.dma_start(x_all[:, :, :], x[0].rearrange("(b p) d -> p b d", p=P)).then_inc(x_loaded, 16)
                if 2 <= g < 2 + DT // 2:
                    t = 2 * (g - 2)
                    sp.dma_start(w_in_sb[:, t:t + 2, :], w_in_v[:, t:t + 2, :]).then_inc(w_loaded, 16)
            sp.wait_ge(cond_added, NCH)
            sp.dma_start(cond_dram[(NCH - 1) * BANK:].rearrange("(a n) -> a n", a=1),
                         cond_row[:, (NCH - 1) % 2, :]).then_inc(cond_stored[(NCH - 1) % 2], 16)
            sp.wait_ge(squares_done, NB)
            sp.wait_ge(ws_transposed, 1 + QT // DT)
            sp.dma_start(w_out_sb[:, :, :], w_out[0].rearrange("(t p) n -> p t n", p=P)).then_inc(w_loaded, 16)
            for i in range(2):
                sp.wait_ge(cond_stored[i], 16 * NCH // 2)
            sp.dma_start(staged_cond[:, :], cond_dram[0:2 * D].rearrange("(t p) -> t p", p=P)).then_inc(cond_reloaded, 16)
            sp.dma_start(gt1[:, :], broadcast(cond_dram[2 * D:3 * D])).then_inc(gt1_loaded, 16)
            sp.wait_ge(w_loaded, 16 * (DT // 2 + 1))

        @block.gpsimd
        def _(pool):
            pool.memset(eps[:, :], EPS).then_inc(eps_set, 1)
            pool.memset(ident[:, :], 0.0).then_inc(ident_done, 1)
            pool.wait_ge(ident_done, 1)
            pool.affine_select(out=ident[:, :], in_=ident[:, :], compare_op=ALU.not_equal, fill=1.0, base=0,
                               pattern=[[-1, P]], channel_multiplier=1).then_inc(ident_done, 1)
            pool.wait_ge(ws_copied, 1)
            pool.affine_select(out=ws[:, :, :], in_=ws[:, :, :], compare_op=ALU.is_ge, fill=0.0, base=0,
                               pattern=[[0, GROUPS], [1, P]], channel_multiplier=-1).then_inc(ws_masked, 1)
            pool.wait_ge(ws_masked, 1)

        @block.scalar
        def _(act):
            act.wait_ge(silu_halved, 1)
            act.activation(silu_tanh[:, :], silu_half[:, :], ACT.Tanh).then_inc(tanh_done, 1)
            for i, to in enumerate((ws[:, :, :], keysT[:, 0:DT, :], keysT[:, DT:, :])):
                act.wait_ge(ws_transposed, i + 1)
                act.copy(to, ws_ps[:, :, :]).then_inc(ws_copied, 1)
            act.wait_ge(x_loaded, 16)
            for b in range(NB):
                if b:
                    act.wait_ge(squares_done, b)
                act.activation(junk, x_all[:, b, :], ACT.Square, accum_out=mean_sq[:, b:b + 1]).then_inc(squares_done, 1)
            act.wait_ge(squares_done, NB)
            act.wait_ge(eps_set, 1)
            act.activation(rms[:, :], mean_sq[:, :], ACT.Sqrt, scale=1.0 / D, bias=eps[:, :]).then_inc(rms_done, 1)

        @block.tensor
        def _(pe):
            pe.wait_ge(ident_done, 2)
            pe.wait_ge(small_loaded, 7 * 16)
            pe.transpose(rows_ps[:, 0:36], staged[:, :], ident[0:36, 0:36]).then_inc(cols_transposed, 1)
            for m in range(CT):
                last = pe.transpose(taps_ps[:, m, 0:TAPS], taps_rows[:, m * P:(m + 1) * P], ident[0:TAPS, 0:TAPS])
            last.then_inc(taps_transposed, 1)
            for h in range(GROUPS):
                last = pe.transpose(ws_ps[:, h, :], ws_raw[:, h, :], ident[:, :])
            last.then_inc(ws_transposed, 1)
            pe.wait_ge(keys_loaded, 16)
            for i in range(QT // DT):
                pe.wait_ge(ws_copied, i + 1)
                for t in range(DT):
                    last = pe.transpose(ws_ps[:, t, :], keys_raw[:, i * DT + t, :], ident[:, :])
                last.then_inc(ws_transposed, 1)
            pe.wait_ge(silu_ready, 1)
            for g in range(NCH):
                pe.wait_ge(w_ada_loaded[g % 2], 16 * (g // 2 + 1))
                if g >= 2:
                    pe.wait_ge(cond_added, g - 1)
                for t in range(DT):
                    last = pe.matmul(cond_ps[g % 2][0:1, :], silu_c[:, t:t + 1], w_ada_sb[g % 2][:, t, :],
                                     start=(t == 0), stop=(t == DT - 1))
                last.then_inc(cond_done, 1)
            pe.wait_ge(cond_reloaded, 16)
            pe.wait_ge(cols_ready, 1)
            pe.transpose(rows_ps[:, 64:80], staged_cond[:, :], ident[0:16, 0:16]).then_inc(cond_transposed, 1)

        @block.vector
        def _(dve):
            ch = Chain(dve, dve_chain)
            dve.wait_ge(cols_transposed, 1)
            dve.tensor_copy(cols[:, :], rows_ps[:, 0:36]).then_inc(cols_ready, 1)
            dve.wait_ge(cols_ready, 1)
            dve.tensor_scalar(silu_half[:, :], cols[:, 0:DT], 0.5, None, ALU.mult).then_inc(silu_halved, 1)
            ch.did(dve.tensor_scalar(gate_bias[:, :], cols[:, 20:24], 0.5, None, ALU.mult))
            dve.wait_ge(tanh_done, 1)
            dve.wait_ge(silu_halved, 1)
            dve.scalar_tensor_tensor(out=silu_c[:, :], in0=silu_tanh[:, :], scalar=1.0, in1=silu_half[:, :],
                                     op0=ALU.add, op1=ALU.mult).then_inc(silu_ready, 1)
            dve.wait_ge(taps_transposed, 1)
            ch.did(dve.tensor_copy(conv_taps[:, :, :], taps_ps[:, :, 0:TAPS]))
            for g in range(NCH):
                dve.wait_ge(cond_done, g + 1)
                dve.wait_ge(b_ada_loaded[g % 2], 16 * (g // 2 + 1))
                if g >= 2:
                    dve.wait_ge(cond_stored[g % 2], 16 * (g // 2))
                dve.tensor_tensor(cond_row[:, g % 2, :], cond_ps[g % 2][0:1, :], bada_row[:, g % 2, :],
                                  ALU.add).then_inc(cond_added, 1)
            dve.wait_ge(rows_loaded, 7 * 16)
            ch.did(dve.tensor_scalar(g_conv, g_conv, 0.5, None, ALU.mult))
            ch.did(dve.tensor_scalar(b_conv, b_conv, 0.5, None, ALU.mult))
            dve.wait_ge(rms_done, 1)
            ch.did(dve.reciprocal(rs1[:, :], rms[:, :]))
            dve.wait_ge(cond_transposed, 1)
            ch.did(dve.tensor_copy(sh1_col[:, :], rows_ps[:, 64:64 + DT]))
            ch.did(dve.tensor_scalar(one_plus[:, :], rows_ps[:, 64 + DT:64 + 2 * DT], 1.0, None, ALU.add))
            ch.wait()
            ch.did(dve.tensor_tensor(g1_col[:, :], one_plus[:, :], cols[:, 8:16], ALU.mult))
            dve.wait_ge(gt1_loaded, 16)
            ch.did(dve.tensor_tensor(gt1_b_out[:, :], gt1_b_out[:, :], gt1[:, :], ALU.mult))
            ch.wait()
    return k


def mixer_block(nc, k, w_in_sb, ident, eps, ss2, experts, gates, x1_dram, w_query, w_q_loaded):
    K1, K2 = 8, 130
    w_out_sb, x_all, ws = k["w_out_sb"], k["x_all"], k["ws"]
    taps, cb, bv = k["conv_taps"], k["cb_col"], k["bv_col"]
    HALF = DT // 2
    with own_semaphores(nc) as sem, ExitStack() as ctx:
        def sb(name, shape):
            return ctx.enter_context(nc.sbuf_tensor(name, shape, F32))

        def ps(name, shape):
            return ctx.enter_context(nc.psum_tensor(name, shape, F32))

        xn = sb("xn", [P, D])
        hT = sb("hT", [P, DT, P])
        gate_tanh = sb("gate_tanh", [P, CT, P])
        a = sb("a", [P, CT, CARRY + P])
        acc = sb("acc", [P, CT, P])
        z = sb("z", [P, 2, DC])
        u = sb("u", [P, DC])
        v = sb("v", [P, GROUPS, GW])
        vn = sb("vn", [P, GROUPS, GW])
        cc = sb("cc", [P, GROUPS, GW])
        total = sb("total", [P, 2, GROUPS])
        var = sb("var", [P, 2, GROUPS])
        std = sb("std", [P, 2, GROUPS])
        silu_tanh = sb("mix_silu_tanh", [P, DC])
        y_conv = sb("y_conv", [P, DC])
        y_gmlp = sb("y_gmlp", [P, GROUPS, GW])
        yT = sb("yT", [P, DT, P])
        yo = gates[:, :, :].rearrange("p b k -> p (b k)")
        squares = experts[:, 0:DC // PAIRS, :].bitcast(F32).rearrange("p b (g w) -> p (b g) w", w=GW)
        turned_ps = ps("turned_ps", [P, DT, P])
        conv_ps = ps("conv_ps", [P, GROUPS, GW])
        val_ps = ps("val_ps", [P, CT, P])
        gates_ps = ps("gates_ps", [P, CT, P])
        wide_ps = ps("wide_ps", [P, 2, BANK])
        mixed_ps = ps("mixed_ps", [P, GROUPS, GW])

        xn_ready = sem("xn_ready")
        xn_turned = sem("xn_turned")
        hT_ready = sem("hT_ready")
        x_biased = sem("x_biased")
        gates_ready = sem("gates_ready")
        gate_tanh_ready = sem("gate_tanh_ready")
        val_ready = sem("val_ready")
        a_ready = sem("a_ready")
        z_ready = sem("z_ready")
        z_biased = sem("z_biased")
        gelu_done = sem("gelu_done")
        v_var = sem("v_var")
        v_std = sem("v_std")
        vn_ready = sem("vn_ready")
        mixed = sem("mixed")
        gmlp_ready = sem("gmlp_ready")
        conv_done = sem("conv_done")
        conv_turned = sem("conv_turned")
        conv_var = sem("conv_var")
        conv_std = sem("conv_std")
        conv_normed = sem("conv_normed")
        conv_tanh = sem("conv_tanh")
        y_ready = sem("y_ready")
        y_turned = sem("y_turned")
        yT_ready = sem("yT_ready")
        out_ready = sem("out_ready")
        carry_cleared = sem("carry_cleared")
        out_taken = sem("out_taken")
        x1_ready = sem("x1_ready")
        x1_squared = sem("x1_squared")
        x1_stored = sem("x1_stored")
        chain1 = sem("chain1")
        chain2 = sem("chain2")
        block = ctx.enter_context(nc.Block())

        @block.sync
        def _(sp):
            x1_v = x1_dram.rearrange("(b p) d -> b p d", p=P)
            w_v = w_query[0].rearrange("(t p) n -> p t n", p=P)
            sp.wait_ge(z_ready, 2 * NB)
            for t in range(0, DT, 2):
                sp.dma_start(w_in_sb[:, t:t + 2, :], w_v[:, t:t + 2, :]).then_inc(w_q_loaded, 16)
            with sp.Fori(0, NB) as b:
                sp.wait_ge(x1_ready, b + 1)
                sp.dma_start(x1_v[b], x_all[:, b, :]).then_inc(x1_stored, 16)
            sp.wait_ge(x1_stored, 16 * NB)

        @block.gpsimd
        def _(pool):
            with pool.Fori(0, NB) as b:
                pool.wait_ge(xn_ready, b + 1)
                pool.tensor_tensor(x_all[:, b, :], x_all[:, b, :], k["gt1_b_out"][:, :], ALU.add).then_inc(x_biased, 1)

        @block.scalar
        def _(act):
            def norm(b):
                act.activation(xn[:, :], x_all[:, b, :], ACT.Copy, scale=k["rs1"][:, bass.ds(b, 1)]).then_inc(xn_ready, 1)

            def project_in(b):
                act.wait_ge(xn_turned, b + 1)
                for i in range(2):
                    for t in range(i * HALF, (i + 1) * HALF):
                        last = act.activation(hT[:, t, :], turned_ps[:, t, :], ACT.Identity,
                                              scale=k["g1_col"][:, t:t + 1], bias=k["sh1_col"][:, t:t + 1])
                    last.then_inc(hT_ready, 1)
                act.wait_ge(gates_ready, b + 1)
                for m in range(CT):
                    last = act.activation(gate_tanh[:, m, :], gates_ps[:, m, :], ACT.Tanh, scale=0.5,
                                          bias=k["gate_bias"][:, m:m + 1])
                last.then_inc(gate_tanh_ready, 1)
                for i, to in ((1, v[:, :, :].rearrange("p h c -> p (h c)")), (0, u[:, :])):
                    act.wait_ge(z_biased, 2 * b + 2 - i)
                    act.activation(to, z[:, i, :], ACT.Gelu_apprx_tanh).then_inc(gelu_done, 1)

            def project_in_end(b):
                act.wait_ge(v_var, b + 1)
                act.activation(std[:, 0, :], var[:, 0, :], ACT.Sqrt, scale=1.0 / GW, bias=eps[:, :]).then_inc(v_std, 1)

            def conv(b):
                act.wait_ge(conv_var, b + 1)
                act.activation(std[:, 1, :], var[:, 1, :], ACT.Sqrt, scale=1.0 / GW, bias=eps[:, :]).then_inc(conv_std, 1)
                act.wait_ge(conv_normed, b + 1)
                act.activation(silu_tanh[:, :], cc[:, :, :].rearrange("p h c -> p (h c)"), ACT.Tanh).then_inc(conv_tanh, 1)

            def turned(b):
                act.wait_ge(y_turned, b + 1)
                act.copy(yT[:, :, :], turned_ps[:, :, :]).then_inc(yT_ready, 1)

            norm(0)
            project_in(0)
            project_in_end(0)
            norm(1)
            project_in(1)
            project_in_end(1)
            conv(0)
            with act.Fori(1, NB - 1) as i:
                norm(i + 1)
                turned(i - 1)
                project_in(i + 1)
                project_in_end(i + 1)
                conv(i)
            turned(NB - 2)
            conv(NB - 1)
            turned(NB - 1)
            for b in range(NB):
                act.wait_ge(x1_ready, b + 1)
                if b:
                    act.wait_ge(x1_squared, b)
                act.activation(xn[:, :], x_all[:, b, :], ACT.Square, accum_out=ss2[:, b:b + 1]).then_inc(x1_squared, 1)

        @block.tensor
        def _(pe):
            def project_in(b, early=False):
                pe.wait_ge(xn_ready, b + 1)
                for t in range(DT):
                    last = pe.transpose(turned_ps[:, t, :], xn[:, t * P:(t + 1) * P], ident[:, :])
                last.then_inc(xn_turned, 1)
                for m, to, sig in ((CT, gates_ps, gates_ready), (0, val_ps, val_ready)):
                    for j in range(CT):
                        for t in range(DT):
                            if (m, j) == (CT, 0) and t % HALF == 0:
                                pe.wait_ge(hT_ready, 2 * b + (t // HALF + 1))
                            last = pe.matmul(to[:, j, :], w_in_sb[:, t, (m + j) * P:(m + j + 1) * P], hT[:, t, :],
                                             start=(t == 0), stop=(t == DT - 1))
                    last.then_inc(sig, 1)
                if not early:
                    pe.wait_ge(out_taken, b - 1)
                for i in (1, 0):
                    for t in range(DT):
                        last = pe.matmul(wide_ps[:, i, :], hT[:, t, :], w_in_sb[:, t, D + i * DC:D + (i + 1) * DC],
                                         start=(t == 0), stop=(t == DT - 1))
                    last.then_inc(z_ready, 1)

            def turn_y(b):
                pe.wait_ge(gmlp_ready, b + 1)
                pe.wait_ge(y_ready, b + 1)
                gm = y_gmlp[:, :, :].rearrange("p h c -> p (h c)")
                for t in range(DT):
                    src = (y_conv[:, :] if t < CT else gm)[:, (t % CT) * P:(t % CT + 1) * P]
                    last = pe.transpose(turned_ps[:, t, :], src, ident[:, :])
                last.then_inc(y_turned, 1)

            def mix(b):
                pe.wait_ge(vn_ready, b + 1)
                for h in range(GROUPS):
                    last = pe.matmul(mixed_ps[:, h, :], ws[:, h, :], vn[:, h, :], start=True, stop=True)
                last.then_inc(mixed, 1)

            def turn_conv(b):
                pe.wait_ge(conv_done, b + 1)
                for m in range(CT):
                    last = pe.transpose(conv_ps[:, 2 * m:2 * m + 2, :].rearrange("p g c -> p (g c)"), acc[:, m, :], ident[:, :])
                last.then_inc(conv_turned, 1)

            def project_out(b, tail=False):
                pe.wait_ge(yT_ready, b + 1)
                if tail:
                    pe.wait_ge(z_biased, 2 * NB)
                    pe.wait_ge(out_taken, b + 1)
                for i in range(2):
                    if not tail:
                        pe.wait_ge(z_biased, 2 * b + 6 - i)
                    for t in range(DT):
                        last = pe.matmul(wide_ps[:, i, :], yT[:, t, :], w_out_sb[:, t, i * BANK:(i + 1) * BANK],
                                         start=(t == 0), stop=(t == DT - 1))
                last.then_inc(out_ready, 1)

            project_in(0, early=True)
            mix(0)
            project_in(1, early=True)
            turn_conv(0)
            with pe.Fori(1, NB - 1) as i:
                turn_y(i - 1)
                mix(i)
                pe.wait_ge(yT_ready, i)
                project_in(i + 1)
                turn_conv(i)
                project_out(i - 1)
            turn_y(NB - 2)
            mix(NB - 1)
            turn_conv(NB - 1)
            project_out(NB - 2, tail=True)
            turn_y(NB - 1)
            project_out(NB - 1, tail=True)

        @block.vector
        def _(dve):
            ch1, ch2 = Chain(dve, chain1, K1), Chain(dve, chain2, K2)

            def over_groups(t):
                return t.unsqueeze(2).to_broadcast([P, GROUPS, GW])

            def moments(ch, src, centred, i, var_ready):
                ch.did(dve.tensor_reduce(total[:, i, :], src, AX.X, ALU.add))
                ch.wait()
                ch.did(dve.scalar_tensor_tensor(out=centred, in0=over_groups(total[:, i, :]), scalar=-1.0 / GW, in1=src,
                                                op0=ALU.mult, op1=ALU.add))
                ch.wait()
                ch.did(dve.tensor_tensor(squares, centred, centred, ALU.mult))
                ch.wait()
                dve.tensor_reduce(var[:, i, :], squares, AX.X, ALU.add).then_inc(var_ready, 1)

            def scaled(ch, t, i, std_ready, b, g, shift, ready):
                dve.wait_ge(std_ready, b + 1)
                ch.did(dve.reciprocal(std[:, i, :], std[:, i, :]))
                ch.wait()
                ch.did(dve.tensor_tensor(t, t, over_groups(std[:, i, :]), ALU.mult))
                ch.wait()
                ch.did(dve.tensor_tensor(t, t, g.rearrange("p (h c) -> p h c", h=GROUPS), ALU.mult))
                ch.wait()
                dve.tensor_tensor(t, t, shift.rearrange("p (h c) -> p h c", h=GROUPS), ALU.add).then_inc(ready, 1)

            def take_a(b):
                ch1.round(b)
                ch1.did(dve.tensor_copy(a[:, :, 0:CARRY], a[:, :, P:P + CARRY]))
                dve.wait_ge(gate_tanh_ready, b + 1)
                ch1.did(dve.tensor_scalar(gate_tanh[:, :, :], gate_tanh[:, :, :], 1.0, 0.5, ALU.add, ALU.mult))
                ch1.wait()
                dve.wait_ge(val_ready, b + 1)
                for m in range(CT):
                    last = dve.scalar_tensor_tensor(out=a[:, m, CARRY:], in0=val_ps[:, m, :], scalar=bv[:, m:m + 1],
                                                    in1=gate_tanh[:, m, :], op0=ALU.add, op1=ALU.mult)
                last.then_inc(a_ready, 1)

            def take_z(b):
                for i in (1, 0):
                    dve.wait_ge(z_ready, 2 * b + 2 - i)
                    dve.tensor_tensor(z[:, i, :], wide_ps[:, i, :], k["bz"][:, i, :], ALU.add).then_inc(z_biased, 1)
                dve.wait_ge(gelu_done, 2 * b + 1)
                moments(ch1, v[:, :, :], vn[:, :, :], 0, v_var)

            def norm_v(b):
                scaled(ch1, vn[:, :, :], 0, v_std, b, k["g_v"], k["b_v"], vn_ready)
                ch1.end()

            def conv(b):
                ch2.round(b)
                dve.wait_ge(a_ready, b + 1)
                for w in range(TAPS):
                    for m in range(CT):
                        src, tap = a[:, m, w:w + P], taps[:, m, w:w + 1]
                        if w == 0:
                            ch2.did(dve.tensor_scalar(acc[:, m, :], src, tap, cb[:, m:m + 1], ALU.mult, ALU.add))
                        else:
                            ch2.wait(behind=CT - 1)
                            ins = dve.scalar_tensor_tensor(out=acc[:, m, :], in0=src, scalar=tap, in1=acc[:, m, :],
                                                           op0=ALU.mult, op1=ALU.add)
                            if (w, m) == (TAPS - 1, CT - 1):
                                ins.then_inc(conv_done, 1)
                            else:
                                ch2.did(ins)

            def gate_mixed(b):
                dve.wait_ge(mixed, b + 1)
                dve.wait_ge(gelu_done, 2 * b + 2)
                ch2.did(dve.tensor_tensor(y_gmlp[:, :, :], mixed_ps[:, :, :], over_groups(k["bs_col"]), ALU.add))
                ch2.wait()
                gm = y_gmlp[:, :, :].rearrange("p h c -> p (h c)")
                dve.tensor_tensor(gm, gm, u[:, :], ALU.mult).then_inc(gmlp_ready, 1)

            def conv_moments(b):
                dve.wait_ge(conv_turned, b + 1)
                moments(ch2, conv_ps[:, :, :], cc[:, :, :], 1, conv_var)

            def conv_norm(b):
                scaled(ch2, cc[:, :, :], 1, conv_std, b, k["g_conv"], k["b_conv"], conv_normed)

            def conv_silu(b):
                dve.wait_ge(conv_normed, b + 1)
                dve.wait_ge(conv_tanh, b + 1)
                dve.scalar_tensor_tensor(out=y_conv[:, :], in0=silu_tanh[:, :], scalar=1.0,
                                         in1=cc[:, :, :].rearrange("p h c -> p (h c)"),
                                         op0=ALU.add, op1=ALU.mult).then_inc(y_ready, 1)
                ch2.end()

            def residual(b):
                dve.wait_ge(out_ready, b + 1)
                dve.tensor_tensor(yo, wide_ps[:, :, :].rearrange("p a n -> p (a n)"), k["gt1"][:, :],
                                  ALU.mult).then_inc(out_taken, 1)
                dve.wait_ge(out_taken, b + 2)
                dve.wait_ge(x_biased, b + 1)
                dve.tensor_tensor(x_all[:, b, :], x_all[:, b, :], yo, ALU.add).then_inc(x1_ready, 1)

            dve.memset(a[:, :, P:P + CARRY], 0.0).then_inc(carry_cleared, 1)
            dve.wait_ge(carry_cleared, 1)
            dve.sem_inc(out_taken, 1)
            take_a(0)
            take_z(0)
            norm_v(0)
            conv(0)
            gate_mixed(0)
            take_a(1)
            take_z(1)
            conv_moments(0)
            norm_v(1)
            conv_norm(0)
            conv_silu(0)
            with dve.Fori(1, NB - 1) as i:
                conv(i)
                gate_mixed(i)
                take_a(i + 1)
                take_z(i + 1)
                conv_moments(i)
                norm_v(i + 1)
                conv_norm(i)
                residual(i - 1)
                conv_silu(i)
            conv(NB - 1)
            gate_mixed(NB - 1)
            conv_moments(NB - 1)
            conv_norm(NB - 1)
            conv_silu(NB - 1)
            residual(NB - 2)
            dve.wait_ge(x1_ready, NB - 1)
            residual(NB - 1)


class Gather:

    def __init__(self, ctx, nc, tag, ring, experts, gates, expert_u, expert_v, with_diag=True):
        def sb(name, shape, dt=F32):
            return ctx.enter_context(nc.sbuf_tensor(f"{name}_{tag}", shape, dt))

        def sem(name):
            return ctx.enter_context(nc.semaphore(f"{name}_{tag}"))

        self.ring, self.experts, self.gates, self.u, self.v = ring, experts, gates, expert_u, expert_v
        self.slots = sb("slots", [P, TOPK, D])
        self.wanted = sb("wanted", [P, ring, TOPK], U32)
        self.dots = sb("dots", [P, ring, TOPK])
        self.dots_gelu = sb("dots_gelu", [P, ring, TOPK])
        self.coef = sb("coef", [P, ring, TOPK])
        if with_diag:
            self.diag = sb("diag", [P, 4, P])
            self.diag_ready = sem("diag_ready")
        self.staged = sem("staged")
        self.claims = sem("claims")
        self.u_used = sem("u_used")
        self.slot_free = sem("slot_free")
        self.landed = [sem(f"landed{j}") for j in range(TOPK)]
        self.gelu_done = sem("dots_gelu_done")
        self.coef_ready = sem("coef_ready")

    def issue(self, pool, n, p, b, first_pair):
        if self.ring == 1:
            pool.wait_ge(self.slot_free, (n + 1) * TOPK)
        pool.tensor_copy(self.wanted[:, p, :], self.experts[:, b, bass.ds(first_pair, TOPK)]).then_inc(self.staged, 1)
        pool.wait_ge(self.staged, n + 1)
        for table, free in ((self.u, self.slot_free), (self.v, self.u_used)):
            for j in range(TOPK):
                pool.wait_ge(free, n * TOPK + (j + 1))
                pool.sem_inc(self.claims, 1)
                pool.indirect_dma_start(self.slots[:, j, :], None, table,
                                        bass.IndirectOffsetOnAxis(ap=self.wanted[:, p, j:j + 1], axis=0)
                                        ).then_inc(self.landed[j], 16)

    def dot(self, dve, n, p, j, h):
        dve.wait_ge(self.landed[j], 32 * n + 16)
        slot = self.slots[:, j, :]
        dve.tensor_tensor_reduce(out=slot, in0=slot, in1=h, scale=1.0, scalar=0.0, op0=ALU.mult, op1=ALU.add,
                                 accum_out=self.dots[:, p, j:j + 1]).then_inc(self.u_used, 1)

    def gelu(self, act, n, p):
        act.wait_ge(self.u_used, (n + 1) * TOPK)
        act.activation(self.dots_gelu[:, p, :], self.dots[:, p, :], ACT.Gelu_apprx_tanh).then_inc(self.gelu_done, 1)

    def weigh(self, dve, n, p, b, first_pair):
        dve.wait_ge(self.gelu_done, n + 1)
        dve.tensor_tensor(self.coef[:, p, :], self.dots_gelu[:, p, :], self.gates[:, b, bass.ds(first_pair, TOPK)],
                          ALU.mult).then_inc(self.coef_ready, 1)

    def diagonal(self, act, n, p, j, ident):
        if j == 0:
            act.wait_ge(self.coef_ready, n + 1)
        act.wait_ge(self.slot_free, n * TOPK + (j + 1 + TOPK - 4))
        act.activation(self.diag[:, j % 4, :], ident[:, :], ACT.Copy, scale=self.coef[:, p, j:j + 1]
                       ).then_inc(self.diag_ready, 1)

    def diagonals(self, act, n, p, ident):
        for j in range(TOPK):
            self.diagonal(act, n, p, j, ident)

    def combine_slot(self, pe, n, j, y_ps, first, last):
        pe.wait_ge(self.diag_ready, n * TOPK + (j + 1))
        pe.wait_ge(self.landed[j], 32 * n + 32)
        for i in range(2):
            ins = pe.matmul(y_ps[:, i, :], self.diag[:, j % 4, :], self.slots[:, j, i * BANK:(i + 1) * BANK],
                            start=(first and j == 0), stop=(last and j == TOPK - 1))
        ins.then_inc(self.slot_free, 1)

    def combine(self, pe, n, y_ps, first, last):
        for j in range(TOPK):
            self.combine_slot(pe, n, j, y_ps, first, last)

    def accumulate(self, dve, n, p, j, y):
        if j == 0:
            dve.wait_ge(self.coef_ready, n + 1)
        dve.wait_ge(self.landed[j], 32 * n + 32)
        dve.wait_ge(self.slot_free, n * TOPK + (TOPK + j))
        dve.scalar_tensor_tensor(out=y, in0=self.slots[:, j, :], scalar=self.coef[:, p, j:j + 1], in1=y,
                                 op0=ALU.mult, op1=ALU.add).then_inc(self.slot_free, 1)


def routing_block(nc, w_q, w_q_loaded, keysT, experts, gates, ident, eps, ss2, x1_dram, cond_dram,
                  h_dram, hT_dram, y_dram, g_norm2, expert_u, expert_v):
    QG = 4
    HG = QG // 2
    NG = QT // QG
    KQ = 173
    with own_semaphores(nc) as sem, ExitStack() as ctx:
        def sb(name, shape, dt=F32):
            return ctx.enter_context(nc.sbuf_tensor(name, shape, dt))

        def ps(name, shape):
            return ctx.enter_context(nc.psum_tensor(name, shape, F32))

        ga = Gather(ctx, nc, "r", 1, experts, gates, expert_u[0], expert_v[0])
        g2 = sb("g2", [P, D])
        sh2 = sb("sh2", [P, D])
        x1 = sb("x1", [P, D])
        h = sb("h", [P, D])
        h_first = sb("h_first", [P, D])
        hT = sb("h2T", [P, DT, P])
        qT = sb("qT", [P, QG, P])
        scores = sb("scores", [P, NG, QG, NK])
        beaten = sb("beaten", [P, QG, NK])
        top = sb("top", [P, QG, TOPK])
        top_at = sb("top_at", [P, QG, TOPK], U32)
        top_at_f = sb("top_at_f", [P, QG, TOPK])
        cand = sb("cand", [P, HG, TOPK, TOPK])
        cand2 = sb("cand2", [P, HG, TOPK * TOPK])
        best_at = sb("best_at", [P, HG, TOPK], U32)
        pos = sb("pos", [P, 2, HG, TOPK], U32)
        pos_f = sb("pos_f", [P, 2, HG * TOPK])
        onehot = sb("onehot", [P, 2 * HG * TOPK, TOPK])
        half_at = sb("half_at", [P, 2, HG * TOPK])
        best = sb("best", [P, HEADS, TOPK])
        expert_f = sb("expert_f", [P, PAIRS])
        sixteen = sb("sixteen", [P, TOPK])
        sixteen_i = sb("sixteen_i", [P, TOPK], I32)
        gate_sum = sb("gate_sum", [P, HEADS])
        rs2 = sb("rs2", [P, NB])
        y_sb = sb("y_sb", [P, D])
        y_ps = ps("y_ps", [P, 2, BANK])
        turned_ps = ps("turned2_ps", [P, DT, P])
        q_ps = ps("q_ps", [P, QG, P])
        s_ps = ps("s_ps", [P, QG, NK])

        rows2_loaded = sem("rows2_loaded")
        g2_ready = sem("g2_ready")
        rms2_ready = sem("rms2_ready")
        rs2_ready = sem("rs2_ready")
        iota_done = sem("iota_done")
        sixteen_ready = sem("sixteen_ready")
        x1_loaded = sem("x1_loaded")
        xn_ready = sem("xn2_ready")
        h_ready = sem("h_ready")
        h_turned = sem("h_turned")
        hT_ready = sem("h2T_ready")
        h_first_ready = sem("h_first_ready")
        h_stored = sem("h_stored")
        hT_stored = sem("hT_stored")
        q_ready = sem("q_ready")
        qT_ready = sem("qT_ready")
        s_ready = sem("s_ready")
        scores_ready = sem("scores_ready")
        scores_seen = sem("scores_seen")
        scores_free = sem("scores_free")
        less_max = sem("less_max")
        exp_done = sem("exp_done")
        chosen = sem("chosen")
        y_copied = sem("y_copied")
        y_stored = sem("y_stored")
        chainq = sem("chainq")
        setup_chain = sem("routing_setup_chain")
        block = ctx.enter_context(nc.Block())
        x1_v = x1_dram.rearrange("(b p) d -> b p d", p=P)

        def slots_beside(g):
            return ((), range(0, 6), range(6, 11), range(11, TOPK))[g]

        @block.sync
        def _(sp):
            sp.dma_start(x1[:, :], x1_v[0]).then_inc(x1_loaded, 16)
            for to, row in ((sh2, cond_dram[3 * D:4 * D]), (y_sb, cond_dram[4 * D:5 * D]), (g2, g_norm2[0])):
                sp.dma_start(to[:, :], broadcast(row)).then_inc(rows2_loaded, 16)

            def store(b):
                sp.wait_ge(h_ready, b + 1)
                sp.dma_start(h_dram[b], h[:, :]).then_inc(h_stored, 16)
                sp.wait_ge(hT_ready, b + 1)
                sp.dma_start(hT_dram[b], hT[:, :, :].rearrange("p t n -> p (t n)")).then_inc(hT_stored, 16)

            with sp.Fori(0, NB - 1) as b:
                sp.wait_ge(xn_ready, b + 1)
                sp.dma_start(x1[:, :], x1_v[b + 1]).then_inc(x1_loaded, 16)
                store(b)
            store(NB - 1)
            sp.wait_ge(y_copied, 1)
            sp.dma_start(y_dram[0], y_sb[:, :]).then_inc(y_stored, 16)
            sp.wait_ge(y_stored, 16)
            sp.wait_ge(h_stored, 16 * NB)
            sp.wait_ge(hT_stored, 16 * NB)

        @block.gpsimd
        def _(pool):
            pool.iota(sixteen_i[:, :], pattern=[[1, TOPK]], base=0, channel_multiplier=0).then_inc(iota_done, 1)
            pool.wait_ge(chosen, 1)
            with pool.Fori(0, HEADS) as n:
                ga.issue(pool, n, 0, 0, n * TOPK)

        @block.scalar
        def _(act):
            def norm(b, first=False):
                act.wait_ge(x1_loaded, 16 * b + 16)
                if not first:
                    act.wait_ge(h_stored, 16 * b)
                act.activation(h[:, :], x1[:, :], ACT.Copy, scale=rs2[:, bass.ds(b, 1)]).then_inc(xn_ready, 1)

            def turned(b, first=False):
                act.wait_ge(h_turned, b + 1)
                if not first:
                    act.wait_ge(hT_stored, 16 * b)
                act.copy(hT[:, :, :], turned_ps[:, :, :]).then_inc(hT_ready, 1)

            def query(b, g, first=False):
                act.wait_ge(q_ready, NG * b + (g + 1))
                act.copy(qT[:, :, :], q_ps[:, :, :]).then_inc(qT_ready, 1)
                act.wait_ge(s_ready, NG * b + (g + 1))
                if not first:
                    act.wait_ge(scores_free, NG * b - (NG - 1 - g))
                act.copy(scores[:, g, :, :], s_ps[:, :, :]).then_inc(scores_ready, 1)

            def softmax(b):
                act.wait_ge(less_max, b + 1)
                act.activation(best[:, :, :], best[:, :, :], ACT.Exp).then_inc(exp_done, 1)

            act.activation(rs2[:, :], ss2[:, :], ACT.Sqrt, scale=1.0 / D, bias=eps[:, :]).then_inc(rms2_ready, 1)
            act.wait_ge(rs2_ready, 1)
            norm(0, first=True)
            turned(0, first=True)
            for g in range(NG):
                query(0, g, first=True)
            softmax(0)
            with act.Fori(1, NB) as b:
                norm(b)
                turned(b)
                query(b, 0)
                ga.gelu(act, b - 1, 0)
                for g in range(NG):
                    if g:
                        query(b, g)
                    for j in slots_beside(g):
                        ga.diagonal(act, b - 1, 0, j, ident)
                softmax(b)
            ga.gelu(act, HEADS - 1, 0)
            ga.diagonals(act, HEADS - 1, 0, ident)

        @block.tensor
        def _(pe):
            def route(b, n=None, first=False):
                pe.wait_ge(h_ready, b + 1)
                for t in range(DT):
                    last = pe.transpose(turned_ps[:, t, :], h[:, t * P:(t + 1) * P], ident[:, :])
                last.then_inc(h_turned, 1)
                pe.wait_ge(hT_ready, b + 1)
                for g in range(NG):
                    for j in range(QG):
                        q = g * QG + j
                        for t in range(DT):
                            last = pe.matmul(q_ps[:, j, :], w_q[:, t, q * P:(q + 1) * P], hT[:, t, :],
                                             start=(t == 0), stop=(t == DT - 1))
                    last.then_inc(q_ready, 1)
                    pe.wait_ge(qT_ready, NG * b + (g + 1))
                    for j in range(QG):
                        last = pe.matmul(s_ps[:, j, :], qT[:, j, :], keysT[:, g * QG + j, :], start=True, stop=True)
                    last.then_inc(s_ready, 1)
                    if n is not None:
                        for j in slots_beside(g):
                            ga.combine_slot(pe, n, j, y_ps, first, False)

            pe.sem_inc(ga.slot_free, TOPK)
            pe.wait_ge(w_q_loaded, 16 * DT // 2)
            route(0)
            route(1, 0, first=True)
            with pe.Fori(2, NB) as b:
                route(b, b - 1)
            ga.combine(pe, HEADS - 1, y_ps, False, True)

        @block.vector
        def _(dve):
            cq, cs = ClearedChain(dve, chainq, KQ), Chain(dve, setup_chain)

            def modulate(b):
                dve.wait_ge(xn_ready, b + 1)
                cq.did(dve.tensor_tensor(h[:, :], h[:, :], g2[:, :], ALU.mult))
                cq.wait()
                dve.tensor_tensor(h[:, :], h[:, :], sh2[:, :], ALU.add).then_inc(h_ready, 1)

            def top16(searches):
                for values, without, to, at in searches:
                    cq.did(dve.max(to[:, 0:8], values))
                cq.wait()
                for values, without, to, at in searches:
                    cq.did(dve.match_replace(without, to[:, 0:8], values, BELOW_ALL))
                for values, without, to, at in searches:
                    cq.did(dve.max_index(at[:, 0:8], to[:, 0:8], values))
                cq.wait()
                for values, without, to, at in searches:
                    cq.did(dve.max(to[:, 8:16], without))
                cq.wait()
                for values, without, to, at in searches:
                    cq.did(dve.max_index(at[:, 8:16], to[:, 8:16], without))

            def choose(b, g):
                dve.wait_ge(scores_ready, NG * b + (g + 1))
                dve.sem_inc(scores_seen, 1)
                top16([(scores[:, g, j, :], beaten[:, j, :], top[:, j, :], top_at[:, j, :]) for j in range(QG)])
                cq.wait()
                dve.tensor_copy(top_at_f[:, :, :], top_at[:, :, :]).then_inc(scores_free, 1)
                for i in range(HG):
                    first = top[:, 2 * i, :].unsqueeze(2).to_broadcast([P, TOPK, TOPK])
                    second = top[:, 2 * i + 1, :].unsqueeze(1).to_broadcast([P, TOPK, TOPK])
                    cq.did(dve.tensor_tensor(cand[:, i, :, :], first, second, ALU.add))
                cq.wait()
                top16([(cand[:, i, :, :].rearrange("p a b -> p (a b)"), cand2[:, i, :],
                        best[:, g * HG + i, :], best_at[:, i, :]) for i in range(HG)])
                cq.wait()
                cq.did(dve.tensor_scalar(pos[:, 0, :, :], best_at[:, :, :], 4, None, ALU.logical_shift_right))
                cq.did(dve.tensor_scalar(pos[:, 1, :, :], best_at[:, :, :], TOPK - 1, None, ALU.bitwise_and))
                cq.wait()
                cq.did(dve.tensor_copy(pos_f[:, :, :], pos[:, :, :, :].rearrange("p a h k -> p a (h k)")))
                dve.wait_ge(scores_free, NG * b + (g + 1))
                cq.wait()
                cq.did(dve.tensor_tensor(onehot[:, :, :], pos_f[:, :, :].rearrange("p a k -> p (a k)").unsqueeze(2)
                                         .to_broadcast([P, 2 * HG * TOPK, TOPK]),
                                         sixteen[:, :].unsqueeze(1).to_broadcast([P, 2 * HG * TOPK, TOPK]), ALU.is_equal))
                cq.wait()
                for i in range(2):
                    for hh in range(HG):
                        part = onehot[:, (i * HG + hh) * TOPK:(i * HG + hh + 1) * TOPK, :]
                        at = top_at_f[:, 2 * hh + i, :].unsqueeze(1).to_broadcast([P, TOPK, TOPK])
                        cq.did(dve.tensor_tensor(part, part, at, ALU.mult))
                cq.wait()
                cq.did(dve.tensor_reduce(half_at[:, :, :].rearrange("p a k -> p (a k)"), onehot[:, :, :], AX.X, ALU.add))
                cq.wait()
                cq.did(dve.scalar_tensor_tensor(out=expert_f[:, g * HG * TOPK:(g + 1) * HG * TOPK], in0=half_at[:, 0, :],
                                                scalar=float(NK), in1=half_at[:, 1, :], op0=ALU.mult, op1=ALU.add))

            def gate(b):
                over_heads = gate_sum[:, :].unsqueeze(2).to_broadcast([P, HEADS, TOPK])
                cq.wait()
                cq.did(dve.tensor_copy(gate_sum[:, :].unsqueeze(2), best[:, :, 0:1]))
                cq.wait()
                dve.tensor_tensor(best[:, :, :], best[:, :, :], over_heads, ALU.subtract).then_inc(less_max, 1)
                dve.wait_ge(exp_done, b + 1)
                cq.did(dve.tensor_reduce(gate_sum[:, :], best[:, :, :], AX.X, ALU.add))
                cq.wait()
                cq.did(dve.reciprocal(gate_sum[:, :], gate_sum[:, :]))
                cq.wait()
                cq.did(dve.tensor_tensor(gates[:, b, :].rearrange("p (h k) -> p h k", h=HEADS), best[:, :, :],
                                         over_heads, ALU.mult))
                cq.wait()
                dve.tensor_copy(experts[:, b, :], expert_f[:, :]).then_inc(chosen, 1)
                dve.wait_ge(chosen, b + 1)
                cq.end()

            def dots(n):
                for j in range(TOPK):
                    ga.dot(dve, n, 0, j, h_first[:, :])
                ga.weigh(dve, n, 0, 0, n * TOPK)

            dve.wait_ge(rms2_ready, 1)
            dve.reciprocal(rs2[:, :], rs2[:, :]).then_inc(rs2_ready, 1)
            dve.wait_ge(iota_done, 1)
            dve.tensor_copy(sixteen[:, :], sixteen_i[:, :]).then_inc(sixteen_ready, 1)
            dve.wait_ge(sixteen_ready, 1)
            dve.wait_ge(rows2_loaded, 3 * 16)
            cs.did(dve.tensor_scalar(y_sb[:, :], y_sb[:, :], 1.0, None, ALU.add))
            cs.wait()
            dve.tensor_tensor(g2[:, :], g2[:, :], y_sb[:, :], ALU.mult).then_inc(g2_ready, 1)
            dve.wait_ge(g2_ready, 1)
            cq.round(True)
            modulate(0)
            dve.wait_ge(h_ready, 1)
            dve.tensor_copy(h_first[:, :], h[:, :]).then_inc(h_first_ready, 1)
            for g in range(NG):
                choose(0, g)
            gate(0)
            dve.wait_ge(h_first_ready, 1)
            with dve.Fori(1, NB) as b:
                cq.round(False)
                modulate(b)
                dots(b - 1)
                for g in range(NG):
                    choose(b, g)
                gate(b)
            dots(HEADS - 1)
            dve.wait_ge(ga.slot_free, (HEADS + 1) * TOPK)
            dve.tensor_copy(y_sb[:, :], y_ps[:, :, :].rearrange("p a n -> p (a n)")).then_inc(y_copied, 1)


def table_block(nc, experts, gates, ident, h_dram, y_dram, table_dram, expert_u, expert_v):
    with ExitStack() as ctx:
        def sb(name, shape, dt=F32):
            return ctx.enter_context(nc.sbuf_tensor(name, shape, dt))

        def ps(name, shape):
            return ctx.enter_context(nc.psum_tensor(name, shape, F32))

        def sem(name):
            return ctx.enter_context(nc.semaphore(name))

        QUAD = 4
        NQ = CHUNK // QUAD
        UNITS = HEADS // NCHUNK
        NQU = NQ // UNITS
        QUAD_LAG, TAKE_LAG = 4, 8
        OH = 4
        ga = Gather(ctx, nc, "t", 2, experts, gates, expert_u[0], expert_v[0])
        h = sb("h_t", [P, D])
        halves_u = sb("halves_u", [P, 2, NDENSE, PAIRS], U32)
        halves = sb("halves", [P, 2, NDENSE, PAIRS])
        by_pair = sb("by_pair", [P, 3, NDENSE * P])
        now = sb("now", [P, 3, CHUNK])
        keys_i = sb("keys_i", [P, NK], I32)
        keys = sb("keys", [P, NK])
        hot1 = sb("hot1", [P, OH, NK])
        hot2 = sb("hot2", [P, OH, NK])
        part = sb("part", [P, 2, NK, CHUNK])
        y_sb = sb("y_sb_t", [P, D])
        y_ps = ps("y_ps_t", [P, 2, BANK])
        pair_ps = ps("pair_ps", [P, 3, P])
        table_ps = [ps(f"table_ps{i}", [P, QUAD, NK]) for i in range(2)]

        h_loaded = sem("h_loaded_t")
        keys_iota = sem("keys_iota")
        keys_ready = sem("keys_ready_t")
        halves_ready = sem("halves_ready")
        pairs_turned = sem("pairs_turned")
        by_pair_ready = sem("by_pair_ready")
        now_ready = sem("now_ready")
        hot_ready = sem("hot_ready")
        hot_used = sem("hot_used")
        quad_taken = sem("quad_taken")
        part_stored = [sem(f"part_stored{i}") for i in range(2)]
        y_copied = sem("y_copied_t")
        y_stored = sem("y_stored_t")
        chain = sem("table_chain")
        chunk_chain = sem("chunk_chain")
        block = ctx.enter_context(nc.Block())

        @block.sync
        def _(sp):
            sp.dma_start(h[:, :], h_dram[1]).then_inc(h_loaded, 16)
            with sp.Fori(0, NCHUNK // 2) as pair:
                c0 = pair * 2
                for c in range(2):
                    sp.wait_ge(quad_taken, (c0 + (c + 1)) * NQ + 2)
                    sp.dma_start(table_dram[c0 + c], part[:, c, :, :]).then_inc(part_stored[c], 16)
            sp.wait_ge(y_copied, 1)
            sp.dma_start(y_dram[1], y_sb[:, :]).then_inc(y_stored, 16)
            sp.wait_ge(y_stored, 16)
            for c in range(2):
                sp.wait_ge(part_stored[c], 16 * (NCHUNK // 2) + 16)

        @block.gpsimd
        def _(pool):
            pool.iota(keys_i[:, :], pattern=[[1, NK]], base=0, channel_multiplier=0).then_inc(keys_iota, 1)
            with pool.Fori(0, HEADS // 2) as pair:
                for p in range(2):
                    n = pair * 2 + p
                    ga.issue(pool, n, p, 1, n * TOPK)


        @block.scalar
        def _(act):
            act.sem_inc(quad_taken, 2)
            for d in range(NDENSE):
                act.wait_ge(pairs_turned, d + 1)
                act.copy(by_pair[:, :, d * P:(d + 1) * P], pair_ps[:, :, :]).then_inc(by_pair_ready, 1)
            act.sem_inc(part_stored[0], 16)
            act.sem_inc(part_stored[1], 16)

            def take_quad(c0, c, k):
                act.wait_ge(hot_used, (c0 + c) * CHUNK + ((k + 1) * QUAD + OH))
                if k == 0:
                    act.wait_ge(part_stored[c], 8 * c0 + 16)
                to = part[:, c, :, k * QUAD:(k + 1) * QUAD].rearrange("p a t -> p t a")
                act.copy(to, table_ps[k % 2][:, :, :]).then_inc(quad_taken, 1)

            with act.Fori(0, NCHUNK // 2) as pair:
                c0 = pair * 2
                for c in range(2):
                    for i in range(UNITS):
                        n = c0 * UNITS + (c * UNITS + i)
                        ga.gelu(act, n, i % 2)
                        for j in range(TOPK):
                            ga.diagonal(act, n, i % 2, j, ident)
                            if j >= TAKE_LAG:
                                take_quad(c0, c, i * NQU + j - TAKE_LAG)
                        for k in range(TOPK - TAKE_LAG, NQU):
                            take_quad(c0, c, i * NQU + k)

        @block.tensor
        def _(pe):
            pe.sem_inc(ga.slot_free, TOPK)
            pe.sem_inc(hot_used, OH)
            for d in range(NDENSE):
                pe.wait_ge(halves_ready, d + 1)
                if d > 0:
                    pe.wait_ge(by_pair_ready, d)
                for i in range(2):
                    pe.transpose(pair_ps[:, i, :], halves[:, i, d, :], ident[:, :])
                pe.transpose(pair_ps[:, 2, :], gates[:, NB - NDENSE + d, :], ident[:, :]).then_inc(pairs_turned, 1)

            def quad(c0, c, k):
                for q in range(QUAD):
                    t = (c0 + c) * CHUNK + (k * QUAD + q + 1)
                    pe.wait_ge(hot_ready, t)
                    if q == 0:
                        pe.wait_ge(quad_taken, (c0 + c) * NQ + (k + 1))
                    ins = pe.matmul(table_ps[k % 2][:, q, :], hot2[:, q, :], hot1[:, q, :], start=True, stop=True)
                    ins.then_inc(hot_used, 1)

            def chunks(c0, first, last):
                for c in range(2):
                    for i in range(UNITS):
                        u = c * UNITS + i
                        for j in range(TOPK):
                            ga.combine_slot(pe, c0 * UNITS + u, j, y_ps, first and u == 0, last and u == 2 * UNITS - 1)
                            if j >= QUAD_LAG:
                                quad(c0, c, i * NQU + j - QUAD_LAG)

            chunks(0, True, False)
            chunks(NCHUNK - 2, False, True)

        @block.vector
        def _(dve):
            ch, cc = Chain(dve, chain), Chain(dve, chunk_chain)
            dve.wait_ge(keys_iota, 1)
            dve.tensor_copy(keys[:, :], keys_i[:, :]).then_inc(keys_ready, 1)
            for d in range(NDENSE):
                e = experts[:, NB - NDENSE + d, :]
                ch.did(dve.tensor_scalar(halves_u[:, 0, d, :], e, 7, None, ALU.logical_shift_right))
                ch.did(dve.tensor_scalar(halves_u[:, 1, d, :], e, NK - 1, None, ALU.bitwise_and))
                ch.wait()
                dve.tensor_copy(halves[:, :, d, :], halves_u[:, :, d, :]).then_inc(halves_ready, 1)
            dve.wait_ge(h_loaded, 16)
            dve.wait_ge(keys_ready, 1)
            dve.wait_ge(by_pair_ready, NDENSE)
            with dve.Fori(0, NCHUNK // 2) as pair:
                c0 = pair * 2
                for c in range(2):
                    t0 = (c0 + c) * CHUNK
                    for i in range(UNITS):
                        n = c0 * UNITS + (c * UNITS + i)
                        for j in range(TOPK):
                            ga.dot(dve, n, i % 2, j, h[:, :])
                        ga.weigh(dve, n, i % 2, 1, n * TOPK)
                        if i == 0:
                            dve.wait_ge(hot_used, t0 + OH)
                            dve.tensor_copy(now[:, :, :], by_pair[:, :, bass.ds(t0, CHUNK)]).then_inc(now_ready, 1)
                            dve.wait_ge(now_ready, c0 + (c + 1))
                        for t in range(i * NQU * QUAD, (i + 1) * NQU * QUAD):
                            o = t % OH
                            dve.wait_ge(hot_used, t0 + (t + 1))
                            dve.tensor_scalar(hot1[:, o, :], keys[:, :], now[:, 0, t:t + 1], now[:, 2, t:t + 1],
                                              ALU.is_equal, ALU.mult)
                            dve.tensor_scalar(hot2[:, o, :], keys[:, :], now[:, 1, t:t + 1], None,
                                              ALU.is_equal).then_inc(hot_ready, 1)
            dve.wait_ge(ga.slot_free, (HEADS + 1) * TOPK)
            dve.tensor_copy(y_sb[:, :], y_ps[:, :, :].rearrange("p a n -> p (a n)")).then_inc(y_copied, 1)


def dense_block(nc, experts, gates, ident, y_all, h_dram, hT_dram, y_dram, table_dram, expert_u, expert_v):
    with ExitStack() as ctx:
        def sb(name, shape, dt=F32):
            return ctx.enter_context(nc.sbuf_tensor(name, shape, dt))

        def ps(name, shape):
            return ctx.enter_context(nc.psum_tensor(name, shape, F32))

        def sem(name):
            return ctx.enter_context(nc.semaphore(name))

        NT = NDENSE * P
        RING = 4
        STEPS = NK // HEADS
        OPS = 2 * NGATHER * TOPK // STEPS
        ga = Gather(ctx, nc, "d", NGATHER, experts, gates, expert_u[0], expert_v[0], with_diag=False)
        h = sb("h_d", [P, NGATHER, D])
        hT = sb("hT_d", [P, DT, NT])
        u_tile = sb("u_tile", [P, RING, D])
        v_tile = sb("v_tile", [P, RING, D])
        g_tile = sb("g_tile", [P, RING, NT])
        uT = sb("uT", [P, 2, DT, P])
        act_sb = sb("act_sb", [P, 2, NT])
        coef = sb("coef_dense", [P, 2, NT])
        uT_ps = ps("uT_ps", [P, DT // 2, P])
        s_ps = ps("s_dense_ps", [P, NT])
        y_ps = [[ps(f"y_dense_ps{d}{i}", [P, BANK]) for i in range(2)] for d in range(NDENSE)]

        h_loaded = sem("h_loaded_d")
        hT_loaded = sem("hT_loaded_d")
        y_loaded = sem("y_loaded_d")
        y_cleared = sem("y_cleared")
        u_landed = [sem(f"u_landed{i}") for i in range(RING)]
        v_landed = [sem(f"v_landed{i}") for i in range(RING)]
        g_landed = [sem(f"g_landed{i}") for i in range(RING)]
        u_half = sem("u_half")
        uT_ready = sem("uT_ready")
        s_ready = sem("s_ready_d")
        act_ready = sem("act_ready")
        c_ready = sem("coef_dense_ready")
        g_used = sem("g_used")
        v_used = sem("v_used")
        y_copied = sem("y_copied_d")
        block = ctx.enter_context(nc.Block())
        u_v = expert_u[0].rearrange("(n p) d -> n p d", p=P)
        v_v = expert_v[0].rearrange("(n p) d -> n p d", p=P)
        HALF = DT // 2

        @block.sync
        def _(sp):
            for d in range(NDENSE):
                sp.dma_start(hT[:, :, d * P:(d + 1) * P],
                             hT_dram[NB - NDENSE + d].rearrange("p (t n) -> p t n", n=P)).then_inc(hT_loaded, 16)
            for i in range(NGATHER):
                sp.dma_start(h[:, i, :], h_dram[2 + i]).then_inc(h_loaded, 16)
            with sp.Fori(0, HEADS) as o:
                for s in range(STEPS):
                    n = o * STEPS + s
                    place = s % RING
                    sp.wait_ge(u_half, n * 2 + 2)
                    sp.dma_start(u_tile[:, place, :], u_v[n]).then_inc(u_landed[place], 16)
                    sp.wait_ge(g_used, n + 1)
                    sp.dma_start(g_tile[:, place, :].rearrange("p (c t) -> p c t", c=NCHUNK),
                                 table_dram[:, :, n, :].rearrange("c p t -> p c t")).then_inc(g_landed[place], 16)
                    sp.wait_ge(v_used, n + 1)
                    sp.dma_start(v_tile[:, place, :], v_v[n]).then_inc(v_landed[place], 16)
            for i in range(2):
                sp.dma_start(y_all[:, i, :], y_dram[i]).then_inc(y_loaded, 16)
            sp.wait_ge(y_loaded, 2 * 16)

        def landings(o, s):
            return o * (16 * STEPS // RING) + 16 * (s // RING + 1)

        @block.gpsimd
        def _(pool):
            with pool.Fori(0, HEADS) as o:
                for i in range(NGATHER):
                    ga.issue(pool, o * NGATHER + i, i, 2 + i, o * TOPK)

        @block.scalar
        def _(act):
            def take_half(o, s, half):
                act.wait_ge(u_half, o * (2 * STEPS) + (2 * (s + RING) + half + 1))
                act.copy(uT[:, s % 2, half * HALF:(half + 1) * HALF, :], uT_ps[:, :, :]).then_inc(uT_ready, 1)

            def unit(o, last=False):
                for s in range(STEPS):
                    following = (o, s + 1) if s < STEPS - 1 else (o + 1, 0)
                    more = not (last and s == STEPS - 1)
                    if more:
                        take_half(*following, 0)
                    act.wait_ge(s_ready, o * STEPS + (s + 1))
                    act.wait_ge(g_used, o * STEPS + (s + RING - 1))
                    act.activation(act_sb[:, s % 2, :], s_ps[:, :], ACT.Gelu_apprx_tanh).then_inc(act_ready, 1)
                    if more:
                        take_half(*following, 1)
                    for i in range(NGATHER):
                        if (2 * i + 1) * TOPK in range(s * OPS + 1, (s + 1) * OPS + 1):
                            ga.gelu(act, o * NGATHER + i, i)

            act.sem_inc(g_used, RING)
            take_half(0, 0, 0)
            take_half(0, 0, 1)
            with act.Fori(0, HEADS - 1) as o:
                unit(o)
            unit(HEADS - 1, last=True)

        @block.tensor
        def _(pe):
            def turn_half(o, s, half):
                n = o * (2 * STEPS) + (2 * s + half)
                if half == 0:
                    pe.wait_ge(u_landed[s % RING], landings(o, s))
                if s or half or not isinstance(o, int) or o > 0:
                    pe.wait_ge(uT_ready, n)
                for t in range(HALF):
                    at = half * HALF + t
                    ins = pe.transpose(uT_ps[:, t, :], u_tile[:, s % RING, at * P:(at + 1) * P], ident[:, :])
                ins.then_inc(u_half, 1)

            def score(o, s):
                pe.wait_ge(uT_ready, o * (2 * STEPS) + (2 * s + 2))
                if s or not isinstance(o, int) or o > 0:
                    pe.wait_ge(act_ready, o * STEPS + s)
                for t in range(DT):
                    ins = pe.matmul(s_ps[:, :], uT[:, s % 2, t, :], hT[:, t, :], start=(t == 0), stop=(t == DT - 1))
                ins.then_inc(s_ready, 1)

            def weigh(o, s, first=False, last=False):
                pe.wait_ge(c_ready, o * STEPS + (s + 1))
                pe.wait_ge(v_landed[s % RING], landings(o, s))
                for d in range(NDENSE):
                    for i in range(2):
                        ins = pe.matmul(y_ps[d][i][:, :], coef[:, s % 2, d * P:(d + 1) * P],
                                        v_tile[:, s % RING, i * BANK:(i + 1) * BANK], start=first, stop=last)
                ins.then_inc(v_used, 1)

            def unit(o, first=False, last=False):
                for s in range(STEPS):
                    following = (o, s + 1) if s < STEPS - 1 else (o + 1, 0)
                    more = not (last and s == STEPS - 1)
                    if more:
                        turn_half(*following, 0)
                    score(o, s)
                    if more:
                        turn_half(*following, 1)
                    if s > 0:
                        weigh(o, s - 1, first=(first and s == 1))
                    elif not first:
                        weigh(o - 1, STEPS - 1)
                if last:
                    weigh(o, STEPS - 1, last=True)

            pe.sem_inc(u_half, 2 * RING)
            pe.sem_inc(v_used, RING)
            pe.wait_ge(hT_loaded, NDENSE * 16)
            turn_half(0, 0, 0)
            turn_half(0, 0, 1)
            unit(0, first=True)
            with pe.Fori(1, HEADS - 1) as o:
                unit(o)
            unit(HEADS - 1, last=True)

        @block.vector
        def _(dve):
            def gathered(o, k):
                i, j = k // (2 * TOPK), k % (2 * TOPK)
                n = o * NGATHER + i
                if j < TOPK:
                    ga.dot(dve, n, i, j, h[:, i, :])
                else:
                    if j == TOPK:
                        ga.weigh(dve, n, i, 2 + i, o * TOPK)
                    ga.accumulate(dve, n, i, j - TOPK, y_all[:, 2 + i, :])

            dve.memset(y_all[:, 2:2 + NGATHER, :], 0.0).then_inc(y_cleared, 1)
            dve.sem_inc(ga.slot_free, TOPK)
            dve.wait_ge(y_cleared, 1)
            dve.wait_ge(h_loaded, 16 * NGATHER)
            with dve.Fori(0, HEADS) as o:
                for s in range(STEPS):
                    for k in range(s * OPS, (s + 1) * OPS):
                        gathered(o, k)
                    n = o * STEPS + s
                    dve.wait_ge(act_ready, n + 1)
                    dve.wait_ge(g_landed[s % RING], landings(o, s))
                    dve.wait_ge(v_used, n + (RING - 1))
                    dve.tensor_tensor(coef[:, s % 2, :], act_sb[:, s % 2, :], g_tile[:, s % RING, :],
                                      ALU.mult).then_inc(c_ready, 1)
                    dve.wait_ge(c_ready, n + 1)
                    dve.sem_inc(g_used, 1)
            dve.wait_ge(v_used, NK + RING)
            for d in range(NDENSE):
                for i in range(2):
                    dve.tensor_copy(y_all[:, NB - NDENSE + d, i * BANK:(i + 1) * BANK], y_ps[d][i][:, :]
                                    ).then_inc(y_copied, 1)
            dve.wait_ge(y_copied, 2 * NDENSE)


def final_block(nc, y_all, eps, x1_dram, cond_dram, g_final, out):
    with ExitStack() as ctx:
        def sb(name, shape):
            return ctx.enter_context(nc.sbuf_tensor(name, shape, F32))

        def sem(name):
            return ctx.enter_context(nc.semaphore(name))

        gt2 = sb("gt2", [P, D])
        gf = sb("gf", [P, D])
        x1 = sb("x1_f", [P, NB, D])
        square = sb("square", [P, D])
        ss = sb("final_ss", [P, NB])
        rs = sb("final_rs", [P, NB])
        rows_loaded = sem("rows_loaded_f")
        x1_loaded = [sem(f"x1_loaded_f{b}") for b in range(NB)]
        gated = sem("gated")
        summed = sem("summed")
        squared = sem("squared")
        rooted = sem("rooted")
        rs_ready = sem("final_rs_ready")
        normed = sem("normed")
        out_ready = sem("out_ready_f")
        out_stored = sem("out_stored_f")
        block = ctx.enter_context(nc.Block())
        x1_v = x1_dram.rearrange("(b p) d -> b p d", p=P)
        out_v = out[0].rearrange("(b p) d -> b p d", p=P)

        @block.sync
        def _(sp):
            sp.dma_start(gt2[:, :], broadcast(cond_dram[5 * D:6 * D])).then_inc(rows_loaded, 16)
            for b in range(NB):
                sp.dma_start(x1[:, b, :], x1_v[b]).then_inc(x1_loaded[b], 16)
            sp.dma_start(gf[:, :], broadcast(g_final)).then_inc(rows_loaded, 16)
            for b in range(NB):
                sp.wait_ge(out_ready, b + 1)
                sp.dma_start(out_v[b], x1[:, b, :]).then_inc(out_stored, 16)
            sp.wait_ge(out_stored, 16 * NB)

        @block.scalar
        def _(act):
            for b in range(NB):
                act.wait_ge(summed, b + 1)
                if b > 0:
                    act.wait_ge(squared, b)
                act.activation(square[:, :], x1[:, b, :], ACT.Square, accum_out=ss[:, b:b + 1]).then_inc(squared, 1)
                act.wait_ge(squared, b + 1)
                act.activation(rs[:, b:b + 1], ss[:, b:b + 1], ACT.Sqrt, scale=1.0 / D, bias=eps[:, :]).then_inc(rooted, 1)
                act.wait_ge(rs_ready, b + 1)
                act.activation(x1[:, b, :], x1[:, b, :], ACT.Copy, scale=rs[:, b:b + 1]).then_inc(normed, 1)

        @block.vector
        def _(dve):
            def add(b):
                if b == 0:
                    dve.wait_ge(rows_loaded, 2 * 16)
                dve.tensor_tensor(y_all[:, b, :], y_all[:, b, :], gt2[:, :], ALU.mult).then_inc(gated, 1)
                dve.wait_ge(gated, b + 1)
                dve.wait_ge(x1_loaded[b], 16)
                dve.tensor_tensor(x1[:, b, :], x1[:, b, :], y_all[:, b, :], ALU.add).then_inc(summed, 1)

            def root(b):
                dve.wait_ge(rooted, b + 1)
                dve.reciprocal(rs[:, b:b + 1], rs[:, b:b + 1]).then_inc(rs_ready, 1)

            def scale(b):
                dve.wait_ge(normed, b + 1)
                dve.tensor_tensor(x1[:, b, :], x1[:, b, :], gf[:, :], ALU.mult).then_inc(out_ready, 1)

            for b in range(NB + 2):
                if b < NB:
                    add(b)
                if 1 <= b <= NB:
                    root(b - 1)
                if b >= 2:
                    scale(b - 2)


_INS = ["x", "c", "w_ada", "b_ada", "g_norm1", "w_in", "b_in", "conv_w", "conv_b", "g_conv_ln", "b_conv_ln",
        "g_v_ln", "b_v_ln", "w_spatial", "b_spatial", "w_out", "b_out", "g_norm2", "w_query", "sub_keys",
        "expert_u", "expert_v", "g_final"]
_OUT = (1, SEQ, D)


def kernel(**inputs):
    import numpy as np
    import concourse.bacc as bacc
    from concourse.bass_utils import run_bass_kernel_spmd

    nc = bacc.Bacc("TRN2", target_bir_lowering=False, num_devices=1)
    arrays, args = {}, []
    for name in _INS:
        a = np.ascontiguousarray(inputs[name])
        arrays[f"in_{name}"] = a
        args.append(nc.dram_tensor(f"in_{name}", a.shape, mybir.dt.from_np(a.dtype), kind="ExternalInput").ap())
    out = nc.dram_tensor("out_0", _OUT, F32, kind="ExternalOutput").ap()
    build(nc, *args, out)
    r = run_bass_kernel_spmd(nc, [arrays], core_ids=[0])
    return r.results[0]["out_0"]
```

```python
from contextlib import ExitStack, contextmanager

import concourse.bass as bass
from concourse import mybir

F32 = mybir.dt.float32
U32 = mybir.dt.uint32
I32 = mybir.dt.int32
BF16 = mybir.dt.bfloat16
ALU = mybir.AluOpType
ACT = mybir.ActivationFunctionType
AX = mybir.AxisListType

P = 128
D = 1024
DT = D // P
SEQ = 1024
NB = SEQ // P
DC = D // 2
CT = DC // P
TAPS = 31
CT_DVE = 3
CARRY = TAPS - 1
GROUPS = 8
GW = DC // GROUPS
N_PROJ = 2 * D
N_COND = 6
HEADS = 8
NK = 128
TOPK = 16
QT = 2 * HEADS
PAIRS = HEADS * TOPK
EPS = 1e-6
BELOW_ALL = -3.0e38
NDENSE = 3
NGATHER = NB - NDENSE - 2
NCHUNK = 4
CHUNK = NDENSE * P // NCHUNK
BANK = 512


@contextmanager
def own_semaphores(nc):
    made = []

    def sem(name):
        made.append(nc.alloc_semaphore(name))
        return made[-1]

    yield sem
    nc.clear_and_free_semaphores(made)
    nc.all_engine_barrier()


class ClearedChain:

    def __init__(self, eng, sem, per_round):
        self.eng, self.sem, self.per_round, self.n = eng, sem, per_round, 0

    def round(self, first):
        if not first:
            self.eng.wait_ge(self.sem, self.per_round)
            self.eng.sem_clear(self.sem)
        self.n = 0

    def did(self, ins):
        ins.then_inc(self.sem, 1)
        self.n += 1

    def wait(self, behind=0):
        self.eng.wait_ge(self.sem, self.n - behind)

    def end(self):
        assert self.n == self.per_round, (self.n, self.per_round)


class Chain:

    def __init__(self, eng, sem, per_round=0):
        self.eng, self.sem, self.per_round = eng, sem, per_round
        self.base, self.n = 0, 0

    def round(self, b):
        self.base, self.n = b * self.per_round, 0

    def did(self, ins):
        ins.then_inc(self.sem, 1)
        self.n += 1

    def wait(self, behind=0):
        self.eng.wait_ge(self.sem, self.base + (self.n - behind))

    def end(self):
        assert self.n == self.per_round, (self.n, self.per_round)


def build(nc, x, c, w_ada, b_ada, g_norm1, w_in, b_in, conv_w, conv_b, g_conv_ln, b_conv_ln, g_v_ln,
          b_v_ln, w_spatial, b_spatial, w_out, b_out, g_norm2, w_query, sub_keys, expert_u, expert_v,
          g_final, out):
    cond_dram = nc.dram_tensor("cond_scratch", [N_COND * D], F32).ap()
    x1_dram = nc.dram_tensor("x1_scratch", [SEQ, D], F32).ap()
    h_dram = nc.dram_tensor("h_scratch", [NB, P, D], F32).ap()
    hT_dram = nc.dram_tensor("hT_scratch", [NB, P, D], F32).ap()
    y_dram = nc.dram_tensor("y_scratch", [2, P, D], F32).ap()
    table_dram = nc.dram_tensor("table_scratch", [NCHUNK, NK, NK, CHUNK], F32).ap()
    with ExitStack() as ctx:
        ident = ctx.enter_context(nc.sbuf_tensor("ident", [P, P], F32))
        eps = ctx.enter_context(nc.sbuf_tensor("eps", [P, 1], F32))
        ss2 = ctx.enter_context(nc.sbuf_tensor("ss2", [P, NB], F32))
        experts = ctx.enter_context(nc.sbuf_tensor("experts", [P, NB, PAIRS], U32))
        gates = ctx.enter_context(nc.sbuf_tensor("gates", [P, NB, PAIRS], F32))
        with ExitStack() as proj:
            keysT = proj.enter_context(nc.sbuf_tensor("keysT", [P, QT, NK], F32))
            w_proj = proj.enter_context(nc.sbuf_tensor("w_proj", [P, DT, N_PROJ], F32))
            w_q_loaded = proj.enter_context(nc.semaphore("w_q_loaded"))
            with ExitStack() as mix:
                consts = setup_block(nc, mix, ident, eps, keysT, w_proj, cond_dram, x, c, w_ada, b_ada, g_norm1,
                                     w_in, b_in, conv_w, conv_b, g_conv_ln, b_conv_ln, g_v_ln, b_v_ln,
                                     w_spatial, b_spatial, w_out, b_out, sub_keys)
                mixer_block(nc, consts, w_proj, ident, eps, ss2, experts, gates, x1_dram, w_query, w_q_loaded)
            routing_block(nc, w_proj, w_q_loaded, keysT, experts, gates, ident, eps, ss2, x1_dram, cond_dram,
                          h_dram, hT_dram, y_dram, g_norm2, expert_u, expert_v)
        table_block(nc, experts, gates, ident, h_dram, y_dram, table_dram, expert_u, expert_v)
        y_all = ctx.enter_context(nc.sbuf_tensor("y_all", [P, NB, D], F32))
        gt2 = ctx.enter_context(nc.sbuf_tensor("gt2", [P, D], F32))
        gf = ctx.enter_context(nc.sbuf_tensor("gf", [P, D], F32))
        dense_block(nc, experts, gates, ident, y_all, gt2, gf, h_dram, hT_dram, y_dram, table_dram, cond_dram,
                    expert_u, expert_v, g_final)
        final_block(nc, y_all, gf, eps, x1_dram, out)


def broadcast(row):
    return row.partition_broadcast(P)


def setup_block(nc, mix, ident, eps, keysT, w_proj, cond_dram, x, c, w_ada, b_ada, g_norm1, w_in, b_in, conv_w, conv_b,
                g_conv_ln, b_conv_ln, g_v_ln, b_v_ln, w_spatial, b_spatial, w_out, b_out, sub_keys):
    k = {}

    def keep(name, shape):
        k[name] = mix.enter_context(nc.sbuf_tensor(name, shape, F32))
        return k[name]

    w_in_sb = w_proj
    w_out_sb = keep("w_out_sb", [P, DT, D])
    x_all = keep("x_all", [P, NB, D])
    rs1 = keep("rs1", [P, NB])
    g1_col = keep("g1_col", [P, DT])
    sh1_col = keep("sh1_col", [P, DT])
    cols = keep("cols", [P, 36])
    gate_bias = keep("gate_bias", [P, CT])
    conv_taps = keep("conv_taps", [P, CT, TAPS])
    ws = keep("ws", [P, GROUPS, P])
    rows = keep("rows", [P, 6, DC])
    gt1 = keep("gt1", [P, D])
    gt1_b_out = keep("gt1_b_out", [P, D])
    C, G1, BIN, CB, BS = (0, 8), (8, 8), (16, 8), (24, 4), (28, 8)
    k["bv_col"], k["cb_col"], k["bs_col"] = cols[:, 16:20], cols[:, 24:28], cols[:, 28:36]
    bz, g_conv, b_conv, g_v, b_v = rows[:, 0:2, :], rows[:, 2, :], rows[:, 3, :], rows[:, 4, :], rows[:, 5, :]
    k.update(bz=bz, g_conv=g_conv, b_conv=b_conv, g_v=g_v, b_v=b_v)
    NCH = N_COND * D // BANK

    with own_semaphores(nc) as sem, ExitStack() as ctx:
        def sb(name, shape):
            return ctx.enter_context(nc.sbuf_tensor(name, shape, F32))

        staged = sb("staged", [36, P])
        staged_cond = sb("staged_cond", [16, P])
        silu_half = sb("silu_half", [P, DT])
        silu_tanh = sb("silu_tanh", [P, DT])
        silu_c = sb("silu_c", [P, DT])
        cond_row = sb("cond_row", [1, 2, BANK])
        one_plus = sb("one_plus", [P, DT])
        mean_sq = sb("mean_sq", [P, NB])
        rms = sb("rms", [P, NB])
        w_ada_all = sb("w_ada_sb", [P, 2, DT, BANK])
        w_ada_sb = [w_ada_all[:, 0, :, :], w_ada_all[:, 1, :, :],
                    w_out_sb[:, DT // 2:, :].rearrange("p t (a n) -> p (t a) n", a=2)]
        junk = w_out_sb[:, 0, :]
        ws_raw = w_out_sb[:, 1, :].rearrange("p (h s) -> p h s", h=GROUPS)
        keys_raw = w_out_sb[:, 2:4, :].rearrange("p a (t d) -> p (a t) d", d=P)
        taps_rows = w_out_sb[0:TAPS, 0, 0:DC]
        bada_row = gt1[0:1, :].rearrange("p (a n) -> p a n", a=2)
        rows_ps = ctx.enter_context(nc.psum_tensor("rows_ps", [P, BANK], F32))
        taps_ps = ctx.enter_context(nc.psum_tensor("taps_ps", [P, CT, TAPS + 1], F32))
        ws_ps = ctx.enter_context(nc.psum_tensor("ws_ps", [P, GROUPS, P], F32))
        cond_ps = [ctx.enter_context(nc.psum_tensor(f"cond_ps{i}", [P, BANK], F32)) for i in range(2)]

        ident_done = sem("ident_done")
        eps_set = sem("eps_set")
        small_loaded = sem("small_loaded")
        keys_loaded = sem("keys_loaded")
        rows_loaded = sem("rows_loaded")
        x_loaded = sem("x_loaded")
        w_ada_loaded = [sem(f"w_ada_loaded{i}") for i in range(3)]
        b_ada_loaded = [sem(f"b_ada_loaded{i}") for i in range(2)]
        w_loaded = sem("w_loaded")
        w_out_loaded = sem("w_out_loaded")
        cols_transposed = sem("cols_transposed")
        cols_ready = sem("cols_ready")
        silu_halved = sem("silu_halved")
        tanh_done = sem("tanh_done")
        silu_ready = sem("silu_ready")
        taps_transposed = sem("taps_transposed")
        ws_transposed = sem("ws_transposed")
        ws_copied = sem("ws_copied")
        ws_masked = sem("ws_masked")
        cond_done = sem("cond_done")
        cond_added = sem("cond_added")
        cond_stored = [sem(f"cond_stored{i}") for i in range(2)]
        cond_reloaded = sem("cond_reloaded")
        cond_transposed = sem("cond_transposed")
        gt1_loaded = sem("gt1_loaded")
        squares_done = sem("squares_done")
        rms_done = sem("rms_done")
        dve_chain = sem("setup_dve_chain")
        block = ctx.enter_context(nc.Block())

        @block.sync
        def _(sp):
            w_in_v = w_in[0].rearrange("(t p) n -> p t n", p=P)
            w_ada_v = w_ada[0].rearrange("(t p) n -> p t n", p=P)
            b_ada_v = b_ada.rearrange("l (g n) -> l g n", n=BANK)
            sp.dma_start(staged[C[0]:C[0] + C[1], :], c[0].rearrange("(t p) -> t p", p=P)).then_inc(small_loaded, 16)
            sp.dma_start(staged[G1[0]:G1[0] + G1[1], :], g_norm1[0].rearrange("(t p) -> t p", p=P)).then_inc(small_loaded, 16)
            sp.dma_start(staged[BIN[0]:BIN[0] + BIN[1], :], b_in[0, 0:D].rearrange("(t p) -> t p", p=P)).then_inc(small_loaded, 16)
            sp.dma_start(staged[CB[0]:CB[0] + CB[1], :], conv_b[0].rearrange("(t p) -> t p", p=P)).then_inc(small_loaded, 16)
            sp.dma_start(staged[BS[0]:BS[0] + BS[1], :], b_spatial[0]).then_inc(small_loaded, 16)
            sp.dma_start(taps_rows[:, :], conv_w[0]).then_inc(small_loaded, 16)
            sp.dma_start(ws_raw, w_spatial[0].rearrange("h t s -> t h s")).then_inc(small_loaded, 16)
            sp.dma_start(keys_raw, sub_keys[0].rearrange("h i n d -> n (h i) d")).then_inc(keys_loaded, 16)
            def store_cond(g):
                sp.wait_ge(cond_added, g + 1)
                sp.dma_start(cond_dram[g * BANK:(g + 1) * BANK].rearrange("(a n) -> a n", a=1),
                             cond_row[:, g % 2, :]).then_inc(cond_stored[g % 2], 16)

            W_IN_AFTER = (7, 9, 10, 11)
            for g in range(NCH):
                if g >= 3:
                    sp.wait_ge(cond_done, g - 2)
                sp.dma_start(w_ada_sb[g % 3], w_ada_v[:, :, g * BANK:(g + 1) * BANK]).then_inc(w_ada_loaded[g % 3], 16)
                if g >= 2:
                    store_cond(g - 2)
                sp.dma_start(bada_row[:, g % 2, :], b_ada_v[:, g, :]).then_inc(b_ada_loaded[g % 2], 16)
                if g == 1:
                    for r, row in ((0, b_in[0, D:D + DC]), (1, b_in[0, D + DC:2 * D]), (2, g_conv_ln[0]),
                                   (3, b_conv_ln[0]), (4, g_v_ln[0]), (5, b_v_ln[0])):
                        sp.dma_start(rows[:, r, :], broadcast(row)).then_inc(rows_loaded, 16)
                    sp.dma_start(gt1_b_out[:, :], broadcast(b_out[0])).then_inc(rows_loaded, 16)
                    sp.dma_start(x_all[:, :, :], x[0].rearrange("(b p) d -> p b d", p=P)).then_inc(x_loaded, 16)
                if g in W_IN_AFTER:
                    t = 2 * W_IN_AFTER.index(g)
                    sp.dma_start(w_in_sb[:, t:t + 2, :], w_in_v[:, t:t + 2, :]).then_inc(w_loaded, 16)
            for g in range(NCH - 2, NCH):
                store_cond(g)
            for i in range(2):
                sp.wait_ge(cond_stored[i], 16 * NCH // 2)
            sp.dma_start(staged_cond[:, :], cond_dram[0:2 * D].rearrange("(t p) -> t p", p=P)).then_inc(cond_reloaded, 16)
            sp.dma_start(gt1[:, :], broadcast(cond_dram[2 * D:3 * D])).then_inc(gt1_loaded, 16)
            sp.wait_ge(w_loaded, 16 * (DT // 2))

        @block.gpsimd
        def _(pool):
            pool.memset(eps[:, :], EPS).then_inc(eps_set, 1)
            pool.memset(ident[:, :], 0.0).then_inc(ident_done, 1)
            pool.wait_ge(ident_done, 1)
            pool.affine_select(out=ident[:, :], in_=ident[:, :], compare_op=ALU.not_equal, fill=1.0, base=0,
                               pattern=[[-1, P]], channel_multiplier=1).then_inc(ident_done, 1)
            pool.wait_ge(ws_copied, 1)
            pool.affine_select(out=ws[:, :, :], in_=ws[:, :, :], compare_op=ALU.is_ge, fill=0.0, base=0,
                               pattern=[[0, GROUPS], [1, P]], channel_multiplier=-1).then_inc(ws_masked, 1)
            pool.wait_ge(ws_masked, 1)
            pool.wait_ge(squares_done, NB)
            pool.wait_ge(ws_transposed, 1 + QT // DT)
            pool.wait_ge(taps_transposed, 1)
            w_out_v = w_out[0].rearrange("(t p) n -> p t n", p=P)
            pool.dma_start(w_out_sb[:, 0:DT // 2, :], w_out_v[:, 0:DT // 2, :]).then_inc(w_out_loaded, 16)
            pool.wait_ge(cond_done, NCH)
            pool.dma_start(w_out_sb[:, DT // 2:, :], w_out_v[:, DT // 2:, :]).then_inc(w_out_loaded, 16)
            pool.wait_ge(w_out_loaded, 2 * 16)

        @block.scalar
        def _(act):
            act.wait_ge(silu_halved, 1)
            act.activation(silu_tanh[:, :], silu_half[:, :], ACT.Tanh).then_inc(tanh_done, 1)
            for i, to in enumerate((ws[:, :, :], keysT[:, 0:DT, :], keysT[:, DT:, :])):
                act.wait_ge(ws_transposed, i + 1)
                act.copy(to, ws_ps[:, :, :]).then_inc(ws_copied, 1)
            act.wait_ge(x_loaded, 16)
            for b in range(NB):
                if b:
                    act.wait_ge(squares_done, b)
                act.activation(junk, x_all[:, b, :], ACT.Square, accum_out=mean_sq[:, b:b + 1]).then_inc(squares_done, 1)
            act.wait_ge(squares_done, NB)
            act.wait_ge(eps_set, 1)
            act.activation(rms[:, :], mean_sq[:, :], ACT.Sqrt, scale=1.0 / D, bias=eps[:, :]).then_inc(rms_done, 1)

        @block.tensor
        def _(pe):
            pe.wait_ge(ident_done, 2)
            pe.wait_ge(small_loaded, 7 * 16)
            pe.transpose(rows_ps[:, 0:36], staged[:, :], ident[0:36, 0:36]).then_inc(cols_transposed, 1)
            for m in range(CT):
                last = pe.transpose(taps_ps[:, m, 0:TAPS], taps_rows[:, m * P:(m + 1) * P], ident[0:TAPS, 0:TAPS])
            last.then_inc(taps_transposed, 1)
            for h in range(GROUPS):
                last = pe.transpose(ws_ps[:, h, :], ws_raw[:, h, :], ident[:, :])
            last.then_inc(ws_transposed, 1)
            pe.wait_ge(keys_loaded, 16)
            for i in range(QT // DT):
                pe.wait_ge(ws_copied, i + 1)
                for t in range(DT):
                    last = pe.transpose(ws_ps[:, t, :], keys_raw[:, i * DT + t, :], ident[:, :])
                last.then_inc(ws_transposed, 1)
            pe.wait_ge(silu_ready, 1)
            for g in range(NCH):
                pe.wait_ge(w_ada_loaded[g % 3], 16 * (g // 3 + 1))
                if g >= 2:
                    pe.wait_ge(cond_added, g - 1)
                for t in range(DT):
                    last = pe.matmul(cond_ps[g % 2][0:1, :], silu_c[:, t:t + 1], w_ada_sb[g % 3][:, t, :],
                                     start=(t == 0), stop=(t == DT - 1))
                last.then_inc(cond_done, 1)
            pe.wait_ge(cond_reloaded, 16)
            pe.wait_ge(cols_ready, 1)
            pe.transpose(rows_ps[:, 64:80], staged_cond[:, :], ident[0:16, 0:16]).then_inc(cond_transposed, 1)

        @block.vector
        def _(dve):
            ch = Chain(dve, dve_chain)
            dve.wait_ge(cols_transposed, 1)
            dve.tensor_copy(cols[:, :], rows_ps[:, 0:36]).then_inc(cols_ready, 1)
            dve.wait_ge(cols_ready, 1)
            dve.tensor_scalar(silu_half[:, :], cols[:, 0:DT], 0.5, None, ALU.mult).then_inc(silu_halved, 1)
            ch.did(dve.tensor_scalar(gate_bias[:, :], cols[:, 20:24], 0.5, None, ALU.mult))
            dve.wait_ge(tanh_done, 1)
            dve.wait_ge(silu_halved, 1)
            dve.scalar_tensor_tensor(out=silu_c[:, :], in0=silu_tanh[:, :], scalar=1.0, in1=silu_half[:, :],
                                     op0=ALU.add, op1=ALU.mult).then_inc(silu_ready, 1)
            dve.wait_ge(taps_transposed, 1)
            ch.did(dve.tensor_copy(conv_taps[:, :, :], taps_ps[:, :, 0:TAPS]))
            for g in range(NCH):
                dve.wait_ge(cond_done, g + 1)
                dve.wait_ge(b_ada_loaded[g % 2], 16 * (g // 2 + 1))
                if g >= 2:
                    dve.wait_ge(cond_stored[g % 2], 16 * (g // 2))
                dve.tensor_tensor(cond_row[:, g % 2, :], cond_ps[g % 2][0:1, :], bada_row[:, g % 2, :],
                                  ALU.add).then_inc(cond_added, 1)
            dve.wait_ge(rows_loaded, 7 * 16)
            ch.did(dve.tensor_scalar(g_conv, g_conv, 0.5, None, ALU.mult))
            ch.did(dve.tensor_scalar(b_conv, b_conv, 0.5, None, ALU.mult))
            dve.wait_ge(rms_done, 1)
            ch.did(dve.reciprocal(rs1[:, :], rms[:, :]))
            dve.wait_ge(cond_transposed, 1)
            ch.did(dve.tensor_copy(sh1_col[:, :], rows_ps[:, 64:64 + DT]))
            ch.did(dve.tensor_scalar(one_plus[:, :], rows_ps[:, 64 + DT:64 + 2 * DT], 1.0, None, ALU.add))
            ch.wait()
            ch.did(dve.tensor_tensor(g1_col[:, :], one_plus[:, :], cols[:, 8:16], ALU.mult))
            dve.wait_ge(gt1_loaded, 16)
            ch.did(dve.tensor_tensor(gt1_b_out[:, :], gt1_b_out[:, :], gt1[:, :], ALU.mult))
            ch.wait()
    return k


def mixer_block(nc, k, w_in_sb, ident, eps, ss2, experts, gates, x1_dram, w_query, w_q_loaded):
    K1, K2 = 8, 99
    KP = (CT - CT_DVE) * (2 * TAPS - 1) - 1
    w_out_sb, x_all, ws = k["w_out_sb"], k["x_all"], k["ws"]
    taps, cb, bv = k["conv_taps"], k["cb_col"], k["bv_col"]
    HALF = DT // 2
    with own_semaphores(nc) as sem, ExitStack() as ctx:
        def sb(name, shape):
            return ctx.enter_context(nc.sbuf_tensor(name, shape, F32))

        def ps(name, shape):
            return ctx.enter_context(nc.psum_tensor(name, shape, F32))

        xn = sb("xn", [P, D])
        hT = sb("hT", [P, DT, P])
        gate_tanh = sb("gate_tanh", [P, CT, P])
        a = sb("a", [P, CT, CARRY + P])
        acc = sb("acc", [P, CT, P])
        z = sb("z", [P, 2, DC])
        u = sb("u", [P, DC])
        v = sb("v", [P, GROUPS, GW])
        vn = sb("vn", [P, GROUPS, GW])
        cc = sb("cc", [P, GROUPS, GW])
        total = sb("total", [P, 2, GROUPS])
        var = sb("var", [P, 2, GROUPS])
        std = sb("std", [P, 2, GROUPS])
        tapped = experts[:, DC // PAIRS:DC // PAIRS + 3 * (CT - CT_DVE), :].bitcast(F32).rearrange(
            "p (w m) c -> p w m c", w=3)
        silu_tanh = sb("mix_silu_tanh", [P, DC])
        y_conv = sb("y_conv", [P, DC])
        y_gmlp = sb("y_gmlp", [P, GROUPS, GW])
        yT = sb("yT", [P, DT, P])
        yo = gates[:, :, :].rearrange("p b k -> p (b k)")
        squares = experts[:, 0:DC // PAIRS, :].bitcast(F32).rearrange("p b (g w) -> p (b g) w", w=GW)
        turned_ps = ps("turned_ps", [P, DT, P])
        conv_ps = ps("conv_ps", [P, GROUPS, GW])
        val_ps = ps("val_ps", [P, CT, P])
        gates_ps = ps("gates_ps", [P, CT, P])
        wide_ps = ps("wide_ps", [P, 2, BANK])
        mixed_ps = ps("mixed_ps", [P, GROUPS, GW])

        xn_ready = sem("xn_ready")
        xn_turned = sem("xn_turned")
        hT_ready = sem("hT_ready")
        x_biased = sem("x_biased")
        gates_ready = sem("gates_ready")
        gate_tanh_ready = sem("gate_tanh_ready")
        val_ready = sem("val_ready")
        a_ready = sem("a_ready")
        z_ready = sem("z_ready")
        z_biased = sem("z_biased")
        gelu_done = sem("gelu_done")
        v_var = sem("v_var")
        v_std = sem("v_std")
        vn_ready = sem("vn_ready")
        mixed = sem("mixed")
        gmlp_ready = sem("gmlp_ready")
        conv_done = sem("conv_done")
        pool_conv_done = sem("pool_conv_done")
        pool_conv_started = sem("pool_conv_started")
        pool_chain = sem("pool_conv_chain")
        conv_turned = sem("conv_turned")
        conv_var = sem("conv_var")
        conv_std = sem("conv_std")
        conv_normed = sem("conv_normed")
        conv_tanh = sem("conv_tanh")
        y_ready = sem("y_ready")
        y_turned = sem("y_turned")
        yT_ready = sem("yT_ready")
        out_ready = sem("out_ready")
        carry_cleared = sem("carry_cleared")
        out_taken = sem("out_taken")
        x1_ready = sem("x1_ready")
        x1_squared = sem("x1_squared")
        x1_stored = sem("x1_stored")
        chain1 = sem("chain1")
        chain2 = sem("chain2")
        block = ctx.enter_context(nc.Block())

        @block.sync
        def _(sp):
            x1_v = x1_dram.rearrange("(b p) d -> b p d", p=P)
            w_v = w_query[0].rearrange("(t p) n -> p t n", p=P)
            sp.wait_ge(z_ready, 2 * NB)
            for t in range(0, DT, 2):
                sp.dma_start(w_in_sb[:, t:t + 2, :], w_v[:, t:t + 2, :]).then_inc(w_q_loaded, 16)
            with sp.Fori(0, NB) as b:
                sp.wait_ge(x1_ready, b + 1)
                sp.dma_start(x1_v[b], x_all[:, b, :]).then_inc(x1_stored, 16)
            sp.wait_ge(x1_stored, 16 * NB)

        @block.gpsimd
        def _(pool):
            ch = ClearedChain(pool, pool_chain, KP)
            tiles = range(CT_DVE, CT)

            def convolve():
                for m in tiles:
                    ch.did(pool.tensor_scalar(acc[:, m, :], a[:, m, 0:P], k["conv_taps"][:, m, 0:1],
                                              k["cb_col"][:, m:m + 1], ALU.mult, ALU.add))
                for w in range(1, TAPS + 1):
                    for m in tiles:
                        if w < TAPS:
                            ch.did(pool.tensor_scalar(tapped[:, w % 3, m - CT_DVE, :], a[:, m, w:w + P],
                                                      k["conv_taps"][:, m, w:w + 1], None, ALU.mult))
                    if w > 1:
                        ch.wait(behind=len(tiles) if w < TAPS else 0)
                        for m in tiles:
                            ins = pool.tensor_tensor(acc[:, m, :], acc[:, m, :], tapped[:, (w - 1) % 3, m - CT_DVE, :], ALU.add)
                            if (w, m) == (TAPS, tiles[-1]):
                                ins.then_inc(pool_conv_done, 1)
                            else:
                                ch.did(ins)

            def block(b, first=False):
                ch.round(first)
                pool.wait_ge(xn_ready, b + 1)
                pool.tensor_tensor(x_all[:, b, :], x_all[:, b, :], k["gt1_b_out"][:, :], ALU.add).then_inc(x_biased, 1)
                pool.wait_ge(a_ready, b + 1)
                if not first:
                    pool.wait_ge(conv_turned, b)
                pool.sem_inc(pool_conv_started, 1)
                convolve()
                ch.end()

            block(0, first=True)
            with pool.Fori(1, NB) as b:
                block(b)

        @block.scalar
        def _(act):
            def norm(b):
                act.activation(xn[:, :], x_all[:, b, :], ACT.Copy, scale=k["rs1"][:, bass.ds(b, 1)]).then_inc(xn_ready, 1)

            def project_in(b):
                act.wait_ge(xn_turned, b + 1)
                for i in range(2):
                    for t in range(i * HALF, (i + 1) * HALF):
                        last = act.activation(hT[:, t, :], turned_ps[:, t, :], ACT.Identity,
                                              scale=k["g1_col"][:, t:t + 1], bias=k["sh1_col"][:, t:t + 1])
                    last.then_inc(hT_ready, 1)
                act.wait_ge(gates_ready, b + 1)
                for m in range(CT):
                    last = act.activation(gate_tanh[:, m, :], gates_ps[:, m, :], ACT.Tanh, scale=0.5,
                                          bias=k["gate_bias"][:, m:m + 1])
                last.then_inc(gate_tanh_ready, 1)
                for i, to in ((1, v[:, :, :].rearrange("p h c -> p (h c)")), (0, u[:, :])):
                    act.wait_ge(z_biased, 2 * b + 2 - i)
                    act.activation(to, z[:, i, :], ACT.Gelu_apprx_tanh).then_inc(gelu_done, 1)

            def project_in_end(b):
                act.wait_ge(v_var, b + 1)
                act.activation(std[:, 0, :], var[:, 0, :], ACT.Sqrt, scale=1.0 / GW, bias=eps[:, :]).then_inc(v_std, 1)

            def conv(b):
                act.wait_ge(conv_var, b + 1)
                act.activation(std[:, 1, :], var[:, 1, :], ACT.Sqrt, scale=1.0 / GW, bias=eps[:, :]).then_inc(conv_std, 1)
                act.wait_ge(conv_normed, b + 1)
                act.activation(silu_tanh[:, :], cc[:, :, :].rearrange("p h c -> p (h c)"), ACT.Tanh).then_inc(conv_tanh, 1)

            def turned(b):
                act.wait_ge(y_turned, b + 1)
                act.copy(yT[:, :, :], turned_ps[:, :, :]).then_inc(yT_ready, 1)

            norm(0)
            project_in(0)
            project_in_end(0)
            norm(1)
            project_in(1)
            project_in_end(1)
            conv(0)
            with act.Fori(1, NB - 1) as i:
                norm(i + 1)
                turned(i - 1)
                project_in(i + 1)
                project_in_end(i + 1)
                conv(i)
            turned(NB - 2)
            conv(NB - 1)
            turned(NB - 1)
            for b in range(NB):
                act.wait_ge(x1_ready, b + 1)
                if b:
                    act.wait_ge(x1_squared, b)
                act.activation(xn[:, :], x_all[:, b, :], ACT.Square, accum_out=ss2[:, b:b + 1]).then_inc(x1_squared, 1)

        @block.tensor
        def _(pe):
            def turn_x(b):
                pe.wait_ge(xn_ready, b + 1)
                for t in range(DT):
                    last = pe.transpose(turned_ps[:, t, :], xn[:, t * P:(t + 1) * P], ident[:, :])
                last.then_inc(xn_turned, 1)

            def project_in(b, early=False):
                for m, to, sig in ((CT, gates_ps, gates_ready), (0, val_ps, val_ready)):
                    for j in range(CT):
                        for t in range(DT):
                            if (m, j) == (CT, 0) and t % HALF == 0:
                                pe.wait_ge(hT_ready, 2 * b + (t // HALF + 1))
                            last = pe.matmul(to[:, j, :], w_in_sb[:, t, (m + j) * P:(m + j + 1) * P], hT[:, t, :],
                                             start=(t == 0), stop=(t == DT - 1))
                    last.then_inc(sig, 1)
                if not early:
                    pe.wait_ge(out_taken, b - 1)
                for i in (1, 0):
                    for t in range(DT):
                        last = pe.matmul(wide_ps[:, i, :], hT[:, t, :], w_in_sb[:, t, D + i * DC:D + (i + 1) * DC],
                                         start=(t == 0), stop=(t == DT - 1))
                    last.then_inc(z_ready, 1)

            def turn_y(b):
                pe.wait_ge(gmlp_ready, b + 1)
                pe.wait_ge(y_ready, b + 1)
                gm = y_gmlp[:, :, :].rearrange("p h c -> p (h c)")
                for t in range(DT):
                    src = (y_conv[:, :] if t < CT else gm)[:, (t % CT) * P:(t % CT + 1) * P]
                    last = pe.transpose(turned_ps[:, t, :], src, ident[:, :])
                last.then_inc(y_turned, 1)

            def mix(b, half=None):
                pe.wait_ge(vn_ready, b + 1)
                for h in range(GROUPS) if half is None else range(half * GROUPS // 2, (half + 1) * GROUPS // 2):
                    last = pe.matmul(mixed_ps[:, h, :], ws[:, h, :], vn[:, h, :], start=True, stop=True)
                if half != 0:
                    last.then_inc(mixed, 1)

            def turn_conv(b):
                pe.wait_ge(conv_done, b + 1)
                pe.wait_ge(pool_conv_done, b + 1)
                for m in range(CT):
                    last = pe.transpose(conv_ps[:, 2 * m:2 * m + 2, :].rearrange("p g c -> p (g c)"), acc[:, m, :], ident[:, :])
                last.then_inc(conv_turned, 1)

            def project_out(b, tail=False):
                pe.wait_ge(yT_ready, b + 1)
                if tail:
                    pe.wait_ge(z_biased, 2 * NB)
                    pe.wait_ge(out_taken, b + 1)
                for i in range(2):
                    if not tail:
                        pe.wait_ge(z_biased, 2 * b + 6 - i)
                    for t in range(DT):
                        last = pe.matmul(wide_ps[:, i, :], yT[:, t, :], w_out_sb[:, t, i * BANK:(i + 1) * BANK],
                                         start=(t == 0), stop=(t == DT - 1))
                last.then_inc(out_ready, 1)

            turn_x(0)
            project_in(0, early=True)
            mix(0)
            turn_x(1)
            project_in(1, early=True)
            turn_conv(0)
            with pe.Fori(1, NB - 1) as i:
                turn_y(i - 1)
                mix(i, 0)
                pe.wait_ge(yT_ready, i)
                turn_x(i + 1)
                mix(i, 1)
                project_in(i + 1)
                turn_conv(i)
                project_out(i - 1)
            turn_y(NB - 2)
            mix(NB - 1)
            turn_conv(NB - 1)
            project_out(NB - 2, tail=True)
            turn_y(NB - 1)
            project_out(NB - 1, tail=True)

        @block.vector
        def _(dve):
            ch1, ch2 = Chain(dve, chain1, K1), Chain(dve, chain2, K2)

            def over_groups(t):
                return t.unsqueeze(2).to_broadcast([P, GROUPS, GW])

            def moments(ch, src, centred, i, var_ready):
                ch.did(dve.tensor_reduce(total[:, i, :], src, AX.X, ALU.add))
                ch.wait()
                ch.did(dve.scalar_tensor_tensor(out=centred, in0=over_groups(total[:, i, :]), scalar=-1.0 / GW, in1=src,
                                                op0=ALU.mult, op1=ALU.add))
                ch.wait()
                ch.did(dve.tensor_tensor(squares, centred, centred, ALU.mult))
                ch.wait()
                dve.tensor_reduce(var[:, i, :], squares, AX.X, ALU.add).then_inc(var_ready, 1)

            def scaled(ch, t, i, std_ready, b, g, shift, ready):
                dve.wait_ge(std_ready, b + 1)
                ch.did(dve.reciprocal(std[:, i, :], std[:, i, :]))
                ch.wait()
                ch.did(dve.tensor_tensor(t, t, over_groups(std[:, i, :]), ALU.mult))
                ch.wait()
                ch.did(dve.tensor_tensor(t, t, g.rearrange("p (h c) -> p h c", h=GROUPS), ALU.mult))
                ch.wait()
                dve.tensor_tensor(t, t, shift.rearrange("p (h c) -> p h c", h=GROUPS), ALU.add).then_inc(ready, 1)

            def take_a(b, first=False):
                ch1.round(b)
                if not first:
                    dve.wait_ge(pool_conv_done, b)
                ch1.did(dve.tensor_copy(a[:, :, 0:CARRY], a[:, :, P:P + CARRY]))
                dve.wait_ge(gate_tanh_ready, b + 1)
                ch1.did(dve.tensor_scalar(gate_tanh[:, :, :], gate_tanh[:, :, :], 1.0, 0.5, ALU.add, ALU.mult))
                ch1.wait()
                dve.wait_ge(val_ready, b + 1)
                for m in range(CT):
                    last = dve.scalar_tensor_tensor(out=a[:, m, CARRY:], in0=val_ps[:, m, :], scalar=bv[:, m:m + 1],
                                                    in1=gate_tanh[:, m, :], op0=ALU.add, op1=ALU.mult)
                last.then_inc(a_ready, 1)

            def take_z(b):
                for i in (1, 0):
                    dve.wait_ge(z_ready, 2 * b + 2 - i)
                    dve.tensor_tensor(z[:, i, :], wide_ps[:, i, :], k["bz"][:, i, :], ALU.add).then_inc(z_biased, 1)
                dve.wait_ge(gelu_done, 2 * b + 1)
                moments(ch1, v[:, :, :], vn[:, :, :], 0, v_var)

            def norm_v(b):
                scaled(ch1, vn[:, :, :], 0, v_std, b, k["g_v"], k["b_v"], vn_ready)
                ch1.end()

            def conv(b):
                ch2.round(b)
                dve.wait_ge(a_ready, b + 1)
                for w in range(TAPS):
                    for m in range(CT_DVE):
                        src, tap = a[:, m, w:w + P], taps[:, m, w:w + 1]
                        if w == 0:
                            ch2.did(dve.tensor_scalar(acc[:, m, :], src, tap, cb[:, m:m + 1], ALU.mult, ALU.add))
                        else:
                            ch2.wait(behind=CT_DVE - 1)
                            ins = dve.scalar_tensor_tensor(out=acc[:, m, :], in0=src, scalar=tap, in1=acc[:, m, :],
                                                           op0=ALU.mult, op1=ALU.add)
                            if (w, m) == (TAPS - 1, CT_DVE - 1):
                                ins.then_inc(conv_done, 1)
                            else:
                                ch2.did(ins)

            def gate_mixed(b):
                dve.wait_ge(mixed, b + 1)
                dve.wait_ge(gelu_done, 2 * b + 2)
                ch2.did(dve.tensor_tensor(y_gmlp[:, :, :], mixed_ps[:, :, :], over_groups(k["bs_col"]), ALU.add))
                ch2.wait()
                gm = y_gmlp[:, :, :].rearrange("p h c -> p (h c)")
                dve.tensor_tensor(gm, gm, u[:, :], ALU.mult).then_inc(gmlp_ready, 1)

            def conv_moments(b):
                dve.wait_ge(conv_turned, b + 1)
                moments(ch2, conv_ps[:, :, :], cc[:, :, :], 1, conv_var)

            def conv_norm(b):
                scaled(ch2, cc[:, :, :], 1, conv_std, b, k["g_conv"], k["b_conv"], conv_normed)

            def conv_silu(b):
                dve.wait_ge(conv_normed, b + 1)
                dve.wait_ge(conv_tanh, b + 1)
                dve.scalar_tensor_tensor(out=y_conv[:, :], in0=silu_tanh[:, :], scalar=1.0,
                                         in1=cc[:, :, :].rearrange("p h c -> p (h c)"),
                                         op0=ALU.add, op1=ALU.mult).then_inc(y_ready, 1)
                ch2.end()

            def residual(b):
                dve.wait_ge(out_ready, b + 1)
                dve.tensor_tensor(yo, wide_ps[:, :, :].rearrange("p a n -> p (a n)"), k["gt1"][:, :],
                                  ALU.mult).then_inc(out_taken, 1)
                dve.wait_ge(out_taken, b + 2)
                dve.wait_ge(x_biased, b + 1)
                dve.tensor_tensor(x_all[:, b, :], x_all[:, b, :], yo, ALU.add).then_inc(x1_ready, 1)

            dve.memset(a[:, :, P:P + CARRY], 0.0).then_inc(carry_cleared, 1)
            dve.wait_ge(carry_cleared, 1)
            dve.sem_inc(out_taken, 1)
            take_a(0, first=True)
            take_z(0)
            norm_v(0)
            conv(0)
            gate_mixed(0)
            take_a(1)
            take_z(1)
            conv_moments(0)
            norm_v(1)
            conv_norm(0)
            conv_silu(0)
            with dve.Fori(1, NB - 1) as i:
                conv(i)
                gate_mixed(i)
                take_a(i + 1)
                take_z(i + 1)
                conv_moments(i)
                norm_v(i + 1)
                conv_norm(i)
                conv_silu(i)
                residual(i - 1)
            conv(NB - 1)
            gate_mixed(NB - 1)
            conv_moments(NB - 1)
            conv_norm(NB - 1)
            conv_silu(NB - 1)
            residual(NB - 2)
            dve.wait_ge(x1_ready, NB - 1)
            residual(NB - 1)


class Gather:

    def __init__(self, ctx, nc, tag, ring, parts, experts, gates, expert_u, expert_v):
        def sb(name, shape, dt=F32):
            return ctx.enter_context(nc.sbuf_tensor(f"{name}_{tag}", shape, dt))

        def sem(name):
            return ctx.enter_context(nc.semaphore(f"{name}_{tag}"))

        self.parts, self.width = parts, TOPK // parts
        self.experts, self.gates, self.u, self.v = experts, gates, expert_u, expert_v
        self.slots = sb("slots", [P, TOPK, D])
        self.wanted = sb("wanted", [P, ring, TOPK], U32)
        places = ring if parts == 1 else 1
        self.dots = sb("dots", [P, places, TOPK])
        self.dots_gelu = sb("dots_gelu", [P, places, TOPK])
        self.coef = sb("coef", [P, places, TOPK])
        if parts == 2:
            self.diag = sb("diag", [P, 4, P])
            self.diag_ready = sem("diag_ready")
        self.staged = sem("staged")
        self.claims = sem("claims")
        self.u_used = sem("u_used")
        self.slot_free = sem("slot_free")
        self.landed = [sem(f"landed{j}") for j in range(TOPK)]
        self.gelu_done = sem("dots_gelu_done")
        self.coef_ready = sem("coef_ready")

    def stage(self, pool, n, p, b, first_pair):
        pool.tensor_copy(self.wanted[:, p, :], self.experts[:, b, bass.ds(first_pair, TOPK)]).then_inc(self.staged, 1)
        pool.wait_ge(self.staged, n + 1)

    def issue(self, pool, table, n, p, half=0):
        free = self.slot_free if table is self.u else self.u_used
        for j in range(half * self.width, (half + 1) * self.width):
            pool.wait_ge(free, n * TOPK + (j + 1))
            pool.sem_inc(self.claims, 1)
            pool.indirect_dma_start(self.slots[:, j, :], None, table,
                                    bass.IndirectOffsetOnAxis(ap=self.wanted[:, p, j:j + 1], axis=0)
                                    ).then_inc(self.landed[j], 16)

    def issue_head(self, pool, n, p, b, more):
        self.issue(pool, self.u, n, p, 1)
        self.issue(pool, self.v, n, p, 0)
        if more:
            self.stage(pool, n + 1, 1 - p, b, (n + 1) * TOPK)
            self.issue(pool, self.u, n + 1, 1 - p, 0)
        self.issue(pool, self.v, n, p, 1)

    def issue_block(self, pool, b):
        self.stage(pool, 0, 0, b, 0)
        self.issue(pool, self.u, 0, 0, 0)
        with pool.Fori(0, HEADS // 2 - 1) as pair:
            for p in range(2):
                self.issue_head(pool, pair * 2 + p, p, b, True)
        for p in range(2):
            self.issue_head(pool, HEADS - 2 + p, p, b, p == 0)

    def dot(self, dve, n, p, j, h):
        dve.wait_ge(self.landed[j], 32 * n + 16)
        slot = self.slots[:, j, :]
        dve.tensor_tensor_reduce(out=slot, in0=slot, in1=h, scale=1.0, scalar=0.0, op0=ALU.mult, op1=ALU.add,
                                 accum_out=self.dots[:, p, j:j + 1]).then_inc(self.u_used, 1)

    def gelu(self, act, n, p, half=0):
        of = slice(half * self.width, (half + 1) * self.width)
        act.wait_ge(self.u_used, n * TOPK + (half + 1) * self.width)
        act.activation(self.dots_gelu[:, p, of], self.dots[:, p, of], ACT.Gelu_apprx_tanh).then_inc(self.gelu_done, 1)

    def weigh(self, dve, n, p, b, first_pair, half=0):
        of = slice(half * self.width, (half + 1) * self.width)
        dve.wait_ge(self.gelu_done, n * self.parts + (half + 1))
        dve.tensor_tensor(self.coef[:, p, of], self.dots_gelu[:, p, of],
                          self.gates[:, b, bass.ds(first_pair + half * self.width, self.width)],
                          ALU.mult).then_inc(self.coef_ready, 1)

    def diagonal(self, act, n, j, ident):
        if j % self.width == 0:
            act.wait_ge(self.coef_ready, n * self.parts + (j // self.width + 1))
        act.wait_ge(self.slot_free, n * TOPK + (j + 1 + TOPK - 4))
        act.activation(self.diag[:, j % 4, :], ident[:, :], ACT.Copy, scale=self.coef[:, 0, j:j + 1]
                       ).then_inc(self.diag_ready, 1)

    def combine(self, pe, n, j, y_ps, first=False, last=False):
        pe.wait_ge(self.diag_ready, n * TOPK + (j + 1))
        pe.wait_ge(self.landed[j], 32 * n + 32)
        for i in range(2):
            ins = pe.matmul(y_ps[:, i, :], self.diag[:, j % 4, :], self.slots[:, j, i * BANK:(i + 1) * BANK],
                            start=(first and j == 0), stop=(last and j == TOPK - 1))
        ins.then_inc(self.slot_free, 1)

    def accumulate(self, dve, n, p, j, y):
        if j == 0:
            dve.wait_ge(self.coef_ready, n + 1)
        dve.wait_ge(self.landed[j], 32 * n + 32)
        dve.wait_ge(self.slot_free, n * TOPK + (TOPK + j))
        dve.scalar_tensor_tensor(out=y, in0=self.slots[:, j, :], scalar=self.coef[:, p, j:j + 1], in1=y,
                                 op0=ALU.mult, op1=ALU.add).then_inc(self.slot_free, 1)


def routing_block(nc, w_q, w_q_loaded, keysT, experts, gates, ident, eps, ss2, x1_dram, cond_dram,
                  h_dram, hT_dram, y_dram, g_norm2, expert_u, expert_v):
    QG = 8
    HG = QG // 2
    NG = QT // QG
    KQ = 160
    with own_semaphores(nc) as sem, ExitStack() as ctx:
        def sb(name, shape, dt=F32):
            return ctx.enter_context(nc.sbuf_tensor(name, shape, dt))

        def ps(name, shape):
            return ctx.enter_context(nc.psum_tensor(name, shape, F32))

        ga = Gather(ctx, nc, "r", 2, 2, experts, gates, expert_u[0], expert_v[0])
        g2 = sb("g2", [P, D])
        sh2 = sb("sh2", [P, D])
        x1 = sb("x1", [P, D])
        h = sb("h", [P, D])
        h_first = sb("h_first", [P, D])
        hT = sb("h2T", [P, DT, P])
        qT = sb("qT", [P, QG, P])
        scores = sb("scores", [P, NG, QG, NK])
        beaten = sb("beaten", [P, QG, NK])
        top = sb("top", [P, QG, TOPK])
        top_at = sb("top_at", [P, QG, TOPK], U32)
        top_at_f = sb("top_at_f", [P, QG, TOPK], BF16)
        cand = sb("cand", [P, HG, TOPK, TOPK])
        cand2 = sb("cand2", [P, HG, TOPK * TOPK])
        best_at = sb("best_at", [P, HG, TOPK], U32)
        pos = sb("pos", [P, 2, HG, TOPK], U32)
        pos_f = sb("pos_f", [P, 2, HG * TOPK], BF16)
        onehot = sb("onehot", [P, 2 * HG * TOPK, TOPK], BF16)
        half_at = sb("half_at", [P, 2, HG * TOPK])
        best = sb("best", [P, HEADS, TOPK])
        expert_f = sb("expert_f", [P, PAIRS])
        sixteen = sb("sixteen", [P, TOPK], BF16)
        sixteen_i = sb("sixteen_i", [P, TOPK], I32)
        gate_sum = sb("gate_sum", [P, HEADS])
        rs2 = sb("rs2", [P, NB])
        y_sb = sb("y_sb", [P, D])
        y_ps = ps("y_ps", [P, 2, BANK])
        turned_ps = ps("turned2_ps", [P, DT, P])
        q_ps = ps("q_ps", [P, QG, P])
        s_ps = ps("s_ps", [P, QG, NK])

        rows2_loaded = sem("rows2_loaded")
        g2_ready = sem("g2_ready")
        rms2_ready = sem("rms2_ready")
        rs2_ready = sem("rs2_ready")
        iota_done = sem("iota_done")
        sixteen_ready = sem("sixteen_ready")
        x1_loaded = sem("x1_loaded")
        xn_ready = sem("xn2_ready")
        h_scaled = sem("h_scaled")
        h_ready = sem("h_ready")
        h_turned = sem("h_turned")
        hT_ready = sem("h2T_ready")
        h_first_ready = sem("h_first_ready")
        h_stored = sem("h_stored")
        hT_stored = sem("hT_stored")
        q_ready = sem("q_ready")
        qT_ready = sem("qT_ready")
        s_ready = sem("s_ready")
        scores_ready = sem("scores_ready")
        scores_seen = sem("scores_seen")
        scores_free = sem("scores_free")
        less_max = sem("less_max")
        exp_done = sem("exp_done")
        chosen = sem("chosen")
        y_copied = sem("y_copied")
        y_stored = sem("y_stored")
        chainq = sem("chainq")
        setup_chain = sem("routing_setup_chain")
        block = ctx.enter_context(nc.Block())
        x1_v = x1_dram.rearrange("(b p) d -> b p d", p=P)

        def half_slots(half):
            return range(half * ga.width, (half + 1) * ga.width)

        @block.sync
        def _(sp):
            sp.dma_start(x1[:, :], x1_v[0]).then_inc(x1_loaded, 16)
            for to, row in ((sh2, cond_dram[3 * D:4 * D]), (y_sb, cond_dram[4 * D:5 * D]), (g2, g_norm2[0])):
                sp.dma_start(to[:, :], broadcast(row)).then_inc(rows2_loaded, 16)

            def store(b):
                sp.wait_ge(h_ready, b + 1)
                sp.dma_start(h_dram[b], h[:, :]).then_inc(h_stored, 16)
                sp.wait_ge(hT_ready, b + 1)
                sp.dma_start(hT_dram[b], hT[:, :, :].rearrange("p t n -> p (t n)")).then_inc(hT_stored, 16)

            with sp.Fori(0, NB - 1) as b:
                sp.wait_ge(xn_ready, b + 1)
                sp.dma_start(x1[:, :], x1_v[b + 1]).then_inc(x1_loaded, 16)
                store(b)
            store(NB - 1)
            sp.wait_ge(y_copied, 1)
            sp.dma_start(y_dram[0], y_sb[:, :]).then_inc(y_stored, 16)
            sp.wait_ge(y_stored, 16)
            sp.wait_ge(h_stored, 16 * NB)
            sp.wait_ge(hT_stored, 16 * NB)

        @block.gpsimd
        def _(pool):
            pool.iota(sixteen_i[:, :], pattern=[[1, TOPK]], base=0, channel_multiplier=0).then_inc(iota_done, 1)
            pool.wait_ge(chosen, 1)
            ga.issue_block(pool, 0)

        @block.scalar
        def _(act):
            def norm(b, first=False):
                act.wait_ge(x1_loaded, 16 * b + 16)
                if not first:
                    act.wait_ge(h_stored, 16 * b)
                act.activation(h[:, :], x1[:, :], ACT.Copy, scale=rs2[:, bass.ds(b, 1)]).then_inc(xn_ready, 1)

            def turned(b, first=False):
                act.wait_ge(h_turned, b + 1)
                if not first:
                    act.wait_ge(hT_stored, 16 * b)
                act.copy(hT[:, :, :], turned_ps[:, :, :]).then_inc(hT_ready, 1)

            def query(b, g, first=False):
                act.wait_ge(q_ready, NG * b + (g + 1))
                act.copy(qT[:, :, :], q_ps[:, :, :]).then_inc(qT_ready, 1)
                act.wait_ge(s_ready, NG * b + (g + 1))
                if not first:
                    act.wait_ge(scores_free, NG * b - (NG - 1 - g))
                act.copy(scores[:, g, :, :], s_ps[:, :, :]).then_inc(scores_ready, 1)

            def softmax(b):
                act.wait_ge(less_max, b + 1)
                act.activation(best[:, :, :], best[:, :, :], ACT.Exp).then_inc(exp_done, 1)

            act.activation(rs2[:, :], ss2[:, :], ACT.Sqrt, scale=1.0 / D, bias=eps[:, :]).then_inc(rms2_ready, 1)
            act.wait_ge(rs2_ready, 1)
            def round(b, more=True):
                n = b - 1
                query(b, 1)
                if more:
                    norm(b + 1)
                ga.gelu(act, n, 0, 0)
                for j in half_slots(0):
                    ga.diagonal(act, n, j, ident)
                if more:
                    turned(b + 1)
                ga.gelu(act, n, 0, 1)
                if more:
                    query(b + 1, 0)
                softmax(b)
                for j in half_slots(1):
                    ga.diagonal(act, n, j, ident)

            norm(0, first=True)
            turned(0, first=True)
            for g in range(NG):
                query(0, g, first=True)
            act.wait_ge(h_first_ready, 1)
            norm(1)
            turned(1)
            query(1, 0)
            softmax(0)
            with act.Fori(1, NB - 1) as b:
                round(b)
            round(NB - 1, more=False)
            for half in range(2):
                ga.gelu(act, HEADS - 1, 0, half)
                for j in range(half * ga.width, (half + 1) * ga.width):
                    ga.diagonal(act, HEADS - 1, j, ident)

        @block.tensor
        def _(pe):
            def turn(b):
                pe.wait_ge(h_ready, b + 1)
                for t in range(DT):
                    last = pe.transpose(turned_ps[:, t, :], h[:, t * P:(t + 1) * P], ident[:, :])
                last.then_inc(h_turned, 1)
                pe.wait_ge(hT_ready, b + 1)

            def query(b, g):
                for j in range(QG):
                    q = g * QG + j
                    for t in range(DT):
                        last = pe.matmul(q_ps[:, j, :], w_q[:, t, q * P:(q + 1) * P], hT[:, t, :],
                                         start=(t == 0), stop=(t == DT - 1))
                last.then_inc(q_ready, 1)
                pe.wait_ge(qT_ready, NG * b + (g + 1))
                for j in range(QG):
                    last = pe.matmul(s_ps[:, j, :], qT[:, j, :], keysT[:, g * QG + j, :], start=True, stop=True)
                last.then_inc(s_ready, 1)

            def round(b, first=False, more=True):
                query(b, 1)
                for j in half_slots(0):
                    ga.combine(pe, b - 1, j, y_ps, first)
                if more:
                    turn(b + 1)
                    query(b + 1, 0)
                for j in half_slots(1):
                    ga.combine(pe, b - 1, j, y_ps)

            pe.sem_inc(ga.slot_free, TOPK)
            pe.wait_ge(w_q_loaded, 16 * DT // 2)
            turn(0)
            for g in range(NG):
                query(0, g)
            turn(1)
            query(1, 0)
            round(1, first=True)
            with pe.Fori(2, NB - 1) as b:
                round(b)
            round(NB - 1, more=False)
            for j in range(TOPK):
                ga.combine(pe, HEADS - 1, j, y_ps, last=True)

        @block.vector
        def _(dve):
            cq, cs = ClearedChain(dve, chainq, KQ), Chain(dve, setup_chain)

            def modulate(b):
                dve.wait_ge(xn_ready, b + 1)
                dve.tensor_tensor(h[:, :], h[:, :], g2[:, :], ALU.mult).then_inc(h_scaled, 1)
                dve.wait_ge(h_scaled, b + 1)
                dve.tensor_tensor(h[:, :], h[:, :], sh2[:, :], ALU.add).then_inc(h_ready, 1)

            def top16(searches):
                for values, without, to, at in searches:
                    cq.did(dve.max(to[:, 0:8], values))
                cq.wait()
                for values, without, to, at in searches:
                    cq.did(dve.match_replace(without, to[:, 0:8], values, BELOW_ALL))
                for values, without, to, at in searches:
                    cq.did(dve.max_index(at[:, 0:8], to[:, 0:8], values))
                cq.wait()
                for values, without, to, at in searches:
                    cq.did(dve.max(to[:, 8:16], without))
                cq.wait()
                for values, without, to, at in searches:
                    cq.did(dve.max_index(at[:, 8:16], to[:, 8:16], without))

            def choose(b, g):
                dve.wait_ge(scores_ready, NG * b + (g + 1))
                dve.sem_inc(scores_seen, 1)
                top16([(scores[:, g, j, :], beaten[:, j, :], top[:, j, :], top_at[:, j, :]) for j in range(QG)])
                cq.wait()
                dve.tensor_copy(top_at_f[:, :, :], top_at[:, :, :]).then_inc(scores_free, 1)
                for i in range(HG):
                    first = top[:, 2 * i, :].unsqueeze(2).to_broadcast([P, TOPK, TOPK])
                    second = top[:, 2 * i + 1, :].unsqueeze(1).to_broadcast([P, TOPK, TOPK])
                    cq.did(dve.tensor_tensor(cand[:, i, :, :], first, second, ALU.add))
                cq.wait()
                top16([(cand[:, i, :, :].rearrange("p a b -> p (a b)"), cand2[:, i, :],
                        best[:, g * HG + i, :], best_at[:, i, :]) for i in range(HG)])
                cq.wait()
                cq.did(dve.tensor_scalar(pos[:, 0, :, :], best_at[:, :, :], 4, None, ALU.logical_shift_right))
                cq.did(dve.tensor_scalar(pos[:, 1, :, :], best_at[:, :, :], TOPK - 1, None, ALU.bitwise_and))
                cq.wait()
                cq.did(dve.tensor_copy(pos_f[:, :, :], pos[:, :, :, :].rearrange("p a h k -> p a (h k)")))
                dve.wait_ge(scores_free, NG * b + (g + 1))
                cq.wait()
                cq.did(dve.tensor_tensor(onehot[:, :, :], pos_f[:, :, :].rearrange("p a k -> p (a k)").unsqueeze(2)
                                         .to_broadcast([P, 2 * HG * TOPK, TOPK]),
                                         sixteen[:, :].unsqueeze(1).to_broadcast([P, 2 * HG * TOPK, TOPK]), ALU.is_equal))
                cq.wait()
                for i in range(2):
                    for hh in range(HG):
                        part = onehot[:, (i * HG + hh) * TOPK:(i * HG + hh + 1) * TOPK, :]
                        at = top_at_f[:, 2 * hh + i, :].unsqueeze(1).to_broadcast([P, TOPK, TOPK])
                        cq.did(dve.tensor_tensor(part, part, at, ALU.mult))
                cq.wait()
                cq.did(dve.tensor_reduce(half_at[:, :, :].rearrange("p a k -> p (a k)"), onehot[:, :, :], AX.X, ALU.add))
                cq.wait()
                cq.did(dve.scalar_tensor_tensor(out=expert_f[:, g * HG * TOPK:(g + 1) * HG * TOPK], in0=half_at[:, 0, :],
                                                scalar=float(NK), in1=half_at[:, 1, :], op0=ALU.mult, op1=ALU.add))

            def gate(b):
                over_heads = gate_sum[:, :].unsqueeze(2).to_broadcast([P, HEADS, TOPK])
                cq.wait()
                cq.did(dve.tensor_copy(gate_sum[:, :].unsqueeze(2), best[:, :, 0:1]))
                cq.wait()
                dve.tensor_tensor(best[:, :, :], best[:, :, :], over_heads, ALU.subtract).then_inc(less_max, 1)
                dve.wait_ge(exp_done, b + 1)
                cq.did(dve.tensor_reduce(gate_sum[:, :], best[:, :, :], AX.X, ALU.add))
                cq.wait()
                cq.did(dve.reciprocal(gate_sum[:, :], gate_sum[:, :]))
                cq.wait()
                cq.did(dve.tensor_tensor(gates[:, b, :].rearrange("p (h k) -> p h k", h=HEADS), best[:, :, :],
                                         over_heads, ALU.mult))
                cq.wait()
                dve.tensor_copy(experts[:, b, :], expert_f[:, :]).then_inc(chosen, 1)
                dve.wait_ge(chosen, b + 1)
                cq.end()

            def dots(n, half):
                for j in range(half * ga.width, (half + 1) * ga.width):
                    ga.dot(dve, n, 0, j, h_first[:, :])

            def weigh(n, half):
                ga.weigh(dve, n, 0, 0, n * TOPK, half)

            dve.wait_ge(rms2_ready, 1)
            dve.reciprocal(rs2[:, :], rs2[:, :]).then_inc(rs2_ready, 1)
            dve.wait_ge(iota_done, 1)
            dve.tensor_copy(sixteen[:, :], sixteen_i[:, :]).then_inc(sixteen_ready, 1)
            dve.wait_ge(sixteen_ready, 1)
            dve.wait_ge(rows2_loaded, 3 * 16)
            cs.did(dve.tensor_scalar(y_sb[:, :], y_sb[:, :], 1.0, None, ALU.add))
            cs.wait()
            dve.tensor_tensor(g2[:, :], g2[:, :], y_sb[:, :], ALU.mult).then_inc(g2_ready, 1)
            dve.wait_ge(g2_ready, 1)
            cq.round(True)
            modulate(0)
            dve.wait_ge(h_ready, 1)
            dve.tensor_copy(h_first[:, :], h[:, :]).then_inc(h_first_ready, 1)
            dve.wait_ge(h_first_ready, 1)
            for g in range(NG):
                if g == NG - 1:
                    modulate(1)
                choose(0, g)
            gate(0)

            def round(b, more=True):
                cq.round(False)
                dots(b - 1, 0)
                choose(b, 0)
                weigh(b - 1, 0)
                if more:
                    modulate(b + 1)
                dots(b - 1, 1)
                choose(b, 1)
                weigh(b - 1, 1)
                gate(b)

            with dve.Fori(1, NB - 1) as b:
                round(b)
            round(NB - 1, more=False)
            for half in range(2):
                dots(HEADS - 1, half)
                weigh(HEADS - 1, half)
            dve.wait_ge(ga.slot_free, (HEADS + 1) * TOPK)
            dve.tensor_copy(y_sb[:, :], y_ps[:, :, :].rearrange("p a n -> p (a n)")).then_inc(y_copied, 1)


def table_block(nc, experts, gates, ident, h_dram, y_dram, table_dram, expert_u, expert_v):
    with ExitStack() as ctx:
        def sb(name, shape, dt=F32):
            return ctx.enter_context(nc.sbuf_tensor(name, shape, dt))

        def ps(name, shape):
            return ctx.enter_context(nc.psum_tensor(name, shape, F32))

        def sem(name):
            return ctx.enter_context(nc.semaphore(name))

        QUAD = 4
        NQ = CHUNK // QUAD
        UNITS = HEADS // NCHUNK
        HALVES = 2 * UNITS
        NQH = NQ // HALVES
        OH = 4
        ga = Gather(ctx, nc, "t", 2, 2, experts, gates, expert_u[0], expert_v[0])
        h = sb("h_t", [P, D])
        halves_u = sb("halves_u", [P, 2, NDENSE, PAIRS], U32)
        halves = sb("halves", [P, 2, NDENSE, PAIRS])
        by_pair = sb("by_pair", [P, 3, NDENSE * P])
        now = sb("now", [P, 3, CHUNK])
        keys_i = sb("keys_i", [P, NK], I32)
        keys = sb("keys", [P, NK])
        hot1 = sb("hot1", [P, OH, NK])
        hot2 = sb("hot2", [P, OH, NK])
        part = sb("part", [P, 2, NK, CHUNK])
        y_sb = sb("y_sb_t", [P, D])
        y_ps = ps("y_ps_t", [P, 2, BANK])
        pair_ps = ps("pair_ps", [P, 3, P])
        table_ps = [ps(f"table_ps{i}", [P, QUAD, NK]) for i in range(2)]

        h_loaded = sem("h_loaded_t")
        keys_iota = sem("keys_iota")
        keys_ready = sem("keys_ready_t")
        halves_ready = sem("halves_ready")
        pairs_turned = sem("pairs_turned")
        by_pair_ready = sem("by_pair_ready")
        now_ready = sem("now_ready")
        hot_ready = sem("hot_ready")
        hot_used = sem("hot_used")
        quad_taken = sem("quad_taken")
        part_stored = [sem(f"part_stored{i}") for i in range(2)]
        y_copied = sem("y_copied_t")
        y_stored = sem("y_stored_t")
        chain = sem("table_chain")
        block = ctx.enter_context(nc.Block())

        QUADS_FROM = 5

        def slots_before(m):
            half = (m - 1) % 2
            return range(half * ga.width, (half + 1) * ga.width)

        @block.sync
        def _(sp):
            sp.dma_start(h[:, :], h_dram[1]).then_inc(h_loaded, 16)
            with sp.Fori(0, NCHUNK // 2) as pair:
                c0 = pair * 2
                for c in range(2):
                    sp.wait_ge(quad_taken, (c0 + (c + 1)) * NQ + 2)
                    sp.dma_start(table_dram[c0 + c], part[:, c, :, :]).then_inc(part_stored[c], 16)
            sp.wait_ge(y_copied, 1)
            sp.dma_start(y_dram[1], y_sb[:, :]).then_inc(y_stored, 16)
            sp.wait_ge(y_stored, 16)
            for c in range(2):
                sp.wait_ge(part_stored[c], 16 * (NCHUNK // 2) + 16)

        @block.gpsimd
        def _(pool):
            pool.iota(keys_i[:, :], pattern=[[1, NK]], base=0, channel_multiplier=0).then_inc(keys_iota, 1)
            ga.issue_block(pool, 1)


        @block.scalar
        def _(act):
            act.sem_inc(quad_taken, 2)
            for d in range(NDENSE):
                act.wait_ge(pairs_turned, d + 1)
                act.copy(by_pair[:, :, d * P:(d + 1) * P], pair_ps[:, :, :]).then_inc(by_pair_ready, 1)
            act.sem_inc(part_stored[0], 16)
            act.sem_inc(part_stored[1], 16)

            def take_quad(c0, c, k):
                act.wait_ge(hot_used, (c0 + c) * CHUNK + ((k + 1) * QUAD + OH))
                if k == 0:
                    act.wait_ge(part_stored[c], 8 * c0 + 16)
                to = part[:, c, :, k * QUAD:(k + 1) * QUAD].rearrange("p a t -> p t a")
                act.copy(to, table_ps[k % 2][:, :, :]).then_inc(quad_taken, 1)

            for m in range(2 * HEADS):
                c0, c, i = m // HALVES // 2 * 2, m // HALVES % 2, m % HALVES
                if m > 0:
                    for j in slots_before(m):
                        ga.diagonal(act, (m - 1) // 2, j, ident)
                ga.gelu(act, m // 2, 0, m % 2)
                for k in range(i * NQH, (i + 1) * NQH):
                    take_quad(c0, c, k)
            for j in slots_before(2 * HEADS):
                ga.diagonal(act, HEADS - 1, j, ident)

        @block.tensor
        def _(pe):
            pe.sem_inc(ga.slot_free, TOPK)
            pe.sem_inc(hot_used, OH)
            for d in range(NDENSE):
                pe.wait_ge(halves_ready, d + 1)
                if d > 0:
                    pe.wait_ge(by_pair_ready, d)
                for i in range(2):
                    pe.transpose(pair_ps[:, i, :], halves[:, i, d, :], ident[:, :])
                pe.transpose(pair_ps[:, 2, :], gates[:, NB - NDENSE + d, :], ident[:, :]).then_inc(pairs_turned, 1)

            def quad(c0, c, k):
                for q in range(QUAD):
                    t = (c0 + c) * CHUNK + (k * QUAD + q + 1)
                    pe.wait_ge(hot_ready, t)
                    if q == 0:
                        pe.wait_ge(quad_taken, (c0 + c) * NQ + (k + 1))
                    ins = pe.matmul(table_ps[k % 2][:, q, :], hot2[:, q, :], hot1[:, q, :], start=True, stop=True)
                    ins.then_inc(hot_used, 1)

            for m in range(2 * HEADS):
                c0, c, i = m // HALVES // 2 * 2, m // HALVES % 2, m % HALVES
                quads = list(range(i * NQH, (i + 1) * NQH))
                if m > 0:
                    for j in slots_before(m):
                        ga.combine(pe, (m - 1) // 2, j, y_ps, first=(m == 1))
                        if j % ga.width >= QUADS_FROM:
                            quad(c0, c, quads.pop(0))
                for k in quads:
                    quad(c0, c, k)
            for j in slots_before(2 * HEADS):
                ga.combine(pe, HEADS - 1, j, y_ps, last=True)

        @block.vector
        def _(dve):
            ch = Chain(dve, chain)
            dve.wait_ge(keys_iota, 1)
            dve.tensor_copy(keys[:, :], keys_i[:, :]).then_inc(keys_ready, 1)
            for d in range(NDENSE):
                e = experts[:, NB - NDENSE + d, :]
                ch.did(dve.tensor_scalar(halves_u[:, 0, d, :], e, 7, None, ALU.logical_shift_right))
                ch.did(dve.tensor_scalar(halves_u[:, 1, d, :], e, NK - 1, None, ALU.bitwise_and))
                ch.wait()
                dve.tensor_copy(halves[:, :, d, :], halves_u[:, :, d, :]).then_inc(halves_ready, 1)
            dve.wait_ge(h_loaded, 16)
            dve.wait_ge(keys_ready, 1)
            dve.wait_ge(by_pair_ready, NDENSE)
            with dve.Fori(0, NCHUNK // 2) as pair:
                c0 = pair * 2
                for c in range(2):
                    t0 = (c0 + c) * CHUNK
                    for i in range(HALVES):
                        n, half = c0 * UNITS + (c * UNITS + i // 2), i % 2
                        for j in range(half * ga.width, (half + 1) * ga.width):
                            ga.dot(dve, n, 0, j, h[:, :])
                        if i == 0:
                            dve.wait_ge(hot_used, t0 + OH)
                            dve.tensor_copy(now[:, :, :], by_pair[:, :, bass.ds(t0, CHUNK)]).then_inc(now_ready, 1)
                            dve.wait_ge(now_ready, c0 + (c + 1))
                        for t in range(i * NQH * QUAD, (i + 1) * NQH * QUAD):
                            o = t % OH
                            dve.wait_ge(hot_used, t0 + (t + 1))
                            dve.tensor_scalar(hot1[:, o, :], keys[:, :], now[:, 0, t:t + 1], now[:, 2, t:t + 1],
                                              ALU.is_equal, ALU.mult)
                            dve.tensor_scalar(hot2[:, o, :], keys[:, :], now[:, 1, t:t + 1], None,
                                              ALU.is_equal).then_inc(hot_ready, 1)
                        ga.weigh(dve, n, 0, 1, n * TOPK, half)
            dve.wait_ge(ga.slot_free, (HEADS + 1) * TOPK)
            dve.tensor_copy(y_sb[:, :], y_ps[:, :, :].rearrange("p a n -> p (a n)")).then_inc(y_copied, 1)


def dense_block(nc, experts, gates, ident, y_all, gt2, gf, h_dram, hT_dram, y_dram, table_dram, cond_dram,
                expert_u, expert_v, g_final):
    with ExitStack() as ctx:
        def sb(name, shape, dt=F32):
            return ctx.enter_context(nc.sbuf_tensor(name, shape, dt))

        def ps(name, shape):
            return ctx.enter_context(nc.psum_tensor(name, shape, F32))

        def sem(name):
            return ctx.enter_context(nc.semaphore(name))

        NT = NDENSE * P
        RING = 4
        STEPS = NK // HEADS
        OPS = 2 * NGATHER * TOPK // STEPS
        ga = Gather(ctx, nc, "d", NGATHER, 1, experts, gates, expert_u[0], expert_v[0])
        h = sb("h_d", [P, NGATHER, D])
        hT = sb("hT_d", [P, DT, NT])
        u_tile = sb("u_tile", [P, RING, D])
        v_tile = sb("v_tile", [P, RING, D])
        g_tile = sb("g_tile", [P, 2, NCHUNK, 2, CHUNK])
        uT = sb("uT", [P, 2, DT, P])
        act_sb = sb("act_sb", [P, 2, NT])
        coef = sb("coef_dense", [P, 2, NT])
        uT_ps = ps("uT_ps", [P, DT // 2, P])
        s_ps = ps("s_dense_ps", [P, NT])
        y_ps = [[ps(f"y_dense_ps{d}{i}", [P, BANK]) for i in range(2)] for d in range(NDENSE)]

        h_loaded = sem("h_loaded_d")
        hT_loaded = sem("hT_loaded_d")
        y_loaded = sem("y_loaded_d")
        y_cleared = sem("y_cleared")
        u_landed = [sem(f"u_landed{i}") for i in range(RING)]
        v_landed = [sem(f"v_landed{i}") for i in range(RING)]
        g_landed = [sem(f"g_landed{i}") for i in range(2)]
        u_half = sem("u_half")
        uT_ready = sem("uT_ready")
        s_ready = sem("s_ready_d")
        act_ready = sem("act_ready")
        c_ready = sem("coef_dense_ready")
        g_used = sem("g_used")
        v_used = sem("v_used")
        y_copied = sem("y_copied_d")
        y_gated = sem("y_gated")
        block = ctx.enter_context(nc.Block())
        u_v = expert_u[0].rearrange("(n p) d -> n p d", p=P)
        v_v = expert_v[0].rearrange("(n p) d -> n p d", p=P)
        table_pairs = table_dram.rearrange("c p (m a) t -> c p m (a t)", a=2)
        HALF = DT // 2

        @block.sync
        def _(sp):
            for d in range(NDENSE):
                sp.dma_start(hT[:, :, d * P:(d + 1) * P],
                             hT_dram[NB - NDENSE + d].rearrange("p (t n) -> p t n", n=P)).then_inc(hT_loaded, 16)
            for i in range(NGATHER):
                sp.dma_start(h[:, i, :], h_dram[2 + i]).then_inc(h_loaded, 16)
            with sp.Fori(0, HEADS) as o:
                for s in range(STEPS):
                    n = o * STEPS + s
                    place = s % RING
                    sp.wait_ge(u_half, n * 2 + 2)
                    sp.dma_start(u_tile[:, place, :], u_v[n]).then_inc(u_landed[place], 16)
                    if s % 2 == 0:
                        sp.wait_ge(g_used, n + 2)
                        sp.dma_start(g_tile[:, s // 2 % 2, :, :, :].rearrange("p c a t -> p c (a t)"),
                                     table_pairs[:, :, o * (STEPS // 2) + s // 2, :].rearrange("c p t -> p c t")
                                     ).then_inc(g_landed[s // 2 % 2], 16)
                    sp.wait_ge(v_used, n + 1)
                    sp.dma_start(v_tile[:, place, :], v_v[n]).then_inc(v_landed[place], 16)
            for i in range(2):
                sp.dma_start(y_all[:, i, :], y_dram[i]).then_inc(y_loaded, 16)
            sp.dma_start(gt2[:, :], broadcast(cond_dram[5 * D:6 * D])).then_inc(y_loaded, 16)
            sp.dma_start(gf[:, :], broadcast(g_final)).then_inc(y_loaded, 16)
            sp.wait_ge(y_loaded, 4 * 16)

        def landings(o, s):
            return o * (16 * STEPS // RING) + 16 * (s // RING + 1)

        @block.gpsimd
        def _(pool):
            with pool.Fori(0, HEADS) as o:
                for i in range(NGATHER):
                    ga.stage(pool, o * NGATHER + i, i, 2 + i, o * TOPK)
                    ga.issue(pool, ga.u, o * NGATHER + i, i)
                    ga.issue(pool, ga.v, o * NGATHER + i, i)
            pool.wait_ge(y_loaded, 4 * 16)
            for b in range(NB - NDENSE):
                if b == 2:
                    pool.wait_ge(ga.slot_free, (NGATHER * HEADS + 1) * TOPK)
                pool.tensor_tensor(y_all[:, b, :], y_all[:, b, :], gt2[:, :], ALU.mult).then_inc(y_gated, 1)
            pool.wait_ge(y_gated, NB - NDENSE)

        @block.scalar
        def _(act):
            def take_half(o, s, half):
                act.wait_ge(u_half, o * (2 * STEPS) + (2 * (s + RING) + half + 1))
                act.copy(uT[:, s % 2, half * HALF:(half + 1) * HALF, :], uT_ps[:, :, :]).then_inc(uT_ready, 1)

            def unit(o, last=False):
                for s in range(STEPS):
                    following = (o, s + 1) if s < STEPS - 1 else (o + 1, 0)
                    more = not (last and s == STEPS - 1)
                    if more:
                        take_half(*following, 0)
                    act.wait_ge(s_ready, o * STEPS + (s + 1))
                    act.wait_ge(g_used, o * STEPS + (s + RING - 1))
                    act.activation(act_sb[:, s % 2, :], s_ps[:, :], ACT.Gelu_apprx_tanh).then_inc(act_ready, 1)
                    if more:
                        take_half(*following, 1)
                    for i in range(NGATHER):
                        if (2 * i + 1) * TOPK in range(s * OPS + 1, (s + 1) * OPS + 1):
                            ga.gelu(act, o * NGATHER + i, i)

            act.sem_inc(g_used, RING)
            take_half(0, 0, 0)
            take_half(0, 0, 1)
            with act.Fori(0, HEADS - 1) as o:
                unit(o)
            unit(HEADS - 1, last=True)

        @block.tensor
        def _(pe):
            def turn_half(o, s, half):
                n = o * (2 * STEPS) + (2 * s + half)
                if half == 0:
                    pe.wait_ge(u_landed[s % RING], landings(o, s))
                if s or half or not isinstance(o, int) or o > 0:
                    pe.wait_ge(uT_ready, n)
                for t in range(HALF):
                    at = half * HALF + t
                    ins = pe.transpose(uT_ps[:, t, :], u_tile[:, s % RING, at * P:(at + 1) * P], ident[:, :])
                ins.then_inc(u_half, 1)

            def score(o, s):
                pe.wait_ge(uT_ready, o * (2 * STEPS) + (2 * s + 2))
                if s or not isinstance(o, int) or o > 0:
                    pe.wait_ge(act_ready, o * STEPS + s)
                for t in range(DT):
                    ins = pe.matmul(s_ps[:, :], uT[:, s % 2, t, :], hT[:, t, :], start=(t == 0), stop=(t == DT - 1))
                ins.then_inc(s_ready, 1)

            def weigh(o, s, first=False, last=False):
                pe.wait_ge(c_ready, o * STEPS + (s + 1))
                pe.wait_ge(v_landed[s % RING], landings(o, s))
                for d in range(NDENSE):
                    for i in range(2):
                        ins = pe.matmul(y_ps[d][i][:, :], coef[:, s % 2, d * P:(d + 1) * P],
                                        v_tile[:, s % RING, i * BANK:(i + 1) * BANK], start=first, stop=last)
                ins.then_inc(v_used, 1)

            def unit(o, first=False, last=False):
                for s in range(STEPS):
                    following = (o, s + 1) if s < STEPS - 1 else (o + 1, 0)
                    more = not (last and s == STEPS - 1)
                    if more:
                        turn_half(*following, 0)
                    score(o, s)
                    if more:
                        turn_half(*following, 1)
                    if s > 0:
                        weigh(o, s - 1, first=(first and s == 1))
                    elif not first:
                        weigh(o - 1, STEPS - 1)
                if last:
                    weigh(o, STEPS - 1, last=True)

            pe.sem_inc(u_half, 2 * RING)
            pe.sem_inc(v_used, RING)
            pe.wait_ge(hT_loaded, NDENSE * 16)
            turn_half(0, 0, 0)
            turn_half(0, 0, 1)
            unit(0, first=True)
            with pe.Fori(1, HEADS - 1) as o:
                unit(o)
            unit(HEADS - 1, last=True)

        @block.vector
        def _(dve):
            def gathered(o, k):
                i, j = k // (2 * TOPK), k % (2 * TOPK)
                n = o * NGATHER + i
                if j < TOPK:
                    ga.dot(dve, n, i, j, h[:, i, :])
                else:
                    if j == TOPK:
                        ga.weigh(dve, n, i, 2 + i, o * TOPK)
                    ga.accumulate(dve, n, i, j - TOPK, y_all[:, 2 + i, :])

            dve.memset(y_all[:, 2:2 + NGATHER, :], 0.0).then_inc(y_cleared, 1)
            dve.sem_inc(ga.slot_free, TOPK)
            dve.wait_ge(y_cleared, 1)
            dve.wait_ge(h_loaded, 16 * NGATHER)
            with dve.Fori(0, HEADS) as o:
                for s in range(STEPS):
                    for k in range(s * OPS, (s + 1) * OPS):
                        gathered(o, k)
                    n = o * STEPS + s
                    dve.wait_ge(act_ready, n + 1)
                    dve.wait_ge(g_landed[s // 2 % 2], o * (16 * STEPS // 4) + 16 * (s // 4 + 1))
                    dve.wait_ge(v_used, n + (RING - 1))
                    dve.tensor_tensor(coef[:, s % 2, :].rearrange("p (c t) -> p c t", c=NCHUNK),
                                      act_sb[:, s % 2, :].rearrange("p (c t) -> p c t", c=NCHUNK),
                                      g_tile[:, s // 2 % 2, :, s % 2, :], ALU.mult).then_inc(c_ready, 1)
                    dve.wait_ge(c_ready, n + 1)
                    dve.sem_inc(g_used, 1)
            dve.wait_ge(v_used, NK + RING)
            dve.wait_ge(y_loaded, 4 * 16)
            for d in range(NDENSE):
                for i in range(2):
                    of = slice(i * BANK, (i + 1) * BANK)
                    dve.tensor_tensor(y_all[:, NB - NDENSE + d, of], y_ps[d][i][:, :], gt2[:, of], ALU.mult
                                      ).then_inc(y_copied, 1)
            dve.wait_ge(y_copied, 2 * NDENSE)


def final_block(nc, y_all, gf, eps, x1_dram, out):
    with ExitStack() as ctx:
        def sb(name, shape):
            return ctx.enter_context(nc.sbuf_tensor(name, shape, F32))

        def sem(name):
            return ctx.enter_context(nc.semaphore(name))

        x1 = sb("x1_f", [P, NB, D])
        square = sb("square", [P, D])
        ss = sb("final_ss", [P, NB])
        rs = sb("final_rs", [P, NB])
        x1_loaded = [sem(f"x1_loaded_f{b}") for b in range(NB)]
        summed = sem("summed")
        squared = sem("squared")
        rooted = sem("rooted")
        rs_ready = sem("final_rs_ready")
        normed = sem("normed")
        out_ready = sem("out_ready_f")
        out_stored = sem("out_stored_f")
        block = ctx.enter_context(nc.Block())
        x1_v = x1_dram.rearrange("(b p) d -> b p d", p=P)
        out_v = out[0].rearrange("(b p) d -> b p d", p=P)

        @block.sync
        def _(sp):
            for b in range(NB):
                sp.dma_start(x1[:, b, :], x1_v[b]).then_inc(x1_loaded[b], 16)
            for b in range(NB):
                sp.wait_ge(out_ready, b + 1)
                sp.dma_start(out_v[b], x1[:, b, :]).then_inc(out_stored, 16)
            sp.wait_ge(out_stored, 16 * NB)

        @block.scalar
        def _(act):
            for b in range(NB):
                act.wait_ge(summed, b + 1)
                if b > 0:
                    act.wait_ge(squared, b)
                act.activation(square[:, :], x1[:, b, :], ACT.Square, accum_out=ss[:, b:b + 1]).then_inc(squared, 1)
                act.wait_ge(squared, b + 1)
                act.activation(rs[:, b:b + 1], ss[:, b:b + 1], ACT.Sqrt, scale=1.0 / D, bias=eps[:, :]).then_inc(rooted, 1)
                act.wait_ge(rs_ready, b + 1)
                act.activation(x1[:, b, :], x1[:, b, :], ACT.Copy, scale=rs[:, b:b + 1]).then_inc(normed, 1)

        @block.vector
        def _(dve):
            def add(b):
                dve.wait_ge(x1_loaded[b], 16)
                dve.tensor_tensor(x1[:, b, :], x1[:, b, :], y_all[:, b, :], ALU.add).then_inc(summed, 1)

            def root(b):
                dve.wait_ge(rooted, b + 1)
                dve.reciprocal(rs[:, b:b + 1], rs[:, b:b + 1]).then_inc(rs_ready, 1)

            def scale(b):
                dve.wait_ge(normed, b + 1)
                dve.tensor_tensor(x1[:, b, :], x1[:, b, :], gf[:, :], ALU.mult).then_inc(out_ready, 1)

            for b in range(NB + 2):
                if b < NB:
                    add(b)
                if 1 <= b <= NB:
                    root(b - 1)
                if b >= 2:
                    scale(b - 2)


_INS = ["x", "c", "w_ada", "b_ada", "g_norm1", "w_in", "b_in", "conv_w", "conv_b", "g_conv_ln", "b_conv_ln",
        "g_v_ln", "b_v_ln", "w_spatial", "b_spatial", "w_out", "b_out", "g_norm2", "w_query", "sub_keys",
        "expert_u", "expert_v", "g_final"]
_OUT = (1, SEQ, D)


def kernel(**inputs):
    import numpy as np
    import concourse.bacc as bacc
    from concourse.bass_utils import run_bass_kernel_spmd

    nc = bacc.Bacc("TRN2", target_bir_lowering=False, num_devices=1)
    arrays, args = {}, []
    for name in _INS:
        a = np.ascontiguousarray(inputs[name])
        arrays[f"in_{name}"] = a
        args.append(nc.dram_tensor(f"in_{name}", a.shape, mybir.dt.from_np(a.dtype), kind="ExternalInput").ap())
    out = nc.dram_tensor("out_0", _OUT, F32, kind="ExternalOutput").ap()
    build(nc, *args, out)
    r = run_bass_kernel_spmd(nc, [arrays], core_ids=[0])
    return r.results[0]["out_0"]
```
